# Optimizing a Trainium2 kernel written in Bass

```python
import math
import jax, jax.numpy as jnp
from jax import lax
import numpy as np

D_MODEL = 1024
BATCH = 1
SEQ = 512
DEPTH = 2

GRID_W = 64
CTX_LEN = 256
HEAD_DIM = 64
D_MIX = D_MODEL
W_SC = D_MIX // 4
W_CF = D_MIX // 4
W_GA = D_MIX // 4
W_WA = D_MIX - W_SC - W_CF - W_GA
N_HEADS_GA = W_GA // HEAD_DIM
N_KV_GA = N_HEADS_GA // 2
N_HEADS_WA = W_WA // HEAD_DIM
N_KV_WA = N_HEADS_WA // 2
SC_WIDTH = 3
CF_WIDTH = 31
WINDOW = 128
BLOCK = 128
ROPE_THETA = 10000.0
N_GROUPS = 4
N_PER_GROUP = 8
N_EXPERTS = N_GROUPS * N_PER_GROUP
TOP_K = 2
D_EXPERT = D_MODEL // 2
MOE_BLOCK = 128
NORM_EPS = 1e-6
NEG = -1e30
PROJ_SIZES = (W_SC, W_SC, W_SC, 2 * W_CF,
              W_GA, N_KV_GA * HEAD_DIM, N_KV_GA * HEAD_DIM,
              W_WA, N_KV_WA * HEAD_DIM, N_KV_WA * HEAD_DIM)
D_IN = sum(PROJ_SIZES)

kernel_name = 'hybrid_head_group_flow_block'

def rms_norm(x, g):
    xf = x.astype(jnp.float32)
    y = xf * lax.rsqrt(jnp.mean(xf * xf, axis=-1, keepdims=True) + NORM_EPS)
    return (y * g.astype(jnp.float32)).astype(x.dtype)

def layer_norm(x, g, b):
    xf = x.astype(jnp.float32)
    mu = jnp.mean(xf, axis=-1, keepdims=True)
    var = jnp.mean(jnp.square(xf - mu), axis=-1, keepdims=True)
    y = (xf - mu) * lax.rsqrt(var + NORM_EPS)
    return (y * g.astype(jnp.float32) + b.astype(jnp.float32)).astype(x.dtype)

def split_proj(z):
    idx = [int(i) for i in np.cumsum(PROJ_SIZES)[:-1]]
    return jnp.split(z, idx, axis=-1)

def heads(t):
    return t.reshape(t.shape[:-1] + (t.shape[-1] // HEAD_DIM, HEAD_DIM))

def axial_rope_tables(n):
    rows = n // GRID_W
    row = jnp.repeat(jnp.arange(rows), GRID_W).astype(jnp.float32)
    col = jnp.tile(jnp.arange(GRID_W), rows).astype(jnp.float32)
    half = HEAD_DIM // 2
    inv = ROPE_THETA ** (-jnp.arange(0, half, 2, dtype=jnp.float32) / half)
    ar = row[:, None] * inv
    ac = col[:, None] * inv
    ang = jnp.concatenate([ar, ar, ac, ac], axis=-1)
    return jnp.cos(ang), jnp.sin(ang)

def apply_rope(x, cos, sin):
    xf = x.astype(jnp.float32)
    x1, x2, x3, x4 = jnp.split(xf, 4, axis=-1)
    rot = jnp.concatenate([-x2, x1, -x4, x3], axis=-1)
    return (xf * cos[:, None, :] + rot * sin[:, None, :]).astype(x.dtype)

def dwconv(x, w):
    return lax.conv_general_dilated(x, w[:, None, :].astype(x.dtype), window_strides=(1,), padding='SAME',
                                    dimension_numbers=('NWC', 'WIO', 'NWC'), feature_group_count=x.shape[-1])

def conv_mixers(b_a, c_a, x_a, u_b, conv_a_w, conv_b_w, conv_b_b, ln_g, ln_b):
    y_a = b_a * dwconv(c_a * x_a, conv_a_w)
    g = u_b[..., :W_CF] * jax.nn.sigmoid(u_b[..., W_CF:])
    g = dwconv(g, conv_b_w) + conv_b_b
    y_b = jax.nn.silu(layer_norm(g, ln_g, ln_b))
    return y_a, y_b

def dense_attn(q, k, v, sink=None):
    B, n, Hq, Dh = q.shape
    Hkv = k.shape[2]
    G = Hq // Hkv
    qg = q.reshape(B, n, Hkv, G, Dh)
    s = jnp.einsum('bqhgd,bkhd->bhgqk', qg, k).astype(jnp.float32) * (Dh ** -0.5)
    if sink is not None:
        sk = jnp.broadcast_to(sink.reshape(1, Hkv, G, 1, 1).astype(jnp.float32), s.shape[:-1] + (1,))
        p = jax.nn.softmax(jnp.concatenate([s, sk], axis=-1), axis=-1)[..., :-1]
    else:
        p = jax.nn.softmax(s, axis=-1)
    o = jnp.einsum('bhgqk,bkhd->bqhgd', p.astype(v.dtype), v)
    return o.reshape(B, n, Hq * Dh)

def global_attn(q, k, v, kc, vc):
    B, S, Hq, Dh = q.shape
    Hkv = k.shape[2]
    G = Hq // Hkv
    nb = S // BLOCK
    kk = jnp.concatenate([k, kc], axis=1)
    vv = jnp.concatenate([v, vc], axis=1)
    qb = jnp.moveaxis(q.reshape(B, nb, BLOCK, Hkv, G, Dh), 1, 0)

    def one_block(qi):
        s = jnp.einsum('bqhgd,bkhd->bhgqk', qi, kk).astype(jnp.float32) * (Dh ** -0.5)
        p = jax.nn.softmax(s, axis=-1).astype(vv.dtype)
        return jnp.einsum('bhgqk,bkhd->bqhgd', p, vv)

    o = lax.map(one_block, qb)
    return jnp.moveaxis(o, 0, 1).reshape(B, S, Hq * Dh)

def window_attn(q, k, v, kc, vc, sink):
    B, S, Hq, Dh = q.shape
    Hkv = k.shape[2]
    G = Hq // Hkv
    nb = S // BLOCK
    pad = ((0, 0), (BLOCK, BLOCK), (0, 0), (0, 0))
    kb = jnp.pad(k, pad).reshape(B, nb + 2, BLOCK, Hkv, Dh)
    vb = jnp.pad(v, pad).reshape(B, nb + 2, BLOCK, Hkv, Dh)
    kwin = jnp.concatenate([kb[:, :-2], kb[:, 1:-1], kb[:, 2:]], axis=2)
    vwin = jnp.concatenate([vb[:, :-2], vb[:, 1:-1], vb[:, 2:]], axis=2)
    qb = q.reshape(B, nb, BLOCK, Hkv, G, Dh)
    scale = Dh ** -0.5
    s_loc = jnp.einsum('bnqhgd,bnkhd->bhgnqk', qb, kwin).astype(jnp.float32) * scale
    qi = jnp.arange(BLOCK)[:, None]
    ki = jnp.arange(3 * BLOCK)[None, :]
    rel = ki - qi
    band = (rel >= BLOCK - WINDOW) & (rel <= BLOCK + WINDOW)
    j = (jnp.arange(nb)[:, None, None] - 1) * BLOCK + ki[None]
    valid = band[None] & (j >= 0) & (j < S)
    s_loc = jnp.where(valid, s_loc, NEG)
    s_ctx = jnp.einsum('bnqhgd,bkhd->bhgnqk', qb, kc).astype(jnp.float32) * scale
    sk = jnp.broadcast_to(sink.reshape(1, Hkv, G, 1, 1, 1).astype(jnp.float32), s_loc.shape[:-1] + (1,))
    p = jax.nn.softmax(jnp.concatenate([s_loc, s_ctx, sk], axis=-1), axis=-1)
    n_loc = 3 * BLOCK
    n_ctx = kc.shape[1]
    p_loc = p[..., :n_loc].astype(v.dtype)
    p_ctx = p[..., n_loc:n_loc + n_ctx].astype(v.dtype)
    o = (jnp.einsum('bhgnqk,bnkhd->bnqhgd', p_loc, vwin)
         + jnp.einsum('bhgnqk,bkhd->bnqhgd', p_ctx, vc))
    return o.reshape(B, S, Hq * Dh)

def hier_moe(h, rg_w, rg_b, re_w, re_b, e_gate, e_up, e_down):
    shp = h.shape
    t = h.reshape(-1, shp[-1])
    T = t.shape[0]
    g_logit = (t @ rg_w + rg_b).astype(jnp.float32)
    grp = jnp.argmax(g_logit, axis=-1)
    p_grp = jnp.take_along_axis(jax.nn.softmax(g_logit, axis=-1), grp[:, None], axis=-1)
    e_logit = (t @ re_w + re_b).astype(jnp.float32).reshape(T, N_GROUPS, N_PER_GROUP)
    e_logit = jnp.take_along_axis(e_logit, grp[:, None, None], axis=1)[:, 0]
    top_v, top_i = lax.top_k(e_logit, TOP_K)
    gate = jax.nn.softmax(top_v, axis=-1) * p_grp
    eid = (grp[:, None] * N_PER_GROUP + top_i).reshape(-1)
    n_assign = T * TOP_K
    order = jnp.argsort(eid)
    e_sorted = eid[order]
    tok_sorted = order // TOP_K
    sizes = jnp.bincount(eid, length=N_EXPERTS)
    padded = (sizes + MOE_BLOCK - 1) // MOE_BLOCK * MOE_BLOCK
    pad_end = jnp.cumsum(padded)
    pad_start = pad_end - padded
    start = jnp.cumsum(sizes) - sizes
    dest = pad_start[e_sorted] + jnp.arange(n_assign) - start[e_sorted]
    n_blocks = -(-n_assign // MOE_BLOCK) + N_EXPERTS
    buf = jnp.zeros((n_blocks * MOE_BLOCK, shp[-1]), t.dtype).at[dest].set(t[tok_sorted])
    blk_e = jnp.minimum(jnp.searchsorted(pad_end, jnp.arange(n_blocks) * MOE_BLOCK, side='right'), N_EXPERTS - 1)

    def expert_block(args):
        xb, e = args
        hdn = jax.nn.silu(xb @ e_gate[e]) * (xb @ e_up[e])
        return hdn @ e_down[e]

    ybuf = lax.map(expert_block, (buf.reshape(n_blocks, MOE_BLOCK, shp[-1]), blk_e))
    ybuf = ybuf.reshape(n_blocks * MOE_BLOCK, shp[-1])
    y = ybuf[dest] * gate.reshape(-1)[order][:, None].astype(t.dtype)
    out = jnp.zeros_like(t).at[tok_sorted].add(y)
    return out.reshape(shp)

def setup_inputs(seed: int = 0) -> dict:
    key = jax.random.key(seed)
    ks = iter(jax.random.split(key, 27))
    L, D = DEPTH, D_MODEL

    def nrm(shape, scale):
        return jax.random.normal(next(ks), shape, jnp.float32) * scale

    def gain(shape):
        return 1.0 + nrm(shape, 0.05)

    return {
        'x': nrm((BATCH, SEQ, D), 1.0),
        'c': nrm((BATCH, D), 1.0),
        'ctx': nrm((BATCH, CTX_LEN, D), 1.0),
        'c_ctx': nrm((D,), 1.0),
        'mod_w': nrm((L, D, 6 * D), 0.5 * D ** -0.5),
        'mod_b': nrm((L, 6 * D), 0.02),
        'norm1_g': gain((L, D)),
        'norm2_g': gain((L, D)),
        'w_in': nrm((L, D, D_IN), D ** -0.5),
        'conv_a_w': nrm((L, SC_WIDTH, W_SC), SC_WIDTH ** -0.5),
        'conv_b_w': nrm((L, CF_WIDTH, W_CF), CF_WIDTH ** -0.5),
        'conv_b_b': nrm((L, W_CF), 0.02),
        'ln_b_g': gain((L, W_CF)),
        'ln_b_b': nrm((L, W_CF), 0.02),
        'qn_c_g': gain((L, HEAD_DIM)),
        'kn_c_g': gain((L, HEAD_DIM)),
        'qn_d_g': gain((L, HEAD_DIM)),
        'kn_d_g': gain((L, HEAD_DIM)),
        'sink_d': nrm((L, N_HEADS_WA), 0.5),
        'w_out': nrm((L, D_MIX, D), D_MIX ** -0.5),
        'rg_w': nrm((L, D, N_GROUPS), D ** -0.5),
        'rg_b': nrm((L, N_GROUPS), 0.01),
        're_w': nrm((L, D, N_EXPERTS), D ** -0.5),
        're_b': nrm((L, N_EXPERTS), 0.01),
        'e_gate': nrm((L, N_EXPERTS, D, D_EXPERT), D ** -0.5),
        'e_up': nrm((L, N_EXPERTS, D, D_EXPERT), D ** -0.5),
        'e_down': nrm((L, N_EXPERTS, D_EXPERT, D), D_EXPERT ** -0.5),
    }

def reference(x, c, ctx, c_ctx, mod_w, mod_b, norm1_g, norm2_g, w_in, conv_a_w, conv_b_w, conv_b_b,
              ln_b_g, ln_b_b, qn_c_g, kn_c_g, qn_d_g, kn_d_g, sink_d, w_out, rg_w, rg_b, re_w, re_b,
              e_gate, e_up, e_down):
    S = x.shape[1]
    cos, sin = axial_rope_tables(S)
    for l in range(DEPTH):
        last = l == DEPTH - 1
        mod = jax.nn.silu(c) @ mod_w[l] + mod_b[l]
        mod_c = jax.nn.silu(c_ctx) @ mod_w[l] + mod_b[l]
        sh1, sc1, g1, sh2, sc2, g2 = jnp.split(mod[:, None, :], 6, axis=-1)
        csh1, csc1, cg1, csh2, csc2, cg2 = jnp.split(mod_c, 6, axis=-1)

        hx = rms_norm(x, norm1_g[l]) * (1 + sc1) + sh1
        hc = rms_norm(ctx, norm1_g[l]) * (1 + csc1) + csh1
        xa_b, xa_c, xa_x, xb_u, xq_g, xk_g, xv_g, xq_w, xk_w, xv_w = split_proj(hx @ w_in[l])
        ca_b, ca_c, ca_x, cb_u, cq_g, ck_g, cv_g, cq_w, ck_w, cv_w = split_proj(hc @ w_in[l])
        kc_g = rms_norm(heads(ck_g), kn_c_g[l])
        vc_g = heads(cv_g)
        kc_w = rms_norm(heads(ck_w), kn_d_g[l])
        vc_w = heads(cv_w)
        ya, yb = conv_mixers(xa_b, xa_c, xa_x, xb_u, conv_a_w[l], conv_b_w[l], conv_b_b[l], ln_b_g[l], ln_b_b[l])
        q_g = apply_rope(rms_norm(heads(xq_g), qn_c_g[l]), cos, sin)
        k_g = apply_rope(rms_norm(heads(xk_g), kn_c_g[l]), cos, sin)
        o_g = global_attn(q_g, k_g, heads(xv_g), kc_g, vc_g)
        q_w = apply_rope(rms_norm(heads(xq_w), qn_d_g[l]), cos, sin)
        k_w = apply_rope(rms_norm(heads(xk_w), kn_d_g[l]), cos, sin)
        o_w = window_attn(q_w, k_w, heads(xv_w), kc_w, vc_w, sink_d[l])
        x = x + g1 * (jnp.concatenate([ya, yb, o_g, o_w], axis=-1) @ w_out[l])

        moe_p = (rg_w[l], rg_b[l], re_w[l], re_b[l], e_gate[l], e_up[l], e_down[l])
        if last:
            hx2 = rms_norm(x, norm2_g[l]) * (1 + sc2) + sh2
            x = x + g2 * hier_moe(hx2, *moe_p)
        else:
            cya, cyb = conv_mixers(ca_b, ca_c, ca_x, cb_u, conv_a_w[l], conv_b_w[l], conv_b_b[l], ln_b_g[l], ln_b_b[l])
            co_g = dense_attn(rms_norm(heads(cq_g), qn_c_g[l]), kc_g, vc_g)
            co_w = dense_attn(rms_norm(heads(cq_w), qn_d_g[l]), kc_w, vc_w, sink_d[l])
            ctx = ctx + cg1 * (jnp.concatenate([cya, cyb, co_g, co_w], axis=-1) @ w_out[l])
            hx2 = rms_norm(x, norm2_g[l]) * (1 + sc2) + sh2
            hc2 = rms_norm(ctx, norm2_g[l]) * (1 + csc2) + csh2
            y = hier_moe(jnp.concatenate([hx2, hc2], axis=1), *moe_p)
            x = x + g2 * y[:, :S]
            ctx = ctx + cg2 * y[:, S:]
    return x


_drawn_inputs = setup_inputs


def setup_inputs(seed=0):
    import zlib

    import numpy as np

    out = dict(_drawn_inputs(seed))
    spreads = {}
    factors = {'ctx': 2.824,
     'conv_b_b': 7.803,
     'ln_b_g': 5.269,
     'ln_b_b': 8.0,
     'qn_c_g': 8.0,
     'kn_c_g': 8.0,
     'qn_d_g': 8.0,
     'kn_d_g': 8.0,
     'sink_d': 8.0,
     'rg_b': 52.759,
     're_b': 6.211}
    for name, (base, spread) in spreads.items():
        noise = np.random.default_rng([zlib.crc32(name.encode()), seed]).standard_normal(out[name].shape)
        drawn = base * np.exp(spread * noise) if base else spread * noise
        out[name] = __import__('jax').numpy.asarray(drawn.astype(out[name].dtype))
    for name, factor in factors.items():
        out[name] = (out[name] * factor).astype(out[name].dtype)
    return out
```

```python
from contextlib import ExitStack

import concourse.bass as bass
from concourse import mybir

F32 = mybir.dt.float32
I32 = mybir.dt.int32
U32 = mybir.dt.uint32
ACT = mybir.ActivationFunctionType
ALU = mybir.AluOpType
AX = mybir.AxisListType

P = 128
D = 1024
KD = D // P
S = 512
C = 256
DEPTH = 2
XT, CT = S // P, C // P
NT = XT + CT
TOK = S + C
HD = 64
SCALE = HD ** -0.5
W_SC, W_CF, TAPS_A, TAPS_B = 256, 256, 3, 31
NG, NPG = 4, 8
NE = NG * NPG
DE = 512
B = 64
MAXB = NE + 2 * TOK // B
EPS = 1e-6
NEG = -1e30
D_IN = 2304
GRID_W = 64
ROPE_THETA = 10000.0

CONST = {}
_at = 0
for _name, _width in (("ident", P), ("ones", P), ("before", P), ("mask_prev", P), ("mask_next", P),
                      ("cos", XT * HD), ("sin", XT * HD), ("slot", B), ("block", B), ("group", NG),
                      ("expert", NE), ("limit", 2 * TOK // B // 2), ("token", NT), ("row", 1), ("eps", 1)):
    CONST[_name] = (_at, _width)
    _at += _width
N_CONST = _at

SMALL = {}
_at = 0
for _name, _width in (("norm1", KD), ("norm2", KD), ("mod_b", 6 * KD), ("conv_a", 2 * TAPS_A),
                      ("conv_b", 2 * TAPS_B), ("conv_bias", 2), ("ln_g", 2), ("ln_b", 2)):
    SMALL[_name] = (_at, _width)
    _at += _width
N_SMALL = _at
N_ROW = 4 * HD + 4 + NG + NE

SLOTS = 6
SLOT = 4096


def chunks_before_experts(layer):
    w_in = [("w_in", layer, a, b) for a, b in ((0, 512), (512, 512), (1024, 256), (1280, 512), (1792, 512))]
    w_out = [("w_out", layer, c * 512, 512) for c in range(2)]
    if layer:
        return w_in + w_out
    mod = [("mod", m, c * 512, 512) for m in range(DEPTH) for c in range(12)]
    return mod[:4] + w_in + mod[4:] + w_out


CHUNKS = [chunks_before_experts(layer) for layer in range(DEPTH)]
FIRST = [0, len(CHUNKS[0]) + 3 * NE]
EXPERTS = [FIRST[layer] + len(CHUNKS[layer]) for layer in range(DEPTH)]


def hybrid_flow_block(nc, x, ctx_tokens, conditions, consts, smalls, rows, w_mod, w_in, w_out, w_router,
                      e_gate, e_up, e_down, out):
    stack = ExitStack()
    with stack:
        def sb(name, shape, dt=F32):
            return stack.enter_context(nc.sbuf_tensor(name, shape, dt))

        def sem(name):
            return stack.enter_context(nc.semaphore(name))

        def sems(name):
            return [sem(f"{name}{layer}") for layer in range(DEPTH)]

        h2_dram = [nc.dram_tensor(f"h2_dram{l}", ((TOK, S)[l], D), F32, kind="Internal").ap() for l in range(DEPTH)]
        y_dram = [nc.dram_tensor(f"y_dram{l}", (2 * (TOK, S)[l] + B, D), F32, kind="Internal").ap() for l in range(DEPTH)]

        ring = sb("ring", [P, SLOTS, SLOT])
        xres = sb("xres", [P, NT, D])
        r1 = sb("r1", [P, 6144])
        r2 = sb("r2", [P, 6144])
        r3 = sb("r3", [P, 6144])
        const = sb("const", [P, N_CONST])
        small = sb("small", [P, DEPTH, N_SMALL])
        row = sb("row", [P, DEPTH, N_ROW])
        cond = sb("cond", [P, KD, 2])
        mod = sb("mod", [P, DEPTH, 6 * KD, 2])
        amp = sb("amp", [P, 2, KD])
        ssq = sb("ssq", [P, NT])
        rstd = sb("rstd", [P, NT])
        qk_sum = sb("qk_sum", [P, 8])
        qk_std = sb("qk_std", [P, 8])
        qk_rstd = sb("qk_rstd", [P, 8])
        stat = sb("stat", [P, 2, 8])
        nsink = sb("nsink", [P, DEPTH, 4])
        router_w = sb("router_w", [P, KD, NG + NE])
        h1T = r1[:, :].rearrange("p (k t) -> p k t", k=KD)
        prob = r1[:, 0:1536].rearrange("p (b n) -> p b n", b=2)
        probT = r1[:, 1536:3072].rearrange("p (b n) -> p b n", b=2)
        o_tok = r1[:, 3072:3328]
        h2T = r1[:, 0:2048].rearrange("p (b k t) -> p b k t", b=2, k=KD)
        h2_tok = r1[:, 2048:4096].rearrange("p (b n) -> p b n", b=2)
        scratch = r1[:, 4096:5120].rearrange("p (b n) -> p b n", b=2)
        diag = r1[:, 5120:6144].rearrange("p (k n) -> p k n", k=KD)
        catT = r2[:, :].rearrange("p (k t) -> p k t", k=8)
        glu_w = 15 + S + 15 + C + 15
        glu = r2[:, 3072:3072 + 2 * glu_w].rearrange("p (i t) -> p i t", i=2)
        square = r2[:, 3072:3072 + 1536].rearrange("p (i t) -> p i t", i=2)
        qk = r2[:, 4704:5088]
        qk_tmp = r2[:, 5088:5472]
        ln_std = r2[:, 4704:4704 + TOK]
        xg = r2[:, 0:1024]
        xgT = r2[:, 1024:1536].rearrange("p (k t) -> p k t", k=KD)
        silu = r2[:, 1536:1792]
        hid = r2[:, 1792:2048].rearrange("p (k t) -> p k t", k=4)
        yT = r2[:, 2048:2560].rearrange("p (k t) -> p k t", k=KD)
        y_tok = r2[:, 2560:3584]
        xn = r3[:, :].rearrange("p (i n) -> p i n", i=NT)
        v_tok = r3[:, 0:1536].rearrange("p (i n) -> p i n", i=NT)
        qT = r3[:, 1536:4608].rearrange("p (i t) -> p i t", i=4)
        kT = r3[:, 4608:6144].rearrange("p (i t) -> p i t", i=2)
        cx_w = 1 + S + 1 + C + 1
        cx = r3[:, 1536:1536 + 2 * cx_w].rearrange("p (i t) -> p i t", i=2)
        conv_a = r3[:, 4608:6144].rearrange("p (i t) -> p i t", i=2)
        g1_b = r3[:, 0:2048].rearrange("p (j n) -> p j n", j=2)
        amp2_b = r3[:, 2048:4096].rearrange("p (j n) -> p j n", j=2)
        sh2_b = r3[:, 4096:6144].rearrange("p (j n) -> p j n", j=2)
        g2_b = r1[:, 0:2048].rearrange("p (j n) -> p j n", j=2)
        y_pair = r1[:, 2048:6144].rearrange("p (b c n) -> p b c n", b=2, c=2)
        diag2 = r3[:, 5120:6144].rearrange("p (k n) -> p k n", k=KD)
        def part(first, *dims):
            n = 1
            for d in dims:
                n *= d
            v = r3[:, first:first + n]
            if len(dims) == 2:
                v = v.rearrange("p (a b) -> p a b", a=dims[0])
            if len(dims) == 3:
                v = v.rearrange("p (a b c) -> p a b c", a=dims[0], b=dims[1])
            return v

        def cst(name):
            a, n = CONST[name]
            return const[:, a:a + n]

        def sml(layer, name):
            a, n = SMALL[name]
            return small[:, layer, a:a + n]

        ident, ones = cst("ident"), cst("ones")
        blk_table = sb("blk_table", [1, NE + 1], I32)
        list_gather = sb("list_gather", [B, MAXB + 1], U32)
        list_scatter = sb("list_scatter", [B, MAXB + 1], U32)
        idx_gather = sb("idx_gather", [B, 1], U32)
        idx_scatter = sb("idx_scatter", [B, 1], U32)
        gates = sb("gates", [P, 2, NT])

        ps = stack.enter_context(nc.psum_tensor("ps", [P, 8, 512], F32))
        ps_flat = ps[:, :, :].rearrange("p b n -> p (b n)")

        consts_in = sem("consts_in")
        x_in = sem("x_in")
        first_half, second_half = sem("first_half"), sem("second_half")
        vec = sem("vector_step")
        act_step = sem("scalar_step")
        cond_ready = sem("cond_ready")
        mod_psum, mod_ready = sems("mod_psum"), sems("mod_ready")
        xn_ready = sems("xn_ready")
        rms_std = sems("rms_std")
        h1_psum, h1_lat, h1_ctx = sems("h1_psum"), sems("h1_lat"), sems("h1_ctx")
        conv_psum, conv_act, conv_mul = sems("conv_psum"), sems("conv_act"), sems("conv_mul")
        pads_ready = sems("pads_ready")
        qkv_psum, qk_square, qk_sums, qk_stds = sems("qkv_psum"), sems("qk_square"), sems("qk_sums"), sems("qk_stds")
        qk_scaled, qk_ready, qkT_psum, qkT_ready = sems("qk_scaled"), sems("qk_ready"), sems("qkT_psum"), sems("qkT_ready")
        conv_done, ln_psum, ln_centred, ln_sq = sems("conv_done"), sems("ln_psum"), sems("ln_centred"), sems("ln_sq")
        ln_stds, ln_scaled, ln_done = sems("ln_stds"), sems("ln_scaled"), sems("ln_done")
        s_psum, neg_max, exp_done, sink_exp = sems("s_psum"), sems("neg_max"), sems("exp_done"), sems("sink_exp")
        pT_psum, pT_ready, o_psum, o_ready = sems("pT_psum"), sems("pT_ready"), sems("o_psum"), sems("o_ready")
        oT_psum, oT_ready = sems("oT_psum"), sems("oT_ready")
        diag_ready, bc_psum, bc_ready = sems("diag_ready"), sems("bc_psum"), sems("bc_ready")
        out_psum, out_read, x_mid = sems("out_psum"), sems("out_read"), sems("x_mid")
        std2, h2_ready, h2_stored = sems("std2_"), sems("h2_ready"), sems("h2_stored")
        h2T_psum, h2T_ready, logit_psum = sems("h2T_psum"), sems("h2T_ready"), sems("logit_psum")
        router_in = sem("router_in")
        route_exp, route_ask = sems("route_exp"), sems("route_ask")
        chosen, rank_psum, onehots, list_psum, route_done = (sems("chosen"), sems("rank_psum"), sems("onehots"),
                                                             sems("list_psum"), sems("route_done"))
        idx_copied, gathered, scattered = sems("idx_copied"), sems("gathered"), sems("scattered")
        gate_psum, up_psum, silu_ready, hid_ready = sems("gate_psum"), sems("up_psum"), sems("silu_ready"), sems("hid_ready")
        xgT_psum, xgT_ready, yT_psum, yT_ready = sems("xgT_psum"), sems("xgT_ready"), sems("yT_psum"), sems("yT_ready")
        y_psum, y_ready = sems("y_psum"), sems("y_ready")
        y_loaded = [sems("y_loaded_a"), sems("y_loaded_b")]
        x_done = sems("x_done")
        out_stored = sem("out_stored")

        def tiles_of(layer):
            return NT if layer == 0 else XT

        def streams_of(layer):
            return [(0, 0, S), (1, S, C)][:2 if layer == 0 else 1]

        def key_tiles(layer, group, i):
            if i >= XT:
                return 0, 0
            return (0, XT) if group == 0 else (max(i - 1, 0), min(i + 2, XT))

        def units_of(layer):
            return [(i, g, kv, r) for i in range(tiles_of(layer)) for g in range(2) for r in range(2) for kv in range(2)]

        def is_full(layer, i):
            return layer == 0 or i < XT

        LN_MEAN, LN_VAR = 1, 2
        CONV_ACT = {0: 1, 1: 2, 2: 3, 3: 4, 6: 5, 7: 6, 8: 7, 9: 8}
        CONV_MUL = {4: 1, 5: 2}
        QKV_UNITS = 2 * NT
        VECTORS = [("g1", 16, g1_b), ("sh2", 24, sh2_b), ("amp2", None, amp2_b)]

        def bc_list(layer):
            return [(n, m, dst, j) for n, m, dst in VECTORS for j, _, _ in streams_of(layer)]

        block = stack.enter_context(nc.Block())

        def slot_ap(n, width=512):
            return ring[:, n % SLOTS, 0:8 * width].rearrange("p (k n) -> p k n", k=8)

        def down_ap(n):
            return ring[:, n % SLOTS, :].rearrange("p (k n) -> p k n", k=4)

        def loaded(n):
            return 16 * (n + 1)

        PAIR = 16 * 2 * 3

        @block.sync
        def _(sp):
            sp.dma_start(const[:, :], consts).then_inc(consts_in, 16)
            sp.dma_start(small[:, :, :], smalls.rearrange("l p n -> p l n")).then_inc(consts_in, 16)
            sp.dma_start(cond[:, :, :], conditions).then_inc(consts_in, 16)
            for layer in range(DEPTH):
                sp.dma_start(row[:, layer, :], rows[layer].partition_broadcast(P)).then_inc(consts_in, 16)

            matrices = {"mod": w_mod, "w_in": w_in, "w_out": w_out}

            def used(layer, j):
                kind, m, a, _ = CHUNKS[layer][j]
                if kind == "mod":
                    return mod_psum[m], a // 512 + 1
                if kind == "w_in":
                    return {0: (conv_psum[m], 4), 512: (conv_psum[m], 8), 1024: (conv_psum[m], 10),
                            1280: (qkv_psum[m], NT), 1792: (qkv_psum[m], 2 * NT)}[a]
                return out_psum[m], tiles_of(m) * (a // 512 + 1)

            def before_first_half(n):
                if n > 0:
                    sp.wait_ge(first_half, loaded(n - 1))

            def before_second_half(n):
                if n > 0:
                    sp.wait_ge(second_half, loaded(n - 1))

            def load_static(layer, j):
                n = FIRST[layer] + j
                kind, m, a, width = CHUNKS[layer][j]
                if n >= SLOTS and n - SLOTS < EXPERTS[0]:
                    sp.wait_ge(*used(0, n - SLOTS))
                src = matrices[kind][m].rearrange("(k p) n -> p k n", p=P)[:, :, a:a + width]
                dst = slot_ap(n, width)
                before_first_half(n)
                sp.dma_start(dst[:, 0:4, :], src[:, 0:4, :]).then_inc(first_half, 16)
                before_second_half(n)
                sp.dma_start(dst[:, 4:8, :], src[:, 4:8, :]).then_inc(second_half, 16)

            def expert_part(layer, j, e):
                w = (e_gate, e_up, e_down)[j]
                return w[layer, bass.ds(e, 1), :, :].rearrange("o (k p) n -> p (o k) n", p=P)

            count = sp.alloc_register("count")

            def load_expert(layer, j, e, n, turn):
                src = expert_part(layer, j, e)
                dst = slot_ap(n) if j < 2 else down_ap(n)
                half = 4 if j < 2 else 2
                if isinstance(turn, int):
                    before = loaded(n - 1)
                else:
                    before = count
                sp.wait_ge(first_half, before)
                sp.dma_start(dst[:, 0:half, :], src[:, 0:half, :]).then_inc(first_half, 16)
                sp.wait_ge(second_half, before)
                sp.dma_start(dst[:, half:, :], src[:, half:, :]).then_inc(second_half, 16)

            for layer in range(DEPTH):
                for j in range(len(CHUNKS[layer])):
                    if layer and j < SLOTS:
                        s = (gate_psum, up_psum, yT_psum)[j % 3][layer - 1]
                        if j == 0 or j == 3:
                            end = sp.value_load(blk_table[0:1, NE - 1 + j // 3:NE + j // 3], min_val=1, max_val=MAXB)
                        sp.wait_ge(s, end)
                    elif layer:
                        sp.wait_ge(*used(layer, j - SLOTS))
                    load_static(layer, j)
                for n in range(EXPERTS[layer], EXPERTS[layer] + 6):
                    sp.wait_ge(*used(layer, n - SLOTS - FIRST[layer]))
                    load_expert(layer, (n - EXPERTS[layer]) % 3, (n - EXPERTS[layer]) // 3, n, 0)
                sp.wait_ge(route_done[layer], 1)
                with sp.Fori(1, NE // 2) as pair:
                    for odd in range(2):
                        e = 2 * pair + odd
                        end = sp.value_load(blk_table[0:1, bass.ds(e - 1, 1)], min_val=1, max_val=MAXB)
                        for j in range(3):
                            sp.reg_add(count, PAIR * pair, loaded(EXPERTS[layer] + 3 * odd + j - 1))
                            sp.wait_ge((gate_psum, up_psum, yT_psum)[j][layer], end)
                            load_expert(layer, j, e, EXPERTS[layer] + 3 * odd + j, pair)

        @block.tensor
        def _(pe):
            def wait_chunk(n):
                pe.wait_ge(first_half, loaded(n))
                pe.wait_ge(second_half, loaded(n))

            mods_done = [0]

            def mod_chunk(layer, c, n):
                seq = mods_done[0]
                mods_done[0] += 1
                wait_chunk(n)
                if seq >= 2:
                    pe.wait_ge(mod_ready[(seq - 2) // 12], (seq - 2) % 12 + 1)
                w = slot_ap(n)
                for t in range(4):
                    for k in range(KD):
                        mm = pe.matmul(ps[:, 6 + seq % 2, 2 * t:2 * t + 2], w[:, k, t * P:(t + 1) * P],
                                       cond[:, k, :], start=(k == 0), stop=(k == KD - 1))
                mm.then_inc(mod_psum[layer], 1)

            def h1_transposes(layer):
                pe.wait_ge(xn_ready[layer], NT)
                for k in range(KD):
                    if k >= 2:
                        pe.wait_ge(h1_lat[layer], k - 1)
                        pe.wait_ge(h1_ctx[layer], k - 1)
                    for i in range(NT):
                        mm = pe.transpose(ps_flat[:, (k % 2) * 1024 + i * P:(k % 2) * 1024 + (i + 1) * P],
                                          xn[:, i, k * P:(k + 1) * P], ident)
                    mm.then_inc(h1_psum[layer], 1)

            def conv_projection(layer):
                pe.wait_ge(h1_lat[layer], KD)
                pe.wait_ge(h1_ctx[layer], KD)
                n0 = FIRST[layer] + [c[0] for c in CHUNKS[layer]].index("w_in")
                for ct in range(10):
                    n = n0 + ct // 4
                    if ct % 4 == 0:
                        wait_chunk(n)
                    if ct >= 2:
                        if ct - 2 in CONV_ACT:
                            pe.wait_ge(conv_act[layer], CONV_ACT[ct - 2])
                        else:
                            pe.wait_ge(conv_mul[layer], CONV_MUL[ct - 2])
                    w = slot_ap(n, 256 if ct >= 8 else 512)
                    for j, t0, tn in streams_of(layer):
                        for k in range(KD):
                            mm = pe.matmul(ps[:, (ct % 2) * 2 + j, 0:tn], w[:, k, (ct % 4) * P:(ct % 4 + 1) * P],
                                           h1T[:, k, t0:t0 + tn], start=(k == 0), stop=(k == KD - 1))
                    mm.then_inc(conv_psum[layer], 1)

            def qk_transposes(layer, u):
                i = u % NT
                pe.wait_ge(qk_ready[layer], u + 1)
                if u >= 2:
                    pe.wait_ge(qkT_ready[layer], u - 1)
                for r in range(2 if is_full(layer, i) else 0):
                    pe.transpose(ps[:, 6 + u % 2, r * P:(r + 1) * P], qk[:, r * P:(r + 1) * P], ident)
                pe.transpose(ps[:, 6 + u % 2, 2 * P:3 * P], qk[:, 256:384], ident).then_inc(qkT_psum[layer], 1)

            def qkv_projection(layer):
                n0 = FIRST[layer] + [c[0] for c in CHUNKS[layer]].index("w_in") + 3
                for u in range(QKV_UNITS):
                    group, i = divmod(u, NT)
                    if i == 0:
                        wait_chunk(n0 + group)
                    if u >= 2:
                        pe.wait_ge(qk_scaled[layer], u - 1)
                    w = slot_ap(n0 + group)
                    c0 = 0 if is_full(layer, i) else 256
                    for k in range(KD):
                        mm = pe.matmul(ps[:, 4 + u % 2, c0:512], h1T[:, k, i * P:(i + 1) * P], w[:, k, c0:512],
                                       start=(k == 0), stop=(k == KD - 1))
                    mm.then_inc(qkv_psum[layer], 1)
                    if u >= 1:
                        qk_transposes(layer, u - 1)
                qk_transposes(layer, QKV_UNITS - 1)

            def ln_sums(layer, which):
                if which == 0:
                    pe.wait_ge(conv_done[layer], 2 * len(streams_of(layer)))
                    src = catT[:, 2:4, :]
                else:
                    pe.wait_ge(ln_sq[layer], 2)
                    src = square
                for j, t0, tn in streams_of(layer):
                    for i in range(2):
                        mm = pe.matmul(ps[:, 4 + j, 0:tn], ones, src[:, i, t0:t0 + tn], start=(i == 0), stop=(i == 1))
                mm.then_inc(ln_psum[layer], 1)

            def scores(layer, u, unit):
                i, group, kv, r = unit
                a, b = key_tiles(layer, group, i)
                w = (b - a) * P
                half = slice(kv * HD, (kv + 1) * HD)
                q = qT[half, group * 2 + r, i * P:(i + 1) * P]
                bank = (u % 2) * 2
                if u >= 2:
                    pe.wait_ge(exp_done[layer], u - 1)
                if w:
                    masks = []
                    if group == 1 and i > 0:
                        masks.append((512 - w, cst("mask_prev")))
                    if group == 1 and i < XT - 1:
                        masks.append((512 - P, cst("mask_next")))
                    pe.matmul(ps[:, bank, 512 - w:512], q, kT[half, group, a * P:b * P], start=True, stop=not masks)
                    for m, (at, mask) in enumerate(masks):
                        pe.matmul(ps[:, bank, at:at + P], ident, mask, start=False, stop=m == len(masks) - 1)
                pe.matmul(ps[:, bank + 1, 0:C], q, kT[half, group, S:TOK], start=True, stop=True).then_inc(s_psum[layer], 1)

            def attend(layer, u, unit, last_pT):
                i, group, kv, r = unit
                a, b = key_tiles(layer, group, i)
                tiles = list(range(a, b)) + list(range(XT, NT))
                w = (b - a) * P
                pe.wait_ge(exp_done[layer], u + 1)
                if last_pT:
                    pe.wait_ge(*last_pT)
                for n in range(len(tiles)):
                    at = 512 - w + n * P
                    mm = pe.transpose(ps_flat[:, 2048 + at:2048 + at + P], prob[:, u % 2, at:at + P], ident)
                mm.then_inc(pT_psum[layer], 1)

            def weigh(layer, u, unit):
                i, group, kv, r = unit
                a, b = key_tiles(layer, group, i)
                tiles = list(range(a, b)) + list(range(XT, NT))
                w = (b - a) * P
                pe.wait_ge(pT_ready[layer], u + 1)
                if u >= 2:
                    pe.wait_ge(o_ready[layer], u - 1)
                for n, t in enumerate(tiles):
                    at = 512 - w + n * P
                    mm = pe.matmul(ps[:, 6 + u % 2, 0:HD], probT[:, u % 2, at:at + P],
                                   v_tok[:, t, group * P + kv * HD:group * P + (kv + 1) * HD],
                                   start=(n == 0), stop=(n == len(tiles) - 1))
                mm.then_inc(o_psum[layer], 1)

            def attention(layer):
                units = units_of(layer)
                pe.wait_ge(qkT_ready[layer], QKV_UNITS)
                scores(layer, 0, units[0])
                last_pT = None
                for u, unit in enumerate(units):
                    if u == LN_MEAN:
                        pe.wait_ge(*last_pT)
                        ln_sums(layer, 0)
                        last_pT = (ln_centred[layer], 1)
                    if u == LN_VAR:
                        pe.wait_ge(*last_pT)
                        ln_sums(layer, 1)
                        last_pT = (ln_stds[layer], 1)
                    if u + 1 < len(units):
                        scores(layer, u + 1, units[u + 1])
                    attend(layer, u, unit, last_pT)
                    weigh(layer, u, unit)
                    last_pT = (pT_ready[layer], u + 1)
                    if u % 4 == 3:
                        done = u // 4
                        pe.wait_ge(o_ready[layer], u + 1)
                        for j in range(2):
                            mm = pe.transpose(ps[:, 4, j * P:(j + 1) * P], o_tok[:, j * P:(j + 1) * P], ident)
                        mm.then_inc(oT_psum[layer], 1)
                        last_pT = (oT_ready[layer], done + 1)
                return last_pT

            def broadcast(layer, b):
                pe.wait_ge(diag_ready[layer], b + 1)
                if b >= 2:
                    pe.wait_ge(bc_ready[layer], b - 1)
                d = diag if b < len(bc_list(layer)) else diag2
                for half in range(2):
                    mm = pe.matmul(ps[:, (b % 2) * 2 + half, :], ones, d[:, half * 4:half * 4 + 4, :],
                                   start=True, stop=True)
                mm.then_inc(bc_psum[layer], 1)

            def h2_transposes(layer, i):
                pe.wait_ge(h2_ready[layer], i + 1)
                if i >= 1:
                    pe.wait_ge(h2T_ready[layer], i)
                for k in range(KD):
                    mm = pe.transpose(ps_flat[:, 2048 + k * P:2048 + (k + 1) * P], h2_tok[:, i % 2, k * P:(k + 1) * P], ident)
                mm.then_inc(h2T_psum[layer], 1)

            def logits(layer, i):
                if i == 0:
                    pe.wait_ge(router_in, 16 * (layer + 1))
                pe.wait_ge(h2T_ready[layer], i + 1)
                for k in range(KD):
                    mm = pe.matmul(ps[:, 6, i * 36:(i + 1) * 36], h2T[:, i % 2, k, :], router_w[:, k, :],
                                   start=(k == 0), stop=(k == KD - 1))
                mm.then_inc(logit_psum[layer], 1)

            def out_projection(layer):
                tiles = tiles_of(layer)
                nb = len(bc_list(layer))
                n0 = FIRST[layer] + [c[0] for c in CHUNKS[layer]].index("w_out")
                for u in range(2 * tiles):
                    c, i = divmod(u, tiles)
                    if i == 0:
                        wait_chunk(n0 + c)
                    if u < 2:
                        pe.wait_ge(bc_ready[layer], nb)
                        pe.wait_ge(ln_done[layer], 2)
                    else:
                        pe.wait_ge(out_read[layer], u - 1)
                    w = slot_ap(n0 + c)
                    for k in range(8):
                        mm = pe.matmul(ps[:, u % 2, :], catT[:, k, i * P:(i + 1) * P], w[:, k, :],
                                       start=(k == 0), stop=(k == 7))
                    mm.then_inc(out_psum[layer], 1)
                    if c == 1 and i >= 1:
                        h2_transposes(layer, i - 1)
                    if c == 1 and i >= 2:
                        logits(layer, i - 2)
                h2_transposes(layer, tiles - 1)
                logits(layer, tiles - 2)
                logits(layer, tiles - 1)

            def ranks(layer):
                tiles = tiles_of(layer)
                picked = part(0, NT, NE)
                pe.wait_ge(chosen[layer], 1)
                for i in range(tiles):
                    for b in range(i):
                        pe.matmul(ps[:, 0, i * NE:(i + 1) * NE], ones, picked[:, b, :], start=(b == 0), stop=False)
                    pe.matmul(ps[:, 0, i * NE:(i + 1) * NE], cst("before"), picked[:, i, :], start=(i == 0), stop=True)
                for i in range(tiles):
                    mm = pe.matmul(ps[:, 1, 0:NE], ones, picked[:, i, :], start=(i == 0), stop=(i == tiles - 1))
                mm.then_inc(rank_psum[layer], 1)

            def lists(layer):
                n = 2 * tiles_of(layer)
                for a in range(n):
                    pe.wait_ge(onehots[layer], a + 1)
                    mm = pe.matmul(ps[0:B, 2, 0:B], part(2048, 12, B)[:, a, :], part(2816, 12, B)[:, a, :],
                                   start=(a == 0), stop=(a == n - 1))
                mm.then_inc(list_psum[layer], 1)

            count = pe.alloc_register("count")

            def experts(layer):
                blocks = pe.value_load(blk_table[0:1, NE:NE + 1], min_val=1, max_val=MAXB)

                def in_transposes():
                    for k in range(KD):
                        mm = pe.transpose(ps[:, 2, k * B:(k + 1) * B], xg[0:B, k * P:(k + 1) * P], ident[0:B, 0:B])
                    mm.then_inc(xgT_psum[layer], 1)

                def out_transposes():
                    for k in range(KD):
                        mm = pe.transpose(ps_flat[0:B, 2048 + k * P:2048 + (k + 1) * P], yT[:, k, :], ident)
                    mm.then_inc(y_psum[layer], 1)

                pe.wait_ge(gathered[layer], 16)
                in_transposes()
                with pe.Fori(0, NE // 2) as pair:
                    for odd in range(2):
                        n = EXPERTS[layer] + 3 * odd
                        gate, up, down = slot_ap(n), slot_ap(n + 1), down_ap(n + 2)
                        first = pe.value_load(blk_table[0:1, bass.ds(2 * pair + odd, 1)], min_val=0, max_val=MAXB)
                        end = pe.value_load(blk_table[0:1, bass.ds(2 * pair + odd + 1, 1)], min_val=1, max_val=MAXB)
                        with pe.Fori(first, end) as q:
                            pe.wait_ge(xgT_ready[layer], q + 1)
                            pe.wait_ge(first_half, loaded(n) + PAIR * pair)
                            pe.wait_ge(second_half, loaded(n) + PAIR * pair)
                            for f in range(4):
                                for k in range(KD):
                                    mm = pe.matmul(ps[:, 0, f * B:(f + 1) * B], gate[:, k, f * P:(f + 1) * P],
                                                   xgT[:, k, :], start=(k == 0), stop=(k == KD - 1))
                            mm.then_inc(gate_psum[layer], 1)
                            pe.wait_ge(first_half, loaded(n + 1) + PAIR * pair)
                            pe.wait_ge(second_half, loaded(n + 1) + PAIR * pair)
                            for f in range(4):
                                for k in range(KD):
                                    mm = pe.matmul(ps[:, 1, f * B:(f + 1) * B], up[:, k, f * P:(f + 1) * P],
                                                   xgT[:, k, :], start=(k == 0), stop=(k == KD - 1))
                            mm.then_inc(up_psum[layer], 1)
                            pe.reg_add(count, q, 1)
                            pe.wait_ge(consts_in, 80)
                            pe.wait_ge(yT_ready[layer], count)
                            pe.wait_ge(y_ready[layer], count)
                            out_transposes()
                            pe.reg_add(count, 16 * q, 32)
                            pe.wait_ge(consts_in, 80)
                            pe.wait_ge(gathered[layer], count)
                            in_transposes()
                            pe.wait_ge(hid_ready[layer], q + 1)
                            pe.wait_ge(first_half, loaded(n + 2) + PAIR * pair)
                            pe.wait_ge(second_half, loaded(n + 2) + PAIR * pair)
                            for m in range(KD):
                                for k in range(4):
                                    mm = pe.matmul(ps[:, 3, m * B:(m + 1) * B], down[:, k, m * P:(m + 1) * P],
                                                   hid[:, k, :], start=(k == 0), stop=(k == 3))
                            mm.then_inc(yT_psum[layer], 1)
                pe.reg_add(count, blocks, 1)
                pe.wait_ge(consts_in, 80)
                pe.wait_ge(yT_ready[layer], count)
                pe.wait_ge(y_ready[layer], count)
                out_transposes()

            pe.wait_ge(consts_in, 80)
            pe.wait_ge(cond_ready, 1)
            for c in range(4):
                mod_chunk(0, c, c)
            for layer in range(DEPTH):
                h1_transposes(layer)
                conv_projection(layer)
                qkv_projection(layer)
                if layer == 0:
                    for j, (kind, m, a, _) in enumerate(CHUNKS[0]):
                        if kind == "mod" and j >= 4:
                            if mods_done[0] in (4, 5):
                                pe.wait_ge(qkT_ready[0], QKV_UNITS)
                            mod_chunk(m, a // 512, j)
                    pe.wait_ge(mod_ready[1], 12)
                last_pT = attention(layer)
                pe.wait_ge(*last_pT)
                for b in range(len(bc_list(layer))):
                    broadcast(layer, b)
                out_projection(layer)
                ranks(layer)
                lists(layer)
                for j, _, _ in streams_of(layer):
                    if j == 0:
                        pe.wait_ge(route_done[layer], 1)
                    broadcast(layer, len(bc_list(layer)) + j)
                pe.wait_ge(bc_ready[layer], len(bc_list(layer)) + len(streams_of(layer)))
                experts(layer)

        @block.vector
        def _(ve):
            steps = [0]

            def own(ins):
                steps[0] += 1
                ins.then_inc(vec, 1)

            def settle(back=0):
                ve.wait_ge(vec, steps[0] - back)

            def amplitude(layer, name, column):
                for j in range(2):
                    ins = nc.vector.scalar_tensor_tensor(out=amp[:, j, :], in0=mod[:, layer, column:column + KD, j],
                                                         scalar=1.0, in1=sml(layer, name), op0=ALU.add, op1=ALU.mult)
                    own(ins)
                settle()

            mods = [0]

            def mod_copy(layer, c):
                seq = mods[0]
                mods[0] += 1
                ve.wait_ge(mod_psum[layer], c + 1)
                bias = sml(layer, "mod_b")[:, 4 * c:4 * c + 4].unsqueeze(2).to_broadcast([P, 4, 2])
                nc.vector.tensor_tensor(mod[:, layer, 4 * c:4 * c + 4, :],
                                        ps[:, 6 + seq % 2, 0:8].rearrange("p (t j) -> p t j", j=2), bias,
                                        ALU.add).then_inc(mod_ready[layer], 1)

            def scale_tokens(layer):
                ve.wait_ge(rms_std[layer], 1)
                own(nc.vector.reciprocal(rstd[:, :], rstd[:, :]))
                settle()
                for i in range(NT):
                    nc.vector.tensor_scalar(xn[:, i, :], xres[:, i, :], rstd[:, i:i + 1], None,
                                            ALU.mult).then_inc(xn_ready[layer], 1)

            def h1_context(layer):
                for k in range(KD):
                    ve.wait_ge(h1_psum[layer], k + 1)
                    nc.vector.tensor_scalar(h1T[:, k, S:TOK], ps[:, (k % 2) * 2 + 1, 0:C], amp[:, 1, k:k + 1],
                                            mod[:, layer, k, 1:2], ALU.mult, ALU.add).then_inc(h1_ctx[layer], 1)

            def clear_pads(layer):
                for pads in ((cx, (0, 1 + S, 2 + S + C), 1), (glu, (0, 15 + S, 30 + S + C), 15)):
                    for at in pads[1]:
                        ins = nc.vector.memset(pads[0][:, :, at:at + pads[2]], 0.0)
                ins.then_inc(pads_ready[layer], 1)
                ve.wait_ge(pads_ready[layer], 1)

            def conv_a_group(layer):
                w = sml(layer, "conv_a")
                for i in range(2):
                    ve.wait_ge(conv_act[layer], CONV_ACT[2 + i])
                    ve.wait_ge(conv_psum[layer], 5 + i)
                    for j, t0, tn in streams_of(layer):
                        at = t0 + 1 + j
                        ins = nc.vector.tensor_tensor(cx[:, i, at:at + tn], cx[:, i, at:at + tn],
                                                      ps[:, (i % 2) * 2 + j, 0:tn], ALU.mult)
                    ins.then_inc(conv_mul[layer], 1)
                for i in range(2):
                    ve.wait_ge(conv_mul[layer], i + 1)
                    for tap in range(TAPS_A):
                        for j, t0, tn in streams_of(layer):
                            src = cx[:, i, t0 + j + tap:t0 + j + tap + tn]
                            dst = conv_a[:, i, t0:t0 + tn]
                            wt = w[:, i * TAPS_A + tap:i * TAPS_A + tap + 1]
                            if tap == 0:
                                own(nc.vector.tensor_scalar(dst, src, wt, None, ALU.mult))
                            else:
                                own(nc.vector.scalar_tensor_tensor(out=dst, in0=src, scalar=wt, in1=dst,
                                                                   op0=ALU.mult, op1=ALU.add))
                        settle()
                    for j, t0, tn in streams_of(layer):
                        own(nc.vector.tensor_tensor(catT[:, i, t0:t0 + tn], catT[:, i, t0:t0 + tn],
                                                    conv_a[:, i, t0:t0 + tn], ALU.mult))

            def glu_product(layer):
                for i in range(2):
                    ve.wait_ge(conv_act[layer], CONV_ACT[8 + i])
                    for j, t0, tn in streams_of(layer):
                        at = t0 + 15 * (1 + j)
                        own(nc.vector.tensor_tensor(glu[:, i, at:at + tn], glu[:, i, at:at + tn],
                                                    catT[:, 2 + i, t0:t0 + tn], ALU.mult))
                settle()

            def conv_b_tap(layer, tap):
                w = sml(layer, "conv_b")
                ns = len(streams_of(layer))
                for i in range(2):
                    if tap:
                        settle(0 if tap == TAPS_B - 1 else ns)
                    for j, t0, tn in streams_of(layer):
                        src = glu[:, i, t0 + 15 * j + tap:t0 + 15 * j + tap + tn]
                        dst = catT[:, 2 + i, t0:t0 + tn]
                        wt = w[:, i * TAPS_B + tap:i * TAPS_B + tap + 1]
                        if tap == 0:
                            own(nc.vector.tensor_scalar(dst, src, wt, sml(layer, "conv_bias")[:, i:i + 1],
                                                        ALU.mult, ALU.add))
                            continue
                        ins = nc.vector.scalar_tensor_tensor(out=dst, in0=src, scalar=wt, in1=dst,
                                                             op0=ALU.mult, op1=ALU.add)
                        if tap == TAPS_B - 1:
                            ins.then_inc(conv_done[layer], 1)
                        else:
                            own(ins)

            def rotate(layer, u):
                group, i = divmod(u, NT)
                full = is_full(layer, i)
                c0 = 0 if full else 256
                nh = 6 if full else 2
                h0 = 6 - nh
                gains = row[:, layer, group * 2 * HD:(group + 1) * 2 * HD]
                ve.wait_ge(qk_square[layer], u + 1)
                nc.vector.tensor_reduce(qk_sum[:, h0:6], qk_tmp[:, c0:384].rearrange("p (h d) -> p h d", d=HD),
                                        AX.X, ALU.add).then_inc(qk_sums[layer], 1)
                ve.wait_ge(qk_stds[layer], u + 1)
                own(nc.vector.reciprocal(qk_rstd[:, h0:6], qk_std[:, h0:6]))
                settle()
                if u >= 1:
                    ve.wait_ge(qkT_psum[layer], u)
                bank = ps[:, 4 + u % 2, c0:384].rearrange("p (h d) -> p h d", d=HD)
                heads = qk[:, c0:384].rearrange("p (h d) -> p h d", d=HD)
                if full:
                    own(nc.vector.tensor_tensor(qk[:, 0:256].rearrange("p (r kv d) -> p kv r d", r=2, kv=2),
                                                bank[:, 0:4, :].rearrange("p (kv r) d -> p kv r d", kv=2),
                                                qk_rstd[:, 0:4].rearrange("p (kv r) -> p kv r", kv=2).unsqueeze(3)
                                                .to_broadcast([P, 2, 2, HD]), ALU.mult))
                nc.vector.tensor_tensor(heads[:, nh - 2:nh, :], bank[:, nh - 2:nh, :],
                                        qk_rstd[:, 4:6].unsqueeze(2).to_broadcast([P, 2, HD]),
                                        ALU.mult).then_inc(qk_scaled[layer], 1)
                settle()
                ve.wait_ge(qk_scaled[layer], u + 1)
                if full:
                    own(nc.vector.tensor_tensor(heads[:, 0:4, :], heads[:, 0:4, :],
                                                gains[:, 0:HD].unsqueeze(1).to_broadcast([P, 4, HD]), ALU.mult))
                ins = nc.vector.tensor_tensor(heads[:, nh - 2:nh, :], heads[:, nh - 2:nh, :],
                                              gains[:, HD:2 * HD].unsqueeze(1).to_broadcast([P, 2, HD]), ALU.mult)
                if i >= XT:
                    ins.then_inc(qk_ready[layer], 1)
                    return
                own(ins)
                settle()
                cos = cst("cos")[:, i * HD:(i + 1) * HD]
                sin = cst("sin")[:, i * HD:(i + 1) * HD]
                turned = qk_tmp.rearrange("p (h a b d) -> p h a b d", h=6, a=2, b=2)
                plain = qk.rearrange("p (h a b d) -> p h a b d", h=6, a=2, b=2)
                sins = sin.rearrange("p (a b d) -> p a b d", a=2, b=2)
                for b in range(2):
                    own(nc.vector.tensor_tensor(turned[:, :, :, b, :], plain[:, :, :, 1 - b, :],
                                                sins[:, :, b, :].unsqueeze(1).to_broadcast([P, 6, 2, 16]), ALU.mult))
                settle()
                own(nc.vector.tensor_tensor(heads, heads, cos.unsqueeze(1).to_broadcast([P, 6, HD]), ALU.mult))
                settle()
                nc.vector.tensor_tensor(qk[:, :], qk[:, :], qk_tmp[:, :], ALU.add).then_inc(qk_ready[layer], 1)

            def store_qk(layer, u):
                group, i = divmod(u, NT)
                ve.wait_ge(qkT_psum[layer], u + 1)
                bank = ps[:, 6 + u % 2, 0:384].rearrange("p (r t) -> p r t", r=3)
                if is_full(layer, i):
                    own(nc.vector.tensor_copy(qT[:, group * 2:group * 2 + 2, i * P:(i + 1) * P], bank[:, 0:2, :]))
                nc.vector.tensor_copy(kT[:, group, i * P:(i + 1) * P], bank[:, 2, :]).then_inc(qkT_ready[layer], 1)

            def ln_centre(layer):
                ve.wait_ge(ln_psum[layer], 1)
                for i in range(2):
                    for j, t0, tn in streams_of(layer):
                        ins = nc.vector.scalar_tensor_tensor(out=catT[:, 2 + i, t0:t0 + tn], in0=ps[:, 4 + j, 0:tn],
                                                             scalar=-1.0 / W_CF, in1=catT[:, 2 + i, t0:t0 + tn],
                                                             op0=ALU.mult, op1=ALU.add)
                ins.then_inc(ln_centred[layer], 1)

            def ln_scale(layer):
                n = S + (C if layer == 0 else 0)
                ve.wait_ge(ln_stds[layer], 1)
                own(nc.vector.reciprocal(ln_std[:, 0:n], ln_std[:, 0:n]))
                settle()
                for i in range(2):
                    nc.vector.tensor_tensor(catT[:, 2 + i, 0:n], catT[:, 2 + i, 0:n], ln_std[:, 0:n],
                                            ALU.mult).then_inc(ln_scaled[layer], 1)

            def unit_max(layer, u, unit):
                i, group, kv, r = unit
                a, b = key_tiles(layer, group, i)
                w = (b - a) * P
                base = (u % 2) * 1024
                ve.wait_ge(s_psum[layer], u + 1)
                own(nc.vector.tensor_reduce(stat[:, u % 2, 3:4], ps_flat[:, base + 512 - w:base + TOK], AX.X, ALU.max))
                settle()
                if group == 0:
                    ins = nc.vector.tensor_scalar(stat[:, u % 2, 0:1], stat[:, u % 2, 3:4], -SCALE, None, ALU.mult)
                else:
                    h = 2 * kv + r
                    ins = nc.vector.tensor_scalar(stat[:, u % 2, 0:1], stat[:, u % 2, 3:4], -SCALE,
                                                  nsink[:, layer, h:h + 1], ALU.mult, ALU.min)
                ins.then_inc(neg_max[layer], 1)

            def unit_out(layer, u, unit):
                i, group, kv, r = unit
                h = 2 * kv + r
                total = stat[:, u % 2, 1:2]
                if group == 1:
                    ve.wait_ge(sink_exp[layer], 4 * (u // 8) + u % 4 + 1)
                    own(nc.vector.tensor_tensor(total, total, stat[:, u % 2, 2:3], ALU.add))
                    settle()
                else:
                    ve.wait_ge(exp_done[layer], u + 1)
                own(nc.vector.reciprocal(stat[:, u % 2, 4:5], total))
                settle()
                ve.wait_ge(o_psum[layer], u + 1)
                if u >= 4 and u % 4 == 0:
                    ve.wait_ge(oT_psum[layer], u // 4)
                nc.vector.tensor_scalar(o_tok[:, h * HD:(h + 1) * HD], ps[:, 6 + u % 2, 0:HD], stat[:, u % 2, 4:5],
                                        None, ALU.mult).then_inc(o_ready[layer], 1)

            def heads_out(layer, u, unit):
                i, group, _, _ = unit
                ve.wait_ge(oT_psum[layer], u // 4 + 1)
                nc.vector.tensor_copy(catT[:, 4 + 2 * group:6 + 2 * group, i * P:(i + 1) * P],
                                      ps[:, 4, 0:2 * P].rearrange("p (j t) -> p j t", j=2)).then_inc(oT_ready[layer], 1)

            def attention(layer):
                units = units_of(layer)
                unit_max(layer, 0, units[0])
                for u, unit in enumerate(units):
                    if u == LN_MEAN:
                        ln_centre(layer)
                    if u == LN_VAR:
                        ln_scale(layer)
                    if u + 1 < len(units):
                        unit_max(layer, u + 1, units[u + 1])
                    unit_out(layer, u, unit)
                    if u % 4 == 3:
                        heads_out(layer, u, unit)

            def make_diag(layer, b, values, where):
                if b >= 1:
                    ve.wait_ge(bc_psum[layer], b)
                nc.vector.tensor_tensor(where, ident.unsqueeze(1).to_broadcast([P, KD, P]),
                                        values.unsqueeze(2).to_broadcast([P, KD, P]),
                                        ALU.mult).then_inc(diag_ready[layer], 1)

            def residual(layer, u):
                tiles = tiles_of(layer)
                c, i = divmod(u, tiles)
                j = 0 if i < XT else 1
                ve.wait_ge(out_psum[layer], u + 1)
                if u == 0:
                    ve.wait_ge(bc_ready[layer], len(bc_list(layer)))
                cols = slice(c * 512, (c + 1) * 512)
                if u >= 2:
                    ve.wait_ge(x_mid[layer], u - 1)
                nc.vector.tensor_tensor(scratch[:, u % 2, :], ps[:, u % 2, :], g1_b[:, j, cols], ALU.mult).then_inc(out_read[layer], 1)
                ve.wait_ge(out_read[layer], u + 1)
                nc.vector.tensor_tensor(xres[:, i, cols], xres[:, i, cols], scratch[:, u % 2, :], ALU.add).then_inc(x_mid[layer], 1)

            def norm2(layer, i):
                j = 0 if i < XT else 1
                ve.wait_ge(std2[layer], i + 1)
                own(nc.vector.reciprocal(rstd[:, i:i + 1], rstd[:, i:i + 1]))
                settle()
                if i >= 2:
                    ve.wait_ge(h2T_psum[layer], i - 1)
                    ve.wait_ge(h2_stored[layer], 16 * (i - 1))
                own(nc.vector.scalar_tensor_tensor(out=h2_tok[:, i % 2, :], in0=xres[:, i, :], scalar=rstd[:, i:i + 1],
                                                   in1=amp2_b[:, j, :], op0=ALU.mult, op1=ALU.mult))
                settle()
                nc.vector.tensor_tensor(h2_tok[:, i % 2, :], h2_tok[:, i % 2, :], sh2_b[:, j, :],
                                        ALU.add).then_inc(h2_ready[layer], 1)

            def route(layer):
                t = tiles_of(layer)
                picked = part(0, NT, NE)[:, 0:t, :]
                logit = part(192, NT, NG + NE)[:, 0:t, :]
                glog = logit[:, :, 0:NG]
                elog = logit[:, :, NG:NG + NE]
                tmp = part(408, NT, NE)[:, 0:t, :]
                one = [part(600, NT, NE)[:, 0:t, :], part(792, NT, NE)[:, 0:t, :]]
                g_one = part(984, NT, NG)[:, 0:t, :]
                g_tmp = part(1008, NT, NG)[:, 0:t, :]
                best = part(1032, NT)[:, 0:t]
                index = part(1038, NT)[:, 0:t]
                top = [part(1044, NT)[:, 0:t], part(1050, NT)[:, 0:t]]
                p_grp = part(1056, NT)[:, 0:t]
                ask = part(1062, NT, NG + 1)[:, 0:t, :]
                answer = part(1092, NT, NG + 1)[:, 0:t, :]
                rank = part(1130, NT, NE)[:, 0:t, :]
                count = part(1322, NE)
                over = part(1354, NE, 12)
                blocks = part(1738, NE)
                ends = part(1770, NE)
                starts = part(1802, NE)
                zeros = part(1834, NE)
                dest = part(1870, 2, NT)[:, :, 0:t]
                dest_q = part(1882, 2, NT)[:, :, 0:t]
                dest_r = part(1894, 2, NT)[:, :, 0:t]
                int_a = part(1906, 2, NT).bitcast(I32)[:, :, 0:t]
                int_b = part(1918, 2, NT).bitcast(I32)[:, :, 0:t]
                value = part(1930, 2, NT)[:, :, 0:t]
                hot_r = part(2048, 12, B)
                hot_q = part(2816, 12, B)

                def wide(v, n):
                    return v.unsqueeze(2).to_broadcast([P, t, n])

                def over_tiles(v, n):
                    return v.unsqueeze(1).to_broadcast([P, t, n])

                def first_best(values, names, n, best_, hot, work):
                    own(nc.vector.tensor_reduce(best_, values, AX.X, ALU.max))
                    settle()
                    own(nc.vector.tensor_tensor(work, values, wide(best_, n), ALU.is_equal))
                    settle()
                    own(nc.vector.tensor_scalar(work, work, -1000.0, 1000.0, ALU.mult, ALU.add))
                    settle()
                    own(nc.vector.tensor_tensor(work, work, over_tiles(names, n), ALU.add))
                    settle()
                    own(nc.vector.tensor_reduce(index, work, AX.X, ALU.min))
                    settle()
                    own(nc.vector.tensor_tensor(hot, wide(index, n), over_tiles(names, n), ALU.is_equal))
                    settle()

                ve.wait_ge(logit_psum[layer], t)
                own(nc.vector.tensor_tensor(logit, ps[:, 6, 0:t * 36].rearrange("p (i n) -> p i n", n=36),
                                            over_tiles(row[:, layer, 4 * HD + 4:N_ROW], NG + NE), ALU.add))
                settle()
                first_best(glog, cst("group"), NG, best, g_one, g_tmp)
                own(nc.vector.tensor_tensor(ask[:, :, 0:NG], glog, wide(best, NG), ALU.subtract))
                own(nc.vector.tensor_scalar(g_one, g_one, -1.0, -NEG, ALU.add, ALU.mult))
                settle()
                for i in range(t):
                    own(nc.vector.tensor_tensor(elog[:, i, :].rearrange("p (g e) -> p g e", g=NG),
                                                elog[:, i, :].rearrange("p (g e) -> p g e", g=NG),
                                                g_one[:, i, :].unsqueeze(2).to_broadcast([P, NG, NPG]), ALU.add))
                settle()
                first_best(elog, cst("expert"), NE, top[0], one[0], tmp)
                own(nc.vector.tensor_scalar(tmp, one[0], NEG, None, ALU.mult))
                settle()
                own(nc.vector.tensor_tensor(elog, elog, tmp, ALU.add))
                settle()
                first_best(elog, cst("expert"), NE, top[1], one[1], tmp)
                nc.vector.tensor_tensor(picked, one[0], one[1], ALU.add).then_inc(chosen[layer], 1)
                nc.vector.tensor_tensor(ask[:, :, NG:NG + 1], top[1].unsqueeze(2), top[0].unsqueeze(2),
                                        ALU.subtract).then_inc(route_ask[layer], 1)
                own(nc.vector.memset(zeros, 0.0))
                ve.wait_ge(route_exp[layer], 1)
                own(nc.vector.tensor_reduce(p_grp, answer[:, :, 0:NG], AX.X, ALU.add))
                own(nc.vector.tensor_scalar(best.unsqueeze(2), answer[:, :, NG:NG + 1], 1.0, None, ALU.add))
                settle()
                own(nc.vector.tensor_tensor(best, best, p_grp, ALU.mult))
                settle()
                own(nc.vector.reciprocal(gates[:, 0, 0:t], best))
                settle()
                own(nc.vector.tensor_tensor(gates[:, 1, 0:t].unsqueeze(2), gates[:, 0, 0:t].unsqueeze(2),
                                            answer[:, :, NG:NG + 1], ALU.mult))
                ve.wait_ge(rank_psum[layer], 1)
                own(nc.vector.tensor_copy(rank, ps[:, 0, 0:t * NE].rearrange("p (i n) -> p i n", n=NE)))
                own(nc.vector.tensor_copy(count, ps[:, 1, 0:NE]))
                settle()
                own(nc.vector.tensor_tensor(over, count.unsqueeze(2).to_broadcast([P, NE, 12]),
                                            cst("limit").unsqueeze(1).to_broadcast([P, NE, 12]), ALU.is_gt))
                settle()
                own(nc.vector.tensor_reduce(blocks, over, AX.X, ALU.add))
                settle()
                own(nc.vector.tensor_scalar(blocks, blocks, 1.0, None, ALU.max))
                settle()
                own(nc.vector.tensor_tensor_scan(ends, blocks, zeros, 0.0, ALU.add, ALU.add))
                settle()
                own(nc.vector.tensor_tensor(starts, ends, blocks, ALU.subtract))
                settle()
                own(nc.vector.tensor_copy(blk_table[0:1, 0:NE], starts[0:1, :]))
                own(nc.vector.tensor_copy(blk_table[0:1, NE:NE + 1], ends[0:1, NE - 1:NE]))
                own(nc.vector.scalar_tensor_tensor(out=rank, in0=over_tiles(starts, NE), scalar=float(B), in1=rank,
                                                   op0=ALU.mult, op1=ALU.add))
                settle()
                for c in range(2):
                    own(nc.vector.tensor_tensor(tmp, rank, one[c], ALU.mult))
                    settle()
                    own(nc.vector.tensor_reduce(dest[:, c, :], tmp, AX.X, ALU.add))
                    settle()
                own(nc.vector.tensor_copy(int_a, dest))
                settle()
                own(nc.vector.tensor_scalar(int_b, int_a, 6, None, ALU.arith_shift_right))
                own(nc.vector.tensor_scalar(int_a, int_a, B - 1, None, ALU.bitwise_and))
                for c in range(2):
                    own(nc.vector.tensor_scalar(value[:, c, :], cst("token")[:, 0:t], float(c * t * P), None, ALU.add))
                settle()
                own(nc.vector.tensor_copy(dest_q, int_b))
                own(nc.vector.tensor_copy(dest_r, int_a))
                settle()
                for a in range(2 * t):
                    c, i = divmod(a, t)
                    own(nc.vector.tensor_scalar(hot_r[:, a, :], cst("slot"), dest_r[:, c, i:i + 1], None, ALU.is_equal))
                    nc.vector.tensor_scalar(hot_q[:, a, :], cst("block"), dest_q[:, c, i:i + 1], value[:, c, i:i + 1],
                                            ALU.is_equal, ALU.mult).then_inc(onehots[layer], 1)
                ve.wait_ge(list_psum[layer], 1)
                full = part(2048, B)[0:B, :]
                want = part(2112, B)[0:B, :]
                empty = part(2176, B)[0:B, :]
                big = part(2240, B)[0:B, :]
                row0 = part(2304, 1)[0:B, :]
                own(nc.vector.tensor_scalar(full, ps[0:B, 2, 0:B], -1.0, None, ALU.add))
                own(nc.vector.tensor_scalar(row0, cst("row")[0:B, :], float(2 * t * P + 1), None, ALU.add))
                settle()
                own(nc.vector.tensor_scalar(big, full, float(t * P), float(-t * P), ALU.is_ge, ALU.mult))
                own(nc.vector.tensor_scalar(empty, full, 0.0, row0[:, 0:1], ALU.is_lt, ALU.mult))
                settle()
                own(nc.vector.tensor_tensor(want, full, big, ALU.add))
                own(nc.vector.tensor_tensor(empty, empty, full, ALU.add))
                settle()
                own(nc.vector.tensor_scalar(want, want, 0.0, None, ALU.max))
                settle()
                own(nc.vector.tensor_copy(list_gather[:, 0:MAXB + 1], want[:, 0:MAXB + 1]))
                own(nc.vector.tensor_scalar(list_scatter[:, 0:1], row0, -1.0, None, ALU.add))
                settle()
                nc.vector.tensor_copy(list_scatter[:, 1:MAXB + 1], empty[:, 0:MAXB]).then_inc(route_done[layer], 1)

            def experts(layer):
                blocks = ve.value_load(blk_table[0:1, NE:NE + 1], min_val=1, max_val=MAXB)
                nc.vector.memset(yT, 0.0).then_inc(yT_ready[layer], 1)
                ve.wait_ge(xgT_psum[layer], 1)
                nc.vector.tensor_copy(xgT[:, :, :].rearrange("p k t -> p (k t)"), ps[:, 2, :]).then_inc(xgT_ready[layer], 1)
                with ve.Fori(0, blocks) as q:
                    ve.wait_ge(silu_ready[layer], q + 1)
                    ve.wait_ge(up_psum[layer], q + 1)
                    nc.vector.tensor_tensor(hid[:, :, :].rearrange("p k t -> p (k t)"), silu, ps[:, 1, 0:256],
                                            ALU.mult).then_inc(hid_ready[layer], 1)
                    ve.wait_ge(xgT_psum[layer], q + 2)
                    nc.vector.tensor_copy(xgT[:, :, :].rearrange("p k t -> p (k t)"), ps[:, 2, :]).then_inc(xgT_ready[layer], 1)
                    ve.wait_ge(yT_psum[layer], q + 1)
                    nc.vector.tensor_copy(yT[:, :, :].rearrange("p k t -> p (k t)"), ps[:, 3, :]).then_inc(yT_ready[layer], 1)

            def combine(layer, i):
                j = 0 if i < XT else 1
                y = y_pair[:, i % 2, :, :]
                ve.wait_ge(y_loaded[i % 2][layer], 16 * (i // 2 + 1))
                own(nc.vector.tensor_scalar(y[:, 0, :], y[:, 0, :], gates[:, 0, i:i + 1], None, ALU.mult))
                settle()
                own(nc.vector.scalar_tensor_tensor(out=y[:, 0, :], in0=y[:, 1, :], scalar=gates[:, 1, i:i + 1],
                                                   in1=y[:, 0, :], op0=ALU.mult, op1=ALU.add))
                settle()
                own(nc.vector.tensor_tensor(y[:, 0, :], y[:, 0, :], g2_b[:, j, :], ALU.mult))
                settle()
                nc.vector.tensor_tensor(xres[:, i, :], xres[:, i, :], y[:, 0, :], ALU.add).then_inc(x_done[layer], 1)

            ve.wait_ge(consts_in, 80)
            for c in range(4):
                mod_copy(0, c)
            for layer in range(DEPTH):
                own(nc.vector.tensor_scalar(nsink[:, layer, :], row[:, layer, 4 * HD:4 * HD + 4], -1.0, None, ALU.mult))
                ve.wait_ge(mod_ready[layer], 4)
                amplitude(layer, "norm1", KD)
                scale_tokens(layer)
                h1_context(layer)
                clear_pads(layer)
                conv_a_group(layer)
                glu_product(layer)
                taps = 0
                for u in range(QKV_UNITS):
                    rotate(layer, u)
                    for _ in range(2):
                        conv_b_tap(layer, taps)
                        taps += 1
                    store_qk(layer, u)
                while taps < TAPS_B:
                    conv_b_tap(layer, taps)
                    taps += 1
                    if layer == 0:
                        mod_copy(mods[0] // 12, mods[0] % 12)
                if layer == 0:
                    while mods[0] < 24:
                        mod_copy(mods[0] // 12, mods[0] % 12)
                attention(layer)
                amplitude(layer, "norm2", 4 * KD)
                for b, (name, column, _, j) in enumerate(bc_list(layer)):
                    values = amp[:, j, :] if column is None else mod[:, layer, column:column + KD, j]
                    make_diag(layer, b, values, diag)
                tiles = tiles_of(layer)
                for u in range(2 * tiles):
                    residual(layer, u)
                    if u > tiles:
                        norm2(layer, u - tiles - 1)
                norm2(layer, tiles - 1)
                route(layer)
                for j, _, _ in streams_of(layer):
                    make_diag(layer, len(bc_list(layer)) + j, mod[:, layer, 5 * KD:6 * KD, j], diag2)
                experts(layer)
                for i in range(tiles):
                    combine(layer, i)

        @block.scalar
        def _(ac):
            steps = [0]

            def own(ins):
                steps[0] += 1
                ins.then_inc(act_step, 1)

            def settle():
                ac.wait_ge(act_step, steps[0])

            eps = cst("eps")

            def rms_of_tokens(layer):
                for i in range(NT):
                    if layer == 0:
                        if i == 0:
                            ac.wait_ge(x_in, 32)
                    elif i < XT:
                        ac.wait_ge(x_done[layer - 1], i + 1)
                    else:
                        ac.wait_ge(x_done[layer - 1], NT)
                    own(nc.scalar.activation(xn[:, i, :], xres[:, i, :], ACT.Square, accum_out=ssq[:, i:i + 1]))
                settle()
                nc.scalar.activation(rstd[:, :], ssq[:, :], ACT.Sqrt, bias=eps, scale=1.0 / D).then_inc(rms_std[layer], 1)

            def h1_latents(layer):
                for k in range(KD):
                    ac.wait_ge(h1_psum[layer], k + 1)
                    if k == 0:
                        ac.wait_ge(xn_ready[layer], 1)
                    nc.scalar.activation(h1T[:, k, 0:S], ps[:, (k % 2) * 2, :], ACT.Identity, bias=mod[:, layer, k, 0:1],
                                         scale=amp[:, 0, k:k + 1]).then_inc(h1_lat[layer], 1)

            def conv_copies(layer, tiles):
                for ct in tiles:
                    ac.wait_ge(conv_psum[layer], ct + 1)
                    if ct == 2:
                        ac.wait_ge(pads_ready[layer], 1)
                    i = ct % 2
                    for j, t0, tn in streams_of(layer):
                        src = ps[:, i * 2 + j, 0:tn]
                        if ct < 2:
                            ins = nc.scalar.copy(catT[:, i, t0:t0 + tn], src)
                        elif ct < 4:
                            ins = nc.scalar.copy(cx[:, i, t0 + 1 + j:t0 + 1 + j + tn], src)
                        elif ct < 8:
                            ins = nc.scalar.copy(glu[:, i, t0 + 15 * (1 + j):t0 + 15 * (1 + j) + tn], src)
                        else:
                            ins = nc.scalar.activation(catT[:, 2 + i, t0:t0 + tn], src, ACT.Sigmoid)
                    ins.then_inc(conv_act[layer], 1)

            def qkv_copies(layer, u):
                group, i = divmod(u, NT)
                full = is_full(layer, i)
                c0 = 0 if full else 256
                h0 = 0 if full else 4
                ac.wait_ge(qkv_psum[layer], u + 1)
                if u == 0:
                    ac.wait_ge(conv_mul[layer], 2)
                own(nc.scalar.copy(v_tok[:, i, group * P:(group + 1) * P], ps[:, 4 + u % 2, 384:512]))
                if u >= 1:
                    ac.wait_ge(qk_ready[layer], u)
                nc.scalar.activation(qk_tmp[:, c0:384], ps[:, 4 + u % 2, c0:384], ACT.Square).then_inc(qk_square[layer], 1)
                ac.wait_ge(qk_sums[layer], u + 1)
                nc.scalar.activation(qk_std[:, h0:6], qk_sum[:, h0:6], ACT.Sqrt, bias=eps,
                                     scale=1.0 / HD).then_inc(qk_stds[layer], 1)

            def ln_squares(layer):
                n = S + (C if layer == 0 else 0)
                ac.wait_ge(ln_centred[layer], 1)
                for i in range(2):
                    nc.scalar.activation(square[:, i, 0:n], catT[:, 2 + i, 0:n], ACT.Square).then_inc(ln_sq[layer], 1)

            def ln_roots(layer):
                n = S + (C if layer == 0 else 0)
                ac.wait_ge(ln_psum[layer], 2)
                nc.scalar.activation(ln_std[:, 0:n], ps_flat[:, 2048:2048 + n], ACT.Sqrt, bias=eps,
                                     scale=1.0 / W_CF).then_inc(ln_stds[layer], 1)

            def ln_silu(layer):
                n = S + (C if layer == 0 else 0)
                for i in range(2):
                    ac.wait_ge(ln_scaled[layer], i + 1)
                    nc.scalar.activation(catT[:, 2 + i, 0:n], catT[:, 2 + i, 0:n], ACT.Silu,
                                         bias=sml(layer, "ln_b")[:, i:i + 1],
                                         scale=sml(layer, "ln_g")[:, i:i + 1]).then_inc(ln_done[layer], 1)

            def unit_exp(layer, u, unit):
                i, group, kv, r = unit
                a, b = key_tiles(layer, group, i)
                w = (b - a) * P
                base = (u % 2) * 1024
                ac.wait_ge(neg_max[layer], u + 1)
                if u >= 2:
                    ac.wait_ge(pT_psum[layer], u - 1)
                    ac.wait_ge(o_ready[layer], u - 1)
                nc.scalar.activation(prob[:, u % 2, 512 - w:TOK], ps_flat[:, base + 512 - w:base + TOK], ACT.Exp,
                                     bias=stat[:, u % 2, 0:1], scale=SCALE,
                                     accum_out=stat[:, u % 2, 1:2]).then_inc(exp_done[layer], 1)
                if group == 1:
                    h = 2 * kv + r
                    nc.scalar.activation(stat[:, u % 2, 2:3], row[:, layer, 4 * HD + h:4 * HD + h + 1], ACT.Exp,
                                         bias=stat[:, u % 2, 0:1]).then_inc(sink_exp[layer], 1)

            def unit_pT(layer, u, unit):
                i, group, _, _ = unit
                a, b = key_tiles(layer, group, i)
                w = (b - a) * P
                ac.wait_ge(pT_psum[layer], u + 1)
                if u >= 2:
                    ac.wait_ge(o_psum[layer], u - 1)
                nc.scalar.copy(probT[:, u % 2, 512 - w:TOK], ps_flat[:, 2048 + 512 - w:2048 + TOK]).then_inc(pT_ready[layer], 1)

            def attention(layer):
                units = units_of(layer)
                unit_exp(layer, 0, units[0])
                for u, unit in enumerate(units):
                    if u == LN_MEAN:
                        ln_squares(layer)
                    if u == LN_VAR:
                        ln_roots(layer)
                    if u + 1 < len(units):
                        unit_exp(layer, u + 1, units[u + 1])
                    unit_pT(layer, u, unit)
                ln_silu(layer)

            def store_broadcasts(layer, which):
                for b, dst, j in which:
                    ac.wait_ge(bc_psum[layer], b + 1)
                    nc.scalar.copy(dst[:, j, :], ps_flat[:, (b % 2) * 1024:(b % 2) * 1024 + 1024]).then_inc(bc_ready[layer], 1)

            def norm2(layer, i):
                tiles = tiles_of(layer)
                ac.wait_ge(x_mid[layer], tiles + i + 1)
                if i >= 2:
                    ac.wait_ge(h2T_psum[layer], i - 1)
                    ac.wait_ge(h2_stored[layer], 16 * (i - 1))
                own(nc.scalar.activation(h2_tok[:, i % 2, :], xres[:, i, :], ACT.Square, accum_out=ssq[:, i:i + 1]))
                settle()
                nc.scalar.activation(rstd[:, i:i + 1], ssq[:, i:i + 1], ACT.Sqrt, bias=eps, scale=1.0 / D).then_inc(std2[layer], 1)

            def store_h2T(layer, i):
                ac.wait_ge(h2T_psum[layer], i + 1)
                if i >= 2:
                    ac.wait_ge(logit_psum[layer], i - 1)
                nc.scalar.copy(h2T[:, i % 2, :, :].rearrange("p k t -> p (k t)"), ps_flat[:, 2048:3072]).then_inc(h2T_ready[layer], 1)

            def experts(layer):
                blocks = ac.value_load(blk_table[0:1, NE:NE + 1], min_val=1, max_val=MAXB)
                nc.scalar.copy(silu[:, 0:1], ssq[:, 0:1]).then_inc(y_ready[layer], 1)
                ac.wait_ge(y_ready[layer], 1)

                def put_rows():
                    nc.scalar.copy(y_tok[0:B, :], ps_flat[0:B, 2048:3072]).then_inc(y_ready[layer], 1)

                ac.wait_ge(gate_psum[layer], 1)
                nc.scalar.activation(silu, ps[:, 0, 0:256], ACT.Silu).then_inc(silu_ready[layer], 1)
                ac.wait_ge(y_psum[layer], 1)
                put_rows()
                with ac.Fori(1, blocks) as q:
                    ac.wait_ge(gate_psum[layer], q + 1)
                    nc.scalar.activation(silu, ps[:, 0, 0:256], ACT.Silu).then_inc(silu_ready[layer], 1)
                    ac.wait_ge(y_psum[layer], q + 1)
                    ac.wait_ge(scattered[layer], 16 * q)
                    put_rows()
                ac.wait_ge(y_psum[layer], blocks + 1)
                ac.wait_ge(scattered[layer], 16 * blocks)
                put_rows()

            ac.wait_ge(consts_in, 80)
            nc.scalar.activation(cond[:, :, :], cond[:, :, :], ACT.Silu).then_inc(cond_ready, 1)
            for layer in range(DEPTH):
                rms_of_tokens(layer)
                h1_latents(layer)
                conv_copies(layer, [*range(4), *range(6, 10)])
                for u in range(QKV_UNITS):
                    qkv_copies(layer, u)
                attention(layer)
                store_broadcasts(layer, [(b, dst, j) for b, (_, _, dst, j) in enumerate(bc_list(layer))])
                tiles = tiles_of(layer)
                for i in range(tiles):
                    norm2(layer, i)
                    if i >= 1:
                        store_h2T(layer, i - 1)
                store_h2T(layer, tiles - 1)
                ac.wait_ge(route_ask[layer], 1)
                nc.scalar.activation(part(1092, NT, NG + 1)[:, 0:tiles, :], part(1062, NT, NG + 1)[:, 0:tiles, :],
                                     ACT.Exp).then_inc(route_exp[layer], 1)
                store_broadcasts(layer, [(len(bc_list(layer)) + j, g2_b, j) for j, _, _ in streams_of(layer)])
                experts(layer)

        @block.gpsimd
        def _(po):
            count = po.alloc_register("count")
            po.dma_start(xres[:, 0:XT, :], x.rearrange("o (i p) n -> p (o i) n", p=P)).then_inc(x_in, 16)
            po.dma_start(xres[:, XT:NT, :], ctx_tokens.rearrange("o (i p) n -> p (o i) n", p=P)).then_inc(x_in, 16)
            for layer in range(DEPTH):
                tiles = tiles_of(layer)
                if layer:
                    po.wait_ge(logit_psum[layer - 1], tiles_of(layer - 1))
                po.dma_start(router_w[:, :, :], w_router[layer].rearrange("(k p) n -> p k n", p=P)).then_inc(router_in, 16)
                for i in range(tiles):
                    po.wait_ge(h2_ready[layer], i + 1)
                    po.dma_start(h2_dram[layer][i * P:(i + 1) * P, :], h2_tok[:, i % 2, :]).then_inc(h2_stored[layer], 16)
                    po.wait_ge(h2_stored[layer], 16 * (i + 1))
                po.wait_ge(route_done[layer], 1)
                po.wait_ge(bc_ready[layer], len(bc_list(layer)) + 1)
                blocks = po.value_load(blk_table[0:1, NE:NE + 1], min_val=1, max_val=MAXB)

                def gather(q):
                    nc.gpsimd.tensor_copy(idx_gather[:, :], list_gather[:, bass.ds(q, 1)]).then_inc(idx_copied[layer], 1)

                def gather_go():
                    po.indirect_dma_start(out=xg[0:B, :], out_offset=None, in_=h2_dram[layer],
                                          in_offset=bass.IndirectOffsetOnAxis(ap=idx_gather[:, 0:1], axis=0),
                                          ).then_inc(gathered[layer], 16)

                def scatter(q):
                    nc.gpsimd.tensor_copy(idx_scatter[:, :], list_scatter[:, bass.ds(q, 1)]).then_inc(idx_copied[layer], 1)

                def scatter_go():
                    po.indirect_dma_start(out=y_dram[layer], in_=y_tok[0:B, :], in_offset=None,
                                          out_offset=bass.IndirectOffsetOnAxis(ap=idx_scatter[:, 0:1], axis=0),
                                          ).then_inc(scattered[layer], 16)

                gather(0)
                po.wait_ge(idx_copied[layer], 1)
                gather_go()
                with po.Fori(0, blocks) as q:
                    po.reg_add(count, q, 1)
                    po.wait_ge(consts_in, 80)
                    po.wait_ge(xgT_psum[layer], count)
                    gather(q + 1)
                    po.reg_add(count, 2 * q, 2)
                    po.wait_ge(consts_in, 80)
                    po.wait_ge(idx_copied[layer], count)
                    gather_go()
                    po.reg_add(count, q, 2)
                    po.wait_ge(consts_in, 80)
                    po.wait_ge(y_ready[layer], count)
                    scatter(q)
                    po.reg_add(count, 2 * q, 3)
                    po.wait_ge(consts_in, 80)
                    po.wait_ge(idx_copied[layer], count)
                    scatter_go()
                po.reg_add(count, blocks, 2)
                po.wait_ge(consts_in, 80)
                po.wait_ge(y_ready[layer], count)
                scatter(blocks)
                po.reg_add(count, 2 * blocks, 2)
                po.wait_ge(consts_in, 80)
                po.wait_ge(idx_copied[layer], count)
                scatter_go()
                po.reg_add(count, 16 * blocks, 16)
                po.wait_ge(consts_in, 80)
                po.wait_ge(scattered[layer], count)
                for i in range(tiles):
                    if i >= 2:
                        po.wait_ge(x_done[layer], i - 1)
                    t = tiles * P
                    po.dma_start(y_pair[:, i % 2, :, :],
                                 y_dram[layer][0:2 * t, :].rearrange("(c i p) n -> i p c n", c=2, p=P)[i]
                                 ).then_inc(y_loaded[i % 2][layer], 16)
            for i in range(XT):
                po.wait_ge(x_done[DEPTH - 1], i + 1)
                po.dma_start(out[0, i * P:(i + 1) * P, :], xres[:, i, :]).then_inc(out_stored, 16)
            po.wait_ge(out_stored, 16 * XT)


def shape_constants():
    import numpy as np

    c = np.zeros((P, N_CONST), np.float32)

    def put(name, values):
        a, n = CONST[name]
        c[:, a:a + n] = values

    p = np.arange(P, dtype=np.float32)[:, None]
    f = np.arange(P, dtype=np.float32)[None, :]
    put("ident", p == f)
    put("ones", 1.0)
    put("before", p < f)
    put("mask_prev", np.where(f < p, NEG, 0.0))
    put("mask_next", np.where(f > p, NEG, 0.0))
    half = HD // 2
    inv = np.float32(ROPE_THETA) ** (-np.arange(0, half, 2, dtype=np.float32) / np.float32(half))
    token = np.arange(S)
    ar = (token // GRID_W).astype(np.float32)[:, None] * inv
    ac = (token % GRID_W).astype(np.float32)[:, None] * inv
    angle = np.concatenate([ar, ar, ac, ac], axis=-1)
    sign = np.tile(np.repeat(np.float32([-1, 1]), half // 2), 2)
    put("cos", np.cos(angle).reshape(XT, P, HD).transpose(1, 0, 2).reshape(P, -1))
    put("sin", (np.sin(angle) * sign).reshape(XT, P, HD).transpose(1, 0, 2).reshape(P, -1))
    put("slot", np.arange(B))
    put("block", np.arange(B))
    put("group", np.arange(NG))
    put("expert", np.arange(NE))
    put("limit", B * np.arange(CONST["limit"][1]))
    put("token", p + P * np.arange(NT) + 1)
    put("row", p)
    put("eps", EPS)
    return c


_OUTS = [((1, S, D), "float32")]


def kernel(**inputs):
    import numpy as _np
    import concourse.bacc as _bacc
    from concourse import mybir as _mybir
    from concourse.bass_utils import run_bass_kernel_spmd as _run

    a = {k: _np.asarray(v) for k, v in inputs.items()}

    def by_partition(v):
        return v.reshape(-1, P).T

    smalls, rows = [], []
    for layer in range(DEPTH):
        smalls.append(_np.concatenate([
            by_partition(a["norm1_g"][layer]), by_partition(a["norm2_g"][layer]), by_partition(a["mod_b"][layer]),
            a["conv_a_w"][layer].reshape(TAPS_A, 2, P).transpose(2, 1, 0).reshape(P, -1),
            a["conv_b_w"][layer].reshape(TAPS_B, 2, P).transpose(2, 1, 0).reshape(P, -1),
            by_partition(a["conv_b_b"][layer]), by_partition(a["ln_b_g"][layer]), by_partition(a["ln_b_b"][layer]),
        ], axis=1))
        rows.append(_np.concatenate([a["qn_c_g"][layer], a["kn_c_g"][layer], a["qn_d_g"][layer], a["kn_d_g"][layer],
                                     a["sink_d"][layer], a["rg_b"][layer], a["re_b"][layer]]))
    arrays = {
        "x": a["x"], "ctx_tokens": a["ctx"],
        "conditions": _np.stack([by_partition(a["c"][0]), by_partition(a["c_ctx"])], axis=2),
        "consts": shape_constants(), "smalls": _np.stack(smalls), "rows": _np.stack(rows),
        "w_mod": a["mod_w"], "w_in": a["w_in"], "w_out": a["w_out"],
        "w_router": _np.concatenate([a["rg_w"], a["re_w"]], axis=2),
        "e_gate": a["e_gate"], "e_up": a["e_up"], "e_down": a["e_down"],
    }
    arrays = {f"in_{k}_dram": _np.ascontiguousarray(v) for k, v in arrays.items()}
    nc = _bacc.Bacc("TRN2", target_bir_lowering=False, num_devices=1)
    args = [nc.dram_tensor(k, v.shape, _mybir.dt.from_np(v.dtype), kind="ExternalInput").ap() for k, v in arrays.items()]
    for i, (shape, dtype) in enumerate(_OUTS):
        args.append(nc.dram_tensor(f"out_{i}_dram", shape, _mybir.dt.from_np(_np.dtype(dtype)), kind="ExternalOutput").ap())
    hybrid_flow_block(nc, *args)
    r = _run(nc, [arrays], core_ids=[0])
    got = tuple(r.results[0][f"out_{i}_dram"] for i in range(len(_OUTS)))
    return got[0]
```

```python
from contextlib import ExitStack

import concourse.bass as bass
from concourse import mybir

F32 = mybir.dt.float32
I32 = mybir.dt.int32
U32 = mybir.dt.uint32
ACT = mybir.ActivationFunctionType
ALU = mybir.AluOpType
AX = mybir.AxisListType

P = 128
D = 1024
KD = D // P
S = 512
C = 256
DEPTH = 2
XT, CT = S // P, C // P
NT = XT + CT
TOK = S + C
HD = 64
SCALE = HD ** -0.5
W_SC, W_CF, TAPS_A, TAPS_B = 256, 256, 3, 31
NG, NPG = 4, 8
NE = NG * NPG
DE = 512
B = 64
MAXB = NE + 2 * TOK // B
EPS = 1e-6
NEG = -1e30
D_IN = 2304
GRID_W = 64
ROPE_THETA = 10000.0

CONST = {}
_at = 0
for _name, _width in (("ident", P), ("ones", P), ("before", P), ("mask_prev", P), ("mask_next", P),
                      ("cos", XT * HD), ("sin", XT * HD), ("slot", 2 * B), ("limit", 2 * TOK // B // 2),
                      ("token", NT), ("slot_row", 1), ("half", 1), ("select", 2), ("eps", 1)):
    CONST[_name] = (_at, _width)
    _at += _width
N_CONST = _at

SMALL = {}
_at = 0
for _name, _width in (("norm1", KD), ("norm2", KD), ("mod_b", 6 * KD), ("conv_a", 2 * TAPS_A),
                      ("conv_b", 2 * TAPS_B), ("conv_bias", 2), ("ln_g", 2), ("ln_b", 2)):
    SMALL[_name] = (_at, _width)
    _at += _width
N_SMALL = _at
N_ROW = 4 * HD + 4 + NG + NE

SLOTS = 6
SLOT = 4096


QKV_UNITS = 2 * NT
CONV_ORDER = (6, 7, 8, 9, 0, 1, 2, 3, 4, 5)


def steps_before_attention(layer):
    conv = [("conv", ct) for ct in CONV_ORDER]
    qkv = [("qkv", u) for u in range(QKV_UNITS)]
    if layer:
        return conv + qkv
    mod = [("mod", n) for n in range(12 * DEPTH)]
    steps = mod[:MOD_FIRST]
    for n, step in enumerate(conv + qkv):
        steps.append(step)
        if MOD_FIRST + n < len(mod):
            steps.append(mod[MOD_FIRST + n])
    return steps


MOD_FIRST = 4
MOD_CONV = MOD_FIRST + 10


def chunk_of(layer, step):
    kind, n = step
    if kind == "mod":
        return "mod", n // 12, n % 12 * 512, 512
    if kind == "conv":
        first = 768 if n >= 6 else 512 if n >= 4 else 0
        return "w_in", layer, first, 256 if first == 512 else 512
    return "w_in", layer, 1280 + n // NT * 512, 512


def chunks_before_experts(layer):
    chunks = []
    for step in steps_before_attention(layer):
        if chunk_of(layer, step) not in chunks:
            chunks.append(chunk_of(layer, step))
    return chunks + [("w_out", layer, c * 512, 512) for c in range(2)]


CHUNKS = [chunks_before_experts(layer) for layer in range(DEPTH)]
FIRST = [0, len(CHUNKS[0]) + 3 * NE]
EXPERTS = [FIRST[layer] + len(CHUNKS[layer]) for layer in range(DEPTH)]


def hybrid_flow_block(nc, x, ctx_tokens, conditions, consts, smalls, rows, w_mod, w_in, w_out, w_router,
                      e_gate, e_up, e_down, out):
    stack = ExitStack()
    with stack:
        def sb(name, shape, dt=F32):
            return stack.enter_context(nc.sbuf_tensor(name, shape, dt))

        def sem(name):
            return stack.enter_context(nc.semaphore(name))

        def sems(name):
            return [sem(f"{name}{layer}") for layer in range(DEPTH)]

        h2_dram = [nc.dram_tensor(f"h2_dram{l}", ((TOK, S)[l] * 2, D // 2), F32, kind="Internal").ap() for l in range(DEPTH)]
        y_dram = [nc.dram_tensor(f"y_dram{l}", ((2 * (TOK, S)[l] + B) * 2, D // 2), F32, kind="Internal").ap() for l in range(DEPTH)]

        ring = sb("ring", [P, SLOTS, SLOT])
        xres = sb("xres", [P, NT, D])
        r1 = sb("r1", [P, 6144])
        r2 = sb("r2", [P, 6144])
        r3 = sb("r3", [P, 6144])
        const = sb("const", [P, N_CONST])
        small = sb("small", [P, DEPTH, N_SMALL])
        row = sb("row", [P, DEPTH, N_ROW])
        cond = sb("cond", [P, KD, 32])
        mod_row = sb("mod_row", [P, 512])
        o_tok = sb("o_tok", [P, 256])
        mod = sb("mod", [P, DEPTH, 6 * KD, 2])
        amp = sb("amp", [P, 2, KD])
        ssq = sb("ssq", [P, NT])
        rstd = sb("rstd", [P, NT])
        qk_sum = sb("qk_sum", [P, 8])
        qk_std = sb("qk_std", [P, 8])
        qk_rstd = sb("qk_rstd", [P, 8])
        stat = sb("stat", [P, 4, 8])
        nsink = sb("nsink", [P, DEPTH, 4])
        router_w = sb("router_w", [P, KD, NG + NE])
        h1T = r1[:, :].rearrange("p (k t) -> p k t", k=KD)
        prob = r1[:, 0:1536].rearrange("p (b n) -> p b n", b=2)
        probT = r1[:, 1536:3072].rearrange("p (b n) -> p b n", b=2)
        kT_pad = r1[:, 3072:6144].rearrange("p (g kv t) -> p g kv t", g=2, kv=2)
        h2T = r1[:, 0:2048].rearrange("p (b k t) -> p b k t", b=2, k=KD)
        h2_tok = r1[:, 2048:4096].rearrange("p (b n) -> p b n", b=2)
        scratch = r1[:, 4096:5120].rearrange("p (b n) -> p b n", b=2)
        diag = r1[:, 5120:6144].rearrange("p (k n) -> p k n", k=KD)
        catT = r2[:, :].rearrange("p (k t) -> p k t", k=8)
        glu_w = 15 + S + 15 + C + 15
        glu = r2[:, 3072:3072 + 2 * glu_w].rearrange("p (i t) -> p i t", i=2)
        square = r2[:, 3072:3072 + 1536].rearrange("p (i t) -> p i t", i=2)
        qk = r2[:, 4704:5088]
        qk_tmp = r2[:, 5088:5472]
        ln_std = r2[:, 4704:4704 + TOK]
        xg = r2[:, 0:512]
        xgT = r2[:, 1024:1536].rearrange("p (j h t) -> p j h t", j=4, h=2)
        silu = r2[:, 1536:1792]
        hid = r2[:, 1792:2048]
        hidT = r2[:, 2048:2304].rearrange("p (j h t) -> p j h t", j=2, h=2)
        y_rows = r2[:, 2560:3072]
        xn = r3[:, :].rearrange("p (i n) -> p i n", i=NT)
        v_tok = r3[:, 0:1536].rearrange("p (i n) -> p i n", i=NT)
        qT = r3[:, 1536:4608].rearrange("p (i t) -> p i t", i=4)
        kT = r3[:, 4608:6144].rearrange("p (i t) -> p i t", i=2)
        cx_w = 1 + S + 1 + C + 1
        cx = r3[:, 1536:1536 + 2 * cx_w].rearrange("p (i t) -> p i t", i=2)
        conv_a = r3[:, 4608:6144].rearrange("p (i t) -> p i t", i=2)
        g1_b = r3[:, 0:2048].rearrange("p (j n) -> p j n", j=2)
        amp2_b = r3[:, 2048:4096].rearrange("p (j n) -> p j n", j=2)
        sh2_b = r3[:, 4096:6144].rearrange("p (j n) -> p j n", j=2)
        g2_b = r1[:, 0:2048].rearrange("p (j n) -> p j n", j=2)
        y_pair = r1[:, 2048:6144].rearrange("p (b c n) -> p b c n", b=2, c=2)
        diag2 = r3[:, 5120:6144].rearrange("p (k n) -> p k n", k=KD)
        def part(first, *dims):
            n = 1
            for d in dims:
                n *= d
            v = r3[:, first:first + n]
            if len(dims) == 2:
                v = v.rearrange("p (a b) -> p a b", a=dims[0])
            if len(dims) == 3:
                v = v.rearrange("p (a b c) -> p a b c", a=dims[0], b=dims[1])
            return v

        def cst(name):
            a, n = CONST[name]
            return const[:, a:a + n]

        def sml(layer, name):
            a, n = SMALL[name]
            return small[:, layer, a:a + n]

        ident, ones = cst("ident"), cst("ones")
        blk_table = sb("blk_table", [1, NE + 1], I32)
        list_gather = sb("list_gather", [P, MAXB + 1], U32)
        list_scatter = sb("list_scatter", [P, MAXB + 1], U32)
        idx_gather = sb("idx_gather", [P, 1], U32)
        idx_scatter = sb("idx_scatter", [P, 1], U32)
        gates = sb("gates", [P, 2, NT])

        ps = stack.enter_context(nc.psum_tensor("ps", [P, 8, 512], F32))
        ps_flat = ps[:, :, :].rearrange("p b n -> p (b n)")

        consts_in = sem("consts_in")
        x_in = sem("x_in")
        first_half, second_half = sem("first_half"), sem("second_half")
        vec = sem("vector_step")
        act_step = sem("scalar_step")
        cond_ready = sem("cond_ready")
        mod_psum = sems("mod_psum")
        mod_rows, mod_turned, mod_ready = sem("mod_rows"), sem("mod_turned"), sem("mod_ready")
        xn_ready = sems("xn_ready")
        rms_std = sems("rms_std")
        h1_psum, h1_lat, h1_ctx = sems("h1_psum"), sems("h1_lat"), sems("h1_ctx")
        conv_psum, conv_act, conv_mul = sems("conv_psum"), sems("conv_act"), sems("conv_mul")
        pads_ready = sems("pads_ready")
        qkv_psum, qk_square, qk_sums, qk_stds = sems("qkv_psum"), sems("qk_square"), sems("qk_sums"), sems("qk_stds")
        qk_scaled, qk_ready, qkT_psum, qkT_ready = sems("qk_scaled"), sems("qk_ready"), sems("qkT_psum"), sems("qkT_ready")
        conv_done, ln_psum, ln_centred, ln_sq = sems("conv_done"), sems("ln_psum"), sems("ln_centred"), sems("ln_sq")
        ln_stds, ln_scaled, ln_done = sems("ln_stds"), sems("ln_scaled"), sems("ln_done")
        s_psum, neg_max, exp_done, sink_exp = sems("s_psum"), sems("neg_max"), sems("exp_done"), sems("sink_exp")
        pT_psum, pT_ready, o_psum, o_ready = sems("pT_psum"), sems("pT_ready"), sems("o_psum"), sems("o_ready")
        keys_padded = sems("keys_padded")
        oT_psum, oT_ready = sems("oT_psum"), sems("oT_ready")
        diag_ready, bc_psum, bc_ready = sems("diag_ready"), sems("bc_psum"), sems("bc_ready")
        out_psum, out_read, x_mid = sems("out_psum"), sems("out_read"), sems("x_mid")
        std2, h2_ready, h2_stored = sems("std2_"), sems("h2_ready"), sems("h2_stored")
        h2T_psum, h2T_ready, logit_psum = sems("h2T_psum"), sems("h2T_ready"), sems("logit_psum")
        router_in = sem("router_in")
        route_exp, route_ask = sems("route_exp"), sems("route_ask")
        chosen, rank_psum, onehots, list_psum, route_done = (sems("chosen"), sems("rank_psum"), sems("onehots"),
                                                             sems("list_psum"), sems("route_done"))
        idx_copied, gathered, scattered = sems("idx_copied"), sems("gathered"), sems("scattered")
        gate_psum, up_psum, silu_ready, hid_ready = sems("gate_psum"), sems("up_psum"), sems("silu_ready"), sems("hid_ready")
        xgT_psum, xgT_ready, hidT_psum, hidT_ready = sems("xgT_psum"), sems("xgT_ready"), sems("hidT_psum"), sems("hidT_ready")
        y_psum, y_ready = sems("y_psum"), sems("y_ready")
        y_loaded = [sems("y_loaded_a"), sems("y_loaded_b")]
        y_scaled, x_done = sems("y_scaled"), sems("x_done")
        out_stored = sem("out_stored")

        def tiles_of(layer):
            return NT if layer == 0 else XT

        def streams_of(layer):
            return [(0, 0, S), (1, S, C)][:2 if layer == 0 else 1]

        def key_tiles(layer, group, i):
            if i >= XT:
                return 0, 0
            return (0, XT) if group == 0 else (max(i - 1, 0), min(i + 2, XT))

        def units_of(layer):
            return [(i, g, kv, r) for i in range(tiles_of(layer)) for g in range(2) for r in range(2) for kv in range(2)]

        def is_full(layer, i):
            return layer == 0 or i < XT

        LN_MEAN, LN_VAR = 1, 2
        TAPS_EARLY = 24
        CONV_ACT = {ct: n + 1 for n, ct in enumerate(CONV_ORDER[:8])}
        CONV_MUL = {4: 1, 5: 2}
        CONV_AT = {ct: n for n, ct in enumerate(CONV_ORDER)}
        VECTORS = [("g1", 16, g1_b), ("sh2", 24, sh2_b), ("amp2", None, amp2_b)]

        def bc_list(layer):
            return [(n, m, dst, j) for n, m, dst in VECTORS for j, _, _ in streams_of(layer)]

        block = stack.enter_context(nc.Block())

        def chunk_index(layer, step):
            return FIRST[layer] + CHUNKS[layer].index(chunk_of(layer, step))

        def mod_bank(n):
            return 5 + n % 2 if n < MOD_CONV else n % 2

        def turned_bank(n):
            return 7 if n < MOD_CONV else 2

        def slot_ap(n, width=512):
            return ring[:, n % SLOTS, 0:8 * width].rearrange("p (k n) -> p k n", k=8)

        def down_ap(n):
            return ring[:, n % SLOTS, :].rearrange("p (k n) -> p k n", k=4)

        def loaded(n):
            return 16 * (n + 1)

        PAIR = 16 * 2 * 3

        @block.sync
        def _(sp):
            sp.dma_start(const[:, :], consts).then_inc(consts_in, 16)
            sp.dma_start(small[:, :, :], smalls.rearrange("l p n -> p l n")).then_inc(consts_in, 16)
            sp.dma_start(cond[:, :, :], conditions).then_inc(consts_in, 16)
            for layer in range(DEPTH):
                sp.dma_start(row[:, layer, :], rows[layer].partition_broadcast(P)).then_inc(consts_in, 16)

            matrices = {"mod": w_mod, "w_in": w_in, "w_out": w_out}

            def used(layer, j):
                kind, m, a, _ = CHUNKS[layer][j]
                if kind == "mod":
                    return mod_psum[m], a // 512 + 1
                if kind == "w_in":
                    return {768: (conv_psum[m], 4), 0: (conv_psum[m], 8), 512: (conv_psum[m], 10),
                            1280: (qkv_psum[m], NT), 1792: (qkv_psum[m], 2 * NT)}[a]
                return out_psum[m], tiles_of(m) * (a // 512 + 1)

            def before_first_half(n):
                if n > 0:
                    sp.wait_ge(first_half, loaded(n - 1))

            def before_second_half(n):
                if n > 0:
                    sp.wait_ge(second_half, loaded(n - 1))

            def load_static(layer, j):
                n = FIRST[layer] + j
                kind, m, a, width = CHUNKS[layer][j]
                if n >= SLOTS and n - SLOTS < EXPERTS[0]:
                    sp.wait_ge(*used(0, n - SLOTS))
                src = matrices[kind][m].rearrange("(k p) n -> p k n", p=P)[:, :, a:a + width]
                dst = slot_ap(n, width)
                before_first_half(n)
                sp.dma_start(dst[:, 0:4, :], src[:, 0:4, :]).then_inc(first_half, 16)
                before_second_half(n)
                sp.dma_start(dst[:, 4:8, :], src[:, 4:8, :]).then_inc(second_half, 16)

            def expert_part(layer, j, e):
                w = (e_gate, e_up, e_down)[j]
                return w[layer, bass.ds(e, 1), :, :].rearrange("o (k p) n -> p (o k) n", p=P)

            count = sp.alloc_register("count")

            def load_expert(layer, j, e, n, turn):
                src = expert_part(layer, j, e)
                dst = slot_ap(n) if j < 2 else down_ap(n)
                half = 4 if j < 2 else 2
                if isinstance(turn, int):
                    before = loaded(n - 1)
                else:
                    before = count
                sp.wait_ge(first_half, before)
                sp.dma_start(dst[:, 0:half, :], src[:, 0:half, :]).then_inc(first_half, 16)
                sp.wait_ge(second_half, before)
                sp.dma_start(dst[:, half:, :], src[:, half:, :]).then_inc(second_half, 16)

            for layer in range(DEPTH):
                for j in range(len(CHUNKS[layer])):
                    if layer and j < SLOTS:
                        s = (gate_psum, up_psum, y_psum)[j % 3][layer - 1]
                        if j == 0 or j == 3:
                            end = sp.value_load(blk_table[0:1, NE - 1 + j // 3:NE + j // 3], min_val=1, max_val=MAXB)
                        sp.wait_ge(s, end)
                        if j == 1:
                            for half in range(2):
                                sp.wait_ge(y_loaded[half][layer - 1], 16 * tiles_of(layer - 1) // 2)
                    elif layer:
                        sp.wait_ge(*used(layer, j - SLOTS))
                    load_static(layer, j)
                for n in range(EXPERTS[layer], EXPERTS[layer] + 6):
                    sp.wait_ge(*used(layer, n - SLOTS - FIRST[layer]))
                    load_expert(layer, (n - EXPERTS[layer]) % 3, (n - EXPERTS[layer]) // 3, n, 0)
                sp.wait_ge(route_done[layer], 1)
                with sp.Fori(1, NE // 2) as pair:
                    for odd in range(2):
                        e = 2 * pair + odd
                        end = sp.value_load(blk_table[0:1, bass.ds(e - 1, 1)], min_val=1, max_val=MAXB)
                        for j in range(3):
                            sp.reg_add(count, PAIR * pair, loaded(EXPERTS[layer] + 3 * odd + j - 1))
                            sp.wait_ge((gate_psum, up_psum, y_psum)[j][layer], end)
                            load_expert(layer, j, e, EXPERTS[layer] + 3 * odd + j, pair)

        @block.tensor
        def _(pe):
            def wait_chunk(n):
                pe.wait_ge(first_half, loaded(n))
                pe.wait_ge(second_half, loaded(n))

            def mod_sums(n):
                wait_chunk(chunk_index(0, ("mod", n)))
                if n >= 2:
                    pe.wait_ge(mod_rows, n - 1)
                w = slot_ap(chunk_index(0, ("mod", n)))
                for k in range(2):
                    for g in range(4):
                        mm = pe.matmul(ps[32 * g:32 * g + 32, mod_bank(n), :], cond[:, 2 * g + k, :], w[:, 2 * g + k, :],
                                       start=(k == 0), stop=(k == 1), tile_position=(0, 32 * g))
                mm.then_inc(mod_psum[n // 12], 1)

            def mod_turn(n):
                pe.wait_ge(mod_rows, n + 1)
                for t in range(4):
                    at = 8 * n + 2 * t
                    mm = pe.matmul(ps[:, turned_bank(n), at:at + 2], mod_row[:, t * P:(t + 1) * P], cst("select"),
                                   start=True, stop=True)
                mm.then_inc(mod_turned, 1)

            def h1_transposes(layer):
                pe.wait_ge(xn_ready[layer], NT)
                for k in range(KD):
                    if k >= 2:
                        pe.wait_ge(h1_lat[layer], k - 1)
                        pe.wait_ge(h1_ctx[layer], k - 1)
                    for i in range(NT):
                        mm = pe.transpose(ps_flat[:, (k % 2) * 1024 + i * P:(k % 2) * 1024 + (i + 1) * P],
                                          xn[:, i, k * P:(k + 1) * P], ident)
                    mm.then_inc(h1_psum[layer], 1)

            def conv_projection(layer, ct):
                _, _, first, width = chunk_of(layer, ("conv", ct))
                n = chunk_index(layer, ("conv", ct))
                at = CONV_AT[ct]
                if at == 0:
                    pe.wait_ge(h1_lat[layer], KD)
                    pe.wait_ge(h1_ctx[layer], KD)
                if at % 4 == 0:
                    wait_chunk(n)
                if at >= 2:
                    pe.wait_ge(conv_act[layer], at - 1)
                w = slot_ap(n, width)
                col = ct * P - first
                for j, t0, tn in streams_of(layer):
                    for k in range(KD):
                        mm = pe.matmul(ps[:, (ct % 2) * 2 + j, 0:tn], w[:, k, col:col + P],
                                       h1T[:, k, t0:t0 + tn], start=(k == 0), stop=(k == KD - 1))
                mm.then_inc(conv_psum[layer], 1)

            def qk_transposes(layer, u):
                i = u % NT
                pe.wait_ge(qk_ready[layer], u + 1)
                if u >= 2:
                    pe.wait_ge(qkT_ready[layer], u - 1)
                elif layer == 0:
                    pe.wait_ge(mod_rows, MOD_CONV)
                    pe.wait_ge(mod_ready, 3)
                for r in range(2 if is_full(layer, i) else 0):
                    pe.transpose(ps[:, 6 + u % 2, r * P:(r + 1) * P], qk[:, r * P:(r + 1) * P], ident)
                pe.transpose(ps[:, 6 + u % 2, 2 * P:3 * P], qk[:, 256:384], ident).then_inc(qkT_psum[layer], 1)

            def qkv_projection(layer, u):
                i = u % NT
                n = chunk_index(layer, ("qkv", u))
                if i == 0:
                    wait_chunk(n)
                if u >= 2:
                    pe.wait_ge(qk_scaled[layer], u - 1)
                c0 = 0 if is_full(layer, i) else 256
                for k in range(KD):
                    mm = pe.matmul(ps[:, 4 + u % 2, c0:512], h1T[:, k, i * P:(i + 1) * P], slot_ap(n)[:, k, c0:512],
                                   start=(k == 0), stop=(k == KD - 1))
                mm.then_inc(qkv_psum[layer], 1)
                if u >= 1:
                    qk_transposes(layer, u - 1)
                if u == QKV_UNITS - 1:
                    qk_transposes(layer, u)

            def ln_sums(layer, which):
                if which == 0:
                    pe.wait_ge(conv_done[layer], 2 * len(streams_of(layer)))
                    src = catT[:, 2:4, :]
                else:
                    pe.wait_ge(ln_sq[layer], 2)
                    src = square
                for j, t0, tn in streams_of(layer):
                    for i in range(2):
                        mm = pe.matmul(ps[:, 4 + j, 0:tn], ones, src[:, i, t0:t0 + tn], start=(i == 0), stop=(i == 1))
                mm.then_inc(ln_psum[layer], 1)

            def scores(layer, u, unit):
                i, group, kv, r = unit
                a, b = key_tiles(layer, group, i)
                w = (b - a) * P
                q = qT[:, group * 2 + r, i * P:(i + 1) * P]
                bank = (u % 2) * 2
                if u >= 2:
                    pe.wait_ge(exp_done[layer], u - 1)
                if u == 0:
                    pe.wait_ge(keys_padded[layer], 8)
                if w:
                    masks = []
                    if group == 1 and i > 0:
                        masks.append((512 - w, cst("mask_prev")))
                    if group == 1 and i < XT - 1:
                        masks.append((512 - P, cst("mask_next")))
                    pe.matmul(ps[:, bank, 512 - w:512], q, kT_pad[:, group, kv, a * P:b * P], start=True, stop=not masks)
                    for m, (at, mask) in enumerate(masks):
                        pe.matmul(ps[:, bank, at:at + P], ident, mask, start=False, stop=m == len(masks) - 1)
                pe.matmul(ps[:, bank + 1, 0:C], q, kT_pad[:, group, kv, S:TOK], start=True, stop=True).then_inc(s_psum[layer], 1)

            def attend(layer, u, unit, last_pT):
                i, group, kv, r = unit
                a, b = key_tiles(layer, group, i)
                tiles = list(range(a, b)) + list(range(XT, NT))
                w = (b - a) * P
                pe.wait_ge(exp_done[layer], u + 1)
                if last_pT:
                    pe.wait_ge(*last_pT)
                for n in range(len(tiles)):
                    at = 512 - w + n * P
                    mm = pe.transpose(ps_flat[:, 2048 + at:2048 + at + P], prob[:, u % 2, at:at + P], ident)
                mm.then_inc(pT_psum[layer], 1)

            def weigh(layer, u, unit):
                i, group, kv, r = unit
                a, b = key_tiles(layer, group, i)
                tiles = list(range(a, b)) + list(range(XT, NT))
                w = (b - a) * P
                pe.wait_ge(pT_ready[layer], u + 1)
                if u >= 2:
                    pe.wait_ge(o_ready[layer], u - 1)
                for n, t in enumerate(tiles):
                    at = 512 - w + n * P
                    mm = pe.matmul(ps[:, 6 + u % 2, 0:HD], probT[:, u % 2, at:at + P],
                                   v_tok[:, t, group * P + kv * HD:group * P + (kv + 1) * HD],
                                   start=(n == 0), stop=(n == len(tiles) - 1))
                mm.then_inc(o_psum[layer], 1)

            def heads_turn(layer, u):
                pe.wait_ge(o_ready[layer], u)
                for j in range(2):
                    mm = pe.transpose(ps[:, 7, (2 + j) * P:(3 + j) * P], o_tok[:, j * P:(j + 1) * P], ident)
                mm.then_inc(oT_psum[layer], 1)

            def attention(layer):
                units = units_of(layer)
                pe.wait_ge(qkT_ready[layer], QKV_UNITS)
                scores(layer, 0, units[0])
                scores(layer, 1, units[1])
                last_pT = None
                for u, unit in enumerate(units):
                    if u == LN_MEAN:
                        pe.wait_ge(*last_pT)
                        ln_sums(layer, 0)
                        last_pT = (ln_centred[layer], 1)
                    if u == LN_VAR:
                        pe.wait_ge(*last_pT)
                        ln_sums(layer, 1)
                        last_pT = (ln_stds[layer], 1)
                    attend(layer, u, unit, last_pT)
                    if u + 2 < len(units):
                        scores(layer, u + 2, units[u + 2])
                    if u % 4 == 0 and u:
                        heads_turn(layer, u)
                    if u % 4 == 1 and u > 1:
                        pe.wait_ge(oT_ready[layer], u // 4)
                    weigh(layer, u, unit)
                    last_pT = (pT_ready[layer], u + 1)
                heads_turn(layer, len(units))
                pe.wait_ge(oT_ready[layer], len(units) // 4)
                return last_pT

            def broadcast(layer, b):
                pe.wait_ge(diag_ready[layer], b + 1)
                if b >= 2:
                    pe.wait_ge(bc_ready[layer], b - 1)
                g2 = b >= len(bc_list(layer))
                bank = 4 if g2 else (b % 2) * 2
                if g2:
                    pe.wait_ge(bc_ready[layer], b)
                for half in range(2):
                    mm = pe.matmul(ps[:, bank + half, :], ones, (diag2 if g2 else diag)[:, half * 4:half * 4 + 4, :],
                                   start=True, stop=True)
                mm.then_inc(bc_psum[layer], 1)

            def h2_transposes(layer, i):
                pe.wait_ge(h2_ready[layer], i + 1)
                if i >= 1:
                    pe.wait_ge(h2T_ready[layer], i)
                for k in range(KD):
                    mm = pe.transpose(ps_flat[:, 2048 + k * P:2048 + (k + 1) * P], h2_tok[:, i % 2, k * P:(k + 1) * P], ident)
                mm.then_inc(h2T_psum[layer], 1)

            def logits(layer, i):
                if i == 0:
                    pe.wait_ge(router_in, 16 * (layer + 1))
                pe.wait_ge(h2T_ready[layer], i + 1)
                for k in range(KD):
                    mm = pe.matmul(ps[:, 6, i * 36:(i + 1) * 36], h2T[:, i % 2, k, :], router_w[:, k, :],
                                   start=(k == 0), stop=(k == KD - 1))
                mm.then_inc(logit_psum[layer], 1)

            def out_projection(layer):
                tiles = tiles_of(layer)
                nb = len(bc_list(layer))
                n0 = FIRST[layer] + [c[0] for c in CHUNKS[layer]].index("w_out")
                for u in range(2 * tiles):
                    c, i = divmod(u, tiles)
                    if i == 0:
                        wait_chunk(n0 + c)
                    if u < 2:
                        pe.wait_ge(bc_ready[layer], nb)
                        pe.wait_ge(ln_done[layer], 2)
                    else:
                        pe.wait_ge(out_read[layer], u - 1)
                    w = slot_ap(n0 + c)
                    for k in range(8):
                        mm = pe.matmul(ps[:, u % 2, :], catT[:, k, i * P:(i + 1) * P], w[:, k, :],
                                       start=(k == 0), stop=(k == 7))
                    mm.then_inc(out_psum[layer], 1)
                    if c == 1 and i >= 1:
                        h2_transposes(layer, i - 1)
                    if c == 1 and i >= 2:
                        logits(layer, i - 2)
                h2_transposes(layer, tiles - 1)
                logits(layer, tiles - 2)
                logits(layer, tiles - 1)

            def ranks(layer):
                tiles = tiles_of(layer)
                picked = part(0, NT, NE)
                pe.wait_ge(chosen[layer], 1)
                pe.matmul(ps[:, 0, 0:tiles * NE], cst("before"), picked[:, 0:tiles, :], start=True, stop=False)
                for back in range(1, tiles):
                    pe.matmul(ps[:, 0, back * NE:tiles * NE], ones, picked[:, 0:tiles - back, :],
                              start=False, stop=back == tiles - 1)
                mm = pe.matmul(ps[:, 1, 0:tiles * NE], ones, picked[:, 0:tiles, :], start=True, stop=True)
                mm.then_inc(rank_psum[layer], 1)

            def lists(layer):
                n = 2 * tiles_of(layer)
                for a in range(n):
                    pe.wait_ge(onehots[layer], a + 1)
                    mm = pe.matmul(ps[:, 2, 0:B], part(2048, 12, 2 * B)[:, a, :], part(3584, 12, B)[:, a, :],
                                   start=(a == 0), stop=(a == n - 1))
                mm.then_inc(list_psum[layer], 1)

            def experts(layer):

                def in_transposes():
                    for j in range(4):
                        mm = pe.transpose(ps[:, 4, j * P:(j + 1) * P], xg[:, j * P:(j + 1) * P], ident)
                    mm.then_inc(xgT_psum[layer], 1)

                def side_by_side(bank, width, x, w, k, last):
                    for g in range(2):
                        mm = pe.matmul(ps[g * B:(g + 1) * B, bank, 0:width], x, w[:, k, g * width:(g + 1) * width],
                                       start=(k == 0), stop=(k == last), tile_position=(0, g * B))
                    return mm

                pe.wait_ge(gathered[layer], 16)
                in_transposes()
                with pe.Fori(0, NE // 2) as pair:
                    for odd in range(2):
                        n = EXPERTS[layer] + 3 * odd
                        gate, up, down = slot_ap(n), slot_ap(n + 1), down_ap(n + 2)
                        first = pe.value_load(blk_table[0:1, bass.ds(2 * pair + odd, 1)], min_val=0, max_val=MAXB)
                        end = pe.value_load(blk_table[0:1, bass.ds(2 * pair + odd + 1, 1)], min_val=1, max_val=MAXB)
                        with pe.Fori(first, end) as q:
                            pe.wait_ge(xgT_ready[layer], q + 1)
                            pe.wait_ge(first_half, loaded(n) + PAIR * pair)
                            for k in range(KD):
                                if k == KD // 2:
                                    pe.wait_ge(second_half, loaded(n) + PAIR * pair)
                                mm = side_by_side(0, DE // 2, xgT[:, k % 4, k // 4, :], gate, k, KD - 1)
                            mm.then_inc(gate_psum[layer], 1)
                            pe.wait_ge(first_half, loaded(n + 1) + PAIR * pair)
                            for k in range(KD):
                                if k == KD // 2:
                                    pe.wait_ge(second_half, loaded(n + 1) + PAIR * pair)
                                mm = side_by_side(1, DE // 2, xgT[:, k % 4, k // 4, :], up, k, KD - 1)
                            mm.then_inc(up_psum[layer], 1)
                            pe.wait_ge(gathered[layer], 16 * q + 32)
                            in_transposes()
                            pe.wait_ge(hid_ready[layer], q + 1)
                            for j in range(2):
                                mm = pe.transpose(ps[:, 2, j * P:(j + 1) * P], hid[:, j * P:(j + 1) * P], ident)
                            mm.then_inc(hidT_psum[layer], 1)
                            pe.wait_ge(y_ready[layer], q + 1)
                            pe.wait_ge(first_half, loaded(n + 2) + PAIR * pair)
                            pe.wait_ge(hidT_ready[layer], q + 1)
                            for k in range(4):
                                if k == 2:
                                    pe.wait_ge(second_half, loaded(n + 2) + PAIR * pair)
                                mm = side_by_side(3, D // 2, hidT[:, k % 2, k // 2, :], down, k, 3)
                            mm.then_inc(y_psum[layer], 1)

            pe.wait_ge(consts_in, 80)
            pe.wait_ge(cond_ready, 1)
            for layer in range(DEPTH):
                turned = None
                started = False
                for kind, n in steps_before_attention(layer):
                    if kind != "mod" and not started:
                        if turned is not None:
                            mod_turn(turned)
                            turned = None
                        h1_transposes(layer)
                        started = True
                    if kind == "conv":
                        conv_projection(layer, n)
                    if kind == "qkv":
                        qkv_projection(layer, n)
                    if turned is not None:
                        mod_turn(turned)
                        turned = None
                    if kind == "mod":
                        if n == MOD_CONV:
                            pe.wait_ge(conv_act[layer], 8)
                            pe.wait_ge(conv_mul[layer], 2)
                        mod_sums(n)
                        turned = n
                if layer == 0:
                    pe.wait_ge(mod_ready, 4)
                last_pT = attention(layer)
                pe.wait_ge(*last_pT)
                for b in range(len(bc_list(layer))):
                    broadcast(layer, b)
                out_projection(layer)
                for j, _, _ in streams_of(layer):
                    broadcast(layer, len(bc_list(layer)) + j)
                ranks(layer)
                lists(layer)
                pe.wait_ge(bc_ready[layer], len(bc_list(layer)) + len(streams_of(layer)))
                pe.wait_ge(route_done[layer], 1)
                experts(layer)

        @block.vector
        def _(ve):
            steps = [0]

            def own(ins):
                steps[0] += 1
                ins.then_inc(vec, 1)

            def settle(back=0):
                ve.wait_ge(vec, steps[0] - back)

            def amplitude(layer, name, column):
                for j in range(2):
                    ins = nc.vector.scalar_tensor_tensor(out=amp[:, j, :], in0=mod[:, layer, column:column + KD, j],
                                                         scalar=1.0, in1=sml(layer, name), op0=ALU.add, op1=ALU.mult)
                    own(ins)
                settle()

            def mod_copy(layer, first, end, n, turned):
                ve.wait_ge(mod_turned, turned)
                bias = sml(layer, "mod_b")[:, 4 * first:4 * end].unsqueeze(2).to_broadcast([P, 4 * (end - first), 2])
                at = 8 * (12 * layer + first)
                nc.vector.tensor_tensor(mod[:, layer, 4 * first:4 * end, :],
                                        ps[:, n, at:at + 8 * (end - first)].rearrange("p (t j) -> p t j", j=2), bias,
                                        ALU.add).then_inc(mod_ready, 1)

            def scale_tokens(layer):
                ve.wait_ge(rms_std[layer], 1)
                own(nc.vector.reciprocal(rstd[:, :], rstd[:, :]))
                settle()
                for i in range(NT):
                    nc.vector.tensor_scalar(xn[:, i, :], xres[:, i, :], rstd[:, i:i + 1], None,
                                            ALU.mult).then_inc(xn_ready[layer], 1)

            def h1_context(layer):
                for k in range(KD):
                    ve.wait_ge(h1_psum[layer], k + 1)
                    nc.vector.tensor_scalar(h1T[:, k, S:TOK], ps[:, (k % 2) * 2 + 1, 0:C], amp[:, 1, k:k + 1],
                                            mod[:, layer, k, 1:2], ALU.mult, ALU.add).then_inc(h1_ctx[layer], 1)

            def clear_pads(layer):
                for pads in ((cx, (0, 1 + S, 2 + S + C), 1), (glu, (0, 15 + S, 30 + S + C), 15)):
                    for at in pads[1]:
                        ins = nc.vector.memset(pads[0][:, :, at:at + pads[2]], 0.0)
                ins.then_inc(pads_ready[layer], 1)
                ve.wait_ge(pads_ready[layer], 1)

            def conv_a_group(layer):
                w = sml(layer, "conv_a")
                for i in range(2):
                    ve.wait_ge(conv_act[layer], CONV_ACT[2 + i])
                    ve.wait_ge(conv_psum[layer], CONV_AT[4 + i] + 1)
                    for j, t0, tn in streams_of(layer):
                        at = t0 + 1 + j
                        ins = nc.vector.tensor_tensor(cx[:, i, at:at + tn], cx[:, i, at:at + tn],
                                                      ps[:, (i % 2) * 2 + j, 0:tn], ALU.mult)
                    ins.then_inc(conv_mul[layer], 1)
                for i in range(2):
                    ve.wait_ge(conv_mul[layer], i + 1)
                    for tap in range(TAPS_A):
                        for j, t0, tn in streams_of(layer):
                            src = cx[:, i, t0 + j + tap:t0 + j + tap + tn]
                            dst = conv_a[:, i, t0:t0 + tn]
                            wt = w[:, i * TAPS_A + tap:i * TAPS_A + tap + 1]
                            if tap == 0:
                                own(nc.vector.tensor_scalar(dst, src, wt, None, ALU.mult))
                            else:
                                own(nc.vector.scalar_tensor_tensor(out=dst, in0=src, scalar=wt, in1=dst,
                                                                   op0=ALU.mult, op1=ALU.add))
                        settle()
                    for j, t0, tn in streams_of(layer):
                        own(nc.vector.tensor_tensor(catT[:, i, t0:t0 + tn], catT[:, i, t0:t0 + tn],
                                                    conv_a[:, i, t0:t0 + tn], ALU.mult))

            def glu_product(layer):
                for i in range(2):
                    ve.wait_ge(conv_act[layer], CONV_ACT[8 + i])
                    for j, t0, tn in streams_of(layer):
                        at = t0 + 15 * (1 + j)
                        own(nc.vector.tensor_tensor(glu[:, i, at:at + tn], glu[:, i, at:at + tn],
                                                    catT[:, 2 + i, t0:t0 + tn], ALU.mult))
                settle()

            def conv_b_tap(layer, tap):
                w = sml(layer, "conv_b")
                ns = len(streams_of(layer))
                for i in range(2):
                    if tap:
                        settle(0 if tap == TAPS_B - 1 else ns)
                    for j, t0, tn in streams_of(layer):
                        src = glu[:, i, t0 + 15 * j + tap:t0 + 15 * j + tap + tn]
                        dst = catT[:, 2 + i, t0:t0 + tn]
                        wt = w[:, i * TAPS_B + tap:i * TAPS_B + tap + 1]
                        if tap == 0:
                            own(nc.vector.tensor_scalar(dst, src, wt, sml(layer, "conv_bias")[:, i:i + 1],
                                                        ALU.mult, ALU.add))
                            continue
                        ins = nc.vector.scalar_tensor_tensor(out=dst, in0=src, scalar=wt, in1=dst,
                                                             op0=ALU.mult, op1=ALU.add)
                        if tap == TAPS_B - 1:
                            ins.then_inc(conv_done[layer], 1)
                        else:
                            own(ins)

            def rotate(layer, u):
                group, i = divmod(u, NT)
                full = is_full(layer, i)
                c0 = 0 if full else 256
                nh = 6 if full else 2
                h0 = 6 - nh
                gains = row[:, layer, group * 2 * HD:(group + 1) * 2 * HD]
                ve.wait_ge(qk_square[layer], u + 1)
                nc.vector.tensor_reduce(qk_sum[:, h0:6], qk_tmp[:, c0:384].rearrange("p (h d) -> p h d", d=HD),
                                        AX.X, ALU.add).then_inc(qk_sums[layer], 1)
                ve.wait_ge(qk_stds[layer], u + 1)
                own(nc.vector.reciprocal(qk_rstd[:, h0:6], qk_std[:, h0:6]))
                settle()
                if u >= 1:
                    ve.wait_ge(qkT_psum[layer], u)
                bank = ps[:, 4 + u % 2, c0:384].rearrange("p (h d) -> p h d", d=HD)
                heads = qk[:, c0:384].rearrange("p (h d) -> p h d", d=HD)
                if full:
                    own(nc.vector.tensor_tensor(qk[:, 0:256].rearrange("p (r kv d) -> p kv r d", r=2, kv=2),
                                                bank[:, 0:4, :].rearrange("p (kv r) d -> p kv r d", kv=2),
                                                qk_rstd[:, 0:4].rearrange("p (kv r) -> p kv r", kv=2).unsqueeze(3)
                                                .to_broadcast([P, 2, 2, HD]), ALU.mult))
                nc.vector.tensor_tensor(heads[:, nh - 2:nh, :], bank[:, nh - 2:nh, :],
                                        qk_rstd[:, 4:6].unsqueeze(2).to_broadcast([P, 2, HD]),
                                        ALU.mult).then_inc(qk_scaled[layer], 1)
                settle()
                ve.wait_ge(qk_scaled[layer], u + 1)
                if full:
                    own(nc.vector.tensor_tensor(heads[:, 0:4, :], heads[:, 0:4, :],
                                                gains[:, 0:HD].unsqueeze(1).to_broadcast([P, 4, HD]), ALU.mult))
                ins = nc.vector.tensor_tensor(heads[:, nh - 2:nh, :], heads[:, nh - 2:nh, :],
                                              gains[:, HD:2 * HD].unsqueeze(1).to_broadcast([P, 2, HD]), ALU.mult)
                if i >= XT:
                    ins.then_inc(qk_ready[layer], 1)
                    return
                own(ins)
                settle()
                cos = cst("cos")[:, i * HD:(i + 1) * HD]
                sin = cst("sin")[:, i * HD:(i + 1) * HD]
                turned = qk_tmp.rearrange("p (h a b d) -> p h a b d", h=6, a=2, b=2)
                plain = qk.rearrange("p (h a b d) -> p h a b d", h=6, a=2, b=2)
                sins = sin.rearrange("p (a b d) -> p a b d", a=2, b=2)
                for b in range(2):
                    own(nc.vector.tensor_tensor(turned[:, :, :, b, :], plain[:, :, :, 1 - b, :],
                                                sins[:, :, b, :].unsqueeze(1).to_broadcast([P, 6, 2, 16]), ALU.mult))
                settle()
                own(nc.vector.tensor_tensor(heads, heads, cos.unsqueeze(1).to_broadcast([P, 6, HD]), ALU.mult))
                settle()
                nc.vector.tensor_tensor(qk[:, :], qk[:, :], qk_tmp[:, :], ALU.add).then_inc(qk_ready[layer], 1)

            def store_qk(layer, u):
                group, i = divmod(u, NT)
                ve.wait_ge(qkT_psum[layer], u + 1)
                bank = ps[:, 6 + u % 2, 0:384].rearrange("p (r t) -> p r t", r=3)
                if is_full(layer, i):
                    own(nc.vector.tensor_copy(qT[:, group * 2:group * 2 + 2, i * P:(i + 1) * P], bank[:, 0:2, :]))
                nc.vector.tensor_copy(kT[:, group, i * P:(i + 1) * P], bank[:, 2, :]).then_inc(qkT_ready[layer], 1)

            def ln_centre(layer):
                ve.wait_ge(ln_psum[layer], 1)
                for i in range(2):
                    for j, t0, tn in streams_of(layer):
                        ins = nc.vector.scalar_tensor_tensor(out=catT[:, 2 + i, t0:t0 + tn], in0=ps[:, 4 + j, 0:tn],
                                                             scalar=-1.0 / W_CF, in1=catT[:, 2 + i, t0:t0 + tn],
                                                             op0=ALU.mult, op1=ALU.add)
                ins.then_inc(ln_centred[layer], 1)

            def ln_scale(layer):
                n = S + (C if layer == 0 else 0)
                ve.wait_ge(ln_stds[layer], 1)
                own(nc.vector.reciprocal(ln_std[:, 0:n], ln_std[:, 0:n]))
                settle()
                for i in range(2):
                    nc.vector.tensor_tensor(catT[:, 2 + i, 0:n], catT[:, 2 + i, 0:n], ln_std[:, 0:n],
                                            ALU.mult).then_inc(ln_scaled[layer], 1)

            def unit_max(layer, u, unit):
                i, group, kv, r = unit
                a, b = key_tiles(layer, group, i)
                w = (b - a) * P
                base = (u % 2) * 1024
                ve.wait_ge(s_psum[layer], u + 1)
                own(nc.vector.tensor_reduce(stat[:, u % 4, 3:4], ps_flat[:, base + 512 - w:base + TOK], AX.X, ALU.max))
                settle()
                if group == 0:
                    ins = nc.vector.tensor_scalar(stat[:, u % 4, 0:1], stat[:, u % 4, 3:4], -SCALE, None, ALU.mult)
                else:
                    h = 2 * kv + r
                    ins = nc.vector.tensor_scalar(stat[:, u % 4, 0:1], stat[:, u % 4, 3:4], -SCALE,
                                                  nsink[:, layer, h:h + 1], ALU.mult, ALU.min)
                ins.then_inc(neg_max[layer], 1)

            def unit_out(layer, u, unit):
                i, group, kv, r = unit
                h = 2 * kv + r
                total = stat[:, u % 4, 1:2]
                if group == 1:
                    ve.wait_ge(sink_exp[layer], 4 * (u // 8) + u % 4 + 1)
                    own(nc.vector.tensor_tensor(total, total, stat[:, u % 4, 2:3], ALU.add))
                    settle()
                else:
                    ve.wait_ge(exp_done[layer], u + 1)
                own(nc.vector.reciprocal(stat[:, u % 4, 4:5], total))
                settle()
                ve.wait_ge(o_psum[layer], u + 1)
                if u >= 4 and u % 4 == 0:
                    ve.wait_ge(oT_psum[layer], u // 4)
                nc.vector.tensor_scalar(o_tok[:, h * HD:(h + 1) * HD], ps[:, 6 + u % 2, 0:HD], stat[:, u % 4, 4:5],
                                        None, ALU.mult).then_inc(o_ready[layer], 1)

            def heads_out(layer, u, unit):
                i, group, _, _ = unit
                ve.wait_ge(oT_psum[layer], u // 4 + 1)
                nc.vector.tensor_copy(catT[:, 4 + 2 * group:6 + 2 * group, i * P:(i + 1) * P],
                                      ps[:, 7, 2 * P:4 * P].rearrange("p (j t) -> p j t", j=2)).then_inc(oT_ready[layer], 1)

            def attention(layer):
                units = units_of(layer)
                unit_max(layer, 0, units[0])
                unit_max(layer, 1, units[1])
                for u, unit in enumerate(units):
                    if u == LN_MEAN:
                        ln_centre(layer)
                    if u == LN_VAR:
                        ln_scale(layer)
                    if u + 2 < len(units):
                        unit_max(layer, u + 2, units[u + 2])
                    if u % 4 == 0 and u:
                        heads_out(layer, u - 1, units[u - 1])
                    unit_out(layer, u, unit)
                heads_out(layer, len(units) - 1, units[-1])

            def make_diag(layer, b, values, where):
                if b >= 1:
                    ve.wait_ge(bc_psum[layer], b)
                nc.vector.tensor_tensor(where, ident.unsqueeze(1).to_broadcast([P, KD, P]),
                                        values.unsqueeze(2).to_broadcast([P, KD, P]),
                                        ALU.mult).then_inc(diag_ready[layer], 1)

            def residual(layer, u):
                tiles = tiles_of(layer)
                c, i = divmod(u, tiles)
                j = 0 if i < XT else 1
                ve.wait_ge(out_psum[layer], u + 1)
                if u == 0:
                    ve.wait_ge(bc_ready[layer], len(bc_list(layer)))
                cols = slice(c * 512, (c + 1) * 512)
                if u >= 2:
                    ve.wait_ge(x_mid[layer], u - 1)
                nc.vector.tensor_tensor(scratch[:, u % 2, :], ps[:, u % 2, :], g1_b[:, j, cols], ALU.mult).then_inc(out_read[layer], 1)
                ve.wait_ge(out_read[layer], u + 1)
                nc.vector.tensor_tensor(xres[:, i, cols], xres[:, i, cols], scratch[:, u % 2, :], ALU.add).then_inc(x_mid[layer], 1)

            def norm2(layer, i):
                j = 0 if i < XT else 1
                ve.wait_ge(std2[layer], i + 1)
                own(nc.vector.reciprocal(rstd[:, i:i + 1], rstd[:, i:i + 1]))
                settle()
                if i >= 2:
                    ve.wait_ge(h2T_psum[layer], i - 1)
                    ve.wait_ge(h2_stored[layer], 16 * (i - 1))
                own(nc.vector.scalar_tensor_tensor(out=h2_tok[:, i % 2, :], in0=xres[:, i, :], scalar=rstd[:, i:i + 1],
                                                   in1=amp2_b[:, j, :], op0=ALU.mult, op1=ALU.mult))
                settle()
                nc.vector.tensor_tensor(h2_tok[:, i % 2, :], h2_tok[:, i % 2, :], sh2_b[:, j, :],
                                        ALU.add).then_inc(h2_ready[layer], 1)

            def route(layer):
                t = tiles_of(layer)
                picked = part(0, NT, NE)[:, 0:t, :]
                logit = part(192, NT, NG + NE)[:, 0:t, :]
                glog = logit[:, :, 0:NG]
                elog = logit[:, :, NG:NG + NE]
                tmp = part(408, NT, NE)[:, 0:t, :]
                one = [part(600, NT, NE)[:, 0:t, :], part(792, NT, NE)[:, 0:t, :]]
                g_one = part(984, NT, NG)[:, 0:t, :]
                g_tmp = part(1008, NT, NG)[:, 0:t, :]
                best = part(1032, NT)[:, 0:t]
                index = part(1038, NT)[:, 0:t]
                top = [part(1044, NT)[:, 0:t], part(1050, NT)[:, 0:t]]
                p_grp = part(1056, NT)[:, 0:t]
                ask = part(1062, NT, NG + 1)[:, 0:t, :]
                answer = part(1092, NT, NG + 1)[:, 0:t, :]
                rank = part(1130, NT, NE)[:, 0:t, :]
                count = part(1322, NE)
                over = part(1354, NE, 12)
                blocks = part(1738, NE)
                ends = part(1770, NE)
                starts = part(1802, NE)
                zeros = part(1834, NE)
                dest = part(1870, 2, NT)[:, :, 0:t]
                dest_q = part(1882, 2, NT)[:, :, 0:t]
                dest_r = part(1894, 2, NT)[:, :, 0:t]
                int_a = part(1906, 2, NT).bitcast(I32)[:, :, 0:t]
                int_b = part(1918, 2, NT).bitcast(I32)[:, :, 0:t]
                value = part(1930, 2, NT)[:, :, 0:t]
                hot_r = part(2048, 12, 2 * B)
                hot_q = part(3584, 12, B)

                def wide(v, n):
                    return v.unsqueeze(2).to_broadcast([P, t, n])

                def over_tiles(v, n):
                    return v.unsqueeze(1).to_broadcast([P, t, n])

                def first_best(values, names, n, best_, hot, work):
                    own(nc.vector.tensor_reduce(best_, values, AX.X, ALU.max))
                    settle()
                    own(nc.vector.tensor_tensor(work, values, wide(best_, n), ALU.is_equal))
                    settle()
                    own(nc.vector.tensor_scalar(work, work, -1000.0, 1000.0, ALU.mult, ALU.add))
                    settle()
                    own(nc.vector.tensor_tensor(work, work, over_tiles(names, n), ALU.add))
                    settle()
                    own(nc.vector.tensor_reduce(index, work, AX.X, ALU.min))
                    settle()
                    own(nc.vector.tensor_tensor(hot, wide(index, n), over_tiles(names, n), ALU.is_equal))
                    settle()

                ve.wait_ge(logit_psum[layer], t)
                own(nc.vector.tensor_tensor(logit, ps[:, 6, 0:t * 36].rearrange("p (i n) -> p i n", n=36),
                                            over_tiles(row[:, layer, 4 * HD + 4:N_ROW], NG + NE), ALU.add))
                settle()
                first_best(glog, cst("slot")[:, 0:NG], NG, best, g_one, g_tmp)
                own(nc.vector.tensor_tensor(ask[:, :, 0:NG], glog, wide(best, NG), ALU.subtract))
                own(nc.vector.tensor_scalar(g_one, g_one, -1.0, -NEG, ALU.add, ALU.mult))
                settle()
                for i in range(t):
                    own(nc.vector.tensor_tensor(elog[:, i, :].rearrange("p (g e) -> p g e", g=NG),
                                                elog[:, i, :].rearrange("p (g e) -> p g e", g=NG),
                                                g_one[:, i, :].unsqueeze(2).to_broadcast([P, NG, NPG]), ALU.add))
                settle()
                first_best(elog, cst("slot")[:, 0:NE], NE, top[0], one[0], tmp)
                own(nc.vector.tensor_scalar(tmp, one[0], NEG, None, ALU.mult))
                settle()
                own(nc.vector.tensor_tensor(elog, elog, tmp, ALU.add))
                settle()
                first_best(elog, cst("slot")[:, 0:NE], NE, top[1], one[1], tmp)
                nc.vector.tensor_tensor(picked, one[0], one[1], ALU.add).then_inc(chosen[layer], 1)
                nc.vector.tensor_tensor(ask[:, :, NG:NG + 1], top[1].unsqueeze(2), top[0].unsqueeze(2),
                                        ALU.subtract).then_inc(route_ask[layer], 1)
                own(nc.vector.memset(zeros, 0.0))
                ve.wait_ge(route_exp[layer], 1)
                own(nc.vector.tensor_reduce(p_grp, answer[:, :, 0:NG], AX.X, ALU.add))
                own(nc.vector.tensor_scalar(best.unsqueeze(2), answer[:, :, NG:NG + 1], 1.0, None, ALU.add))
                settle()
                own(nc.vector.tensor_tensor(best, best, p_grp, ALU.mult))
                settle()
                own(nc.vector.reciprocal(gates[:, 0, 0:t], best))
                settle()
                own(nc.vector.tensor_tensor(gates[:, 1, 0:t].unsqueeze(2), gates[:, 0, 0:t].unsqueeze(2),
                                            answer[:, :, NG:NG + 1], ALU.mult))
                ve.wait_ge(rank_psum[layer], 1)
                own(nc.vector.tensor_copy(rank, ps[:, 0, 0:t * NE].rearrange("p (i n) -> p i n", n=NE)))
                own(nc.vector.tensor_reduce(count, ps[:, 1, 0:t * NE].rearrange("p (i n) -> p n i", n=NE), AX.X, ALU.add))
                settle()
                own(nc.vector.tensor_tensor(over, count.unsqueeze(2).to_broadcast([P, NE, 12]),
                                            cst("limit").unsqueeze(1).to_broadcast([P, NE, 12]), ALU.is_gt))
                settle()
                own(nc.vector.tensor_reduce(blocks, over, AX.X, ALU.add))
                settle()
                own(nc.vector.tensor_scalar(blocks, blocks, 1.0, None, ALU.max))
                settle()
                own(nc.vector.tensor_tensor_scan(ends, blocks, zeros, 0.0, ALU.add, ALU.add))
                settle()
                own(nc.vector.tensor_tensor(starts, ends, blocks, ALU.subtract))
                settle()
                own(nc.vector.tensor_copy(blk_table[0:1, 0:NE], starts[0:1, :]))
                own(nc.vector.tensor_copy(blk_table[0:1, NE:NE + 1], ends[0:1, NE - 1:NE]))
                own(nc.vector.scalar_tensor_tensor(out=rank, in0=over_tiles(starts, NE), scalar=float(B), in1=rank,
                                                   op0=ALU.mult, op1=ALU.add))
                settle()
                for c in range(2):
                    own(nc.vector.tensor_tensor(tmp, rank, one[c], ALU.mult))
                    settle()
                    own(nc.vector.tensor_reduce(dest[:, c, :], tmp, AX.X, ALU.add))
                    settle()
                own(nc.vector.tensor_copy(int_a, dest))
                settle()
                own(nc.vector.tensor_scalar(int_b, int_a, 6, None, ALU.arith_shift_right))
                own(nc.vector.tensor_scalar(int_a, int_a, B - 1, None, ALU.bitwise_and))
                for c in range(2):
                    own(nc.vector.tensor_scalar(value[:, c, :], cst("token")[:, 0:t], float(c * t * P), None, ALU.add))
                settle()
                own(nc.vector.tensor_copy(dest_q, int_b))
                own(nc.vector.tensor_copy(dest_r, int_a))
                settle()
                for a in range(2 * t):
                    c, i = divmod(a, t)
                    own(nc.vector.tensor_scalar(hot_r[:, a, :], cst("slot"), dest_r[:, c, i:i + 1], None, ALU.is_equal))
                    nc.vector.tensor_scalar(hot_q[:, a, :], cst("slot")[:, 0:B], dest_q[:, c, i:i + 1], value[:, c, i:i + 1],
                                            ALU.is_equal, ALU.mult).then_inc(onehots[layer], 1)
                ve.wait_ge(list_psum[layer], 1)
                full = part(2048, B)
                want = part(2112, B)
                empty = part(2176, B)
                big = part(2240, B)
                dump = part(2304, 1)
                half = cst("half")
                own(nc.vector.tensor_scalar(full, ps[:, 2, 0:B], -1.0, None, ALU.add))
                own(nc.vector.tensor_scalar(dump, cst("slot_row"), float(2 * t * P + 1), None, ALU.add))
                settle()
                own(nc.vector.tensor_scalar(big, full, float(t * P), float(-t * P), ALU.is_ge, ALU.mult))
                own(nc.vector.tensor_scalar(empty, full, 0.0, dump[:, 0:1], ALU.is_lt, ALU.mult))
                settle()
                own(nc.vector.tensor_tensor(want, full, big, ALU.add))
                own(nc.vector.tensor_tensor(empty, empty, full, ALU.add))
                settle()
                own(nc.vector.tensor_scalar(want, want, 0.0, 2.0, ALU.max, ALU.mult))
                settle()
                own(nc.vector.tensor_scalar(list_gather[:, 0:MAXB + 1], want[:, 0:MAXB + 1], half, None, ALU.add))
                nc.vector.tensor_scalar(list_scatter[:, 0:MAXB + 1], empty[:, 0:MAXB + 1], 2.0, half, ALU.mult,
                                        ALU.add).then_inc(route_done[layer], 1)
                settle()

            def experts(layer):
                blocks = ve.value_load(blk_table[0:1, NE:NE + 1], min_val=1, max_val=MAXB)
                def turn_in():
                    nc.vector.tensor_copy(xgT[:, :, :, :].rearrange("p j h t -> p (j h t)"),
                                          ps[:, 4, :]).then_inc(xgT_ready[layer], 1)

                ve.wait_ge(xgT_psum[layer], 1)
                turn_in()
                with ve.Fori(0, blocks) as q:
                    ve.wait_ge(silu_ready[layer], q + 1)
                    ve.wait_ge(up_psum[layer], q + 1)
                    nc.vector.tensor_tensor(hid, silu, ps[:, 1, 0:256], ALU.mult).then_inc(hid_ready[layer], 1)
                    ve.wait_ge(hidT_psum[layer], q + 1)
                    nc.vector.tensor_copy(hidT[:, :, :, :].rearrange("p j h t -> p (j h t)"),
                                          ps[:, 2, 0:256]).then_inc(hidT_ready[layer], 1)
                    ve.wait_ge(xgT_psum[layer], q + 2)
                    turn_in()

            def combine(layer, i):
                j = 0 if i < XT else 1
                y = y_pair[:, i % 2, :, :]
                ve.wait_ge(y_loaded[i % 2][layer], 16 * (i // 2 + 1))
                ve.wait_ge(y_scaled[layer], i + 1)
                own(nc.vector.scalar_tensor_tensor(out=y[:, 0, :], in0=y[:, 1, :], scalar=gates[:, 1, i:i + 1],
                                                   in1=y[:, 0, :], op0=ALU.mult, op1=ALU.add))
                settle()
                own(nc.vector.tensor_tensor(y[:, 0, :], y[:, 0, :], g2_b[:, j, :], ALU.mult))
                settle()
                nc.vector.tensor_tensor(xres[:, i, :], xres[:, i, :], y[:, 0, :], ALU.add).then_inc(x_done[layer], 1)

            ve.wait_ge(consts_in, 80)
            mod_copy(0, 0, MOD_FIRST, turned_bank(0), MOD_FIRST)
            for layer in range(DEPTH):
                own(nc.vector.tensor_scalar(nsink[:, layer, :], row[:, layer, 4 * HD:4 * HD + 4], -1.0, None, ALU.mult))
                ve.wait_ge(mod_ready, 1 if layer == 0 else 4)
                amplitude(layer, "norm1", KD)
                scale_tokens(layer)
                h1_context(layer)
                clear_pads(layer)
                glu_product(layer)
                for tap in range(TAPS_EARLY):
                    conv_b_tap(layer, tap)
                conv_a_group(layer)
                if layer == 0:
                    mod_copy(0, MOD_FIRST, 12, turned_bank(MOD_FIRST), MOD_CONV)
                    mod_copy(1, 0, MOD_CONV - 12, turned_bank(MOD_FIRST), MOD_CONV)
                for u in range(QKV_UNITS):
                    rotate(layer, u)
                    if TAPS_EARLY + u < TAPS_B:
                        conv_b_tap(layer, TAPS_EARLY + u)
                    store_qk(layer, u)
                if layer == 0:
                    mod_copy(1, MOD_CONV - 12, 12, turned_bank(MOD_CONV), 24)
                attention(layer)
                amplitude(layer, "norm2", 4 * KD)
                for b, (name, column, _, j) in enumerate(bc_list(layer)):
                    values = amp[:, j, :] if column is None else mod[:, layer, column:column + KD, j]
                    make_diag(layer, b, values, diag)
                tiles = tiles_of(layer)
                for u in range(2 * tiles):
                    if u > tiles:
                        norm2(layer, u - tiles - 1)
                    residual(layer, u)
                norm2(layer, tiles - 1)
                route(layer)
                experts(layer)
                for i in range(tiles):
                    combine(layer, i)

        @block.scalar
        def _(ac):
            steps = [0]

            def own(ins):
                steps[0] += 1
                ins.then_inc(act_step, 1)

            def settle():
                ac.wait_ge(act_step, steps[0])

            eps = cst("eps")

            def rms_of_tokens(layer):
                for i in range(NT):
                    if layer == 0:
                        if i == 0:
                            ac.wait_ge(x_in, 32)
                    else:
                        if i + 1 < NT:
                            if i == 0:
                                combine(layer - 1, 0)
                            combine(layer - 1, i + 1)
                        ac.wait_ge(x_done[layer - 1], i + 1)
                    own(nc.scalar.activation(xn[:, i, :], xres[:, i, :], ACT.Square, accum_out=ssq[:, i:i + 1]))
                settle()
                nc.scalar.activation(rstd[:, :], ssq[:, :], ACT.Sqrt, bias=eps, scale=1.0 / D).then_inc(rms_std[layer], 1)

            def h1_latents(layer):
                for k in range(KD):
                    ac.wait_ge(h1_psum[layer], k + 1)
                    if k == 0:
                        ac.wait_ge(xn_ready[layer], 1)
                    nc.scalar.activation(h1T[:, k, 0:S], ps[:, (k % 2) * 2, :], ACT.Identity, bias=mod[:, layer, k, 0:1],
                                         scale=amp[:, 0, k:k + 1]).then_inc(h1_lat[layer], 1)

            def mod_sums(n):
                ac.wait_ge(mod_psum[n // 12], n % 12 + 1)
                if n >= 1:
                    ac.wait_ge(mod_turned, n)
                nc.scalar.copy(mod_row[:, :], ps[:, mod_bank(n), :]).then_inc(mod_rows, 1)

            def conv_copies(layer, tiles):
                for ct in tiles:
                    ac.wait_ge(conv_psum[layer], CONV_AT[ct] + 1)
                    if ct == 6:
                        ac.wait_ge(pads_ready[layer], 1)
                    i = ct % 2
                    for j, t0, tn in streams_of(layer):
                        src = ps[:, i * 2 + j, 0:tn]
                        if ct < 2:
                            ins = nc.scalar.copy(catT[:, i, t0:t0 + tn], src)
                        elif ct < 4:
                            ins = nc.scalar.copy(cx[:, i, t0 + 1 + j:t0 + 1 + j + tn], src)
                        elif ct < 8:
                            ins = nc.scalar.copy(glu[:, i, t0 + 15 * (1 + j):t0 + 15 * (1 + j) + tn], src)
                        else:
                            ins = nc.scalar.activation(catT[:, 2 + i, t0:t0 + tn], src, ACT.Sigmoid)
                    ins.then_inc(conv_act[layer], 1)

            def qkv_copies(layer, u):
                group, i = divmod(u, NT)
                full = is_full(layer, i)
                c0 = 0 if full else 256
                h0 = 0 if full else 4
                ac.wait_ge(qkv_psum[layer], u + 1)
                if u == 0:
                    ac.wait_ge(conv_mul[layer], 2)
                own(nc.scalar.copy(v_tok[:, i, group * P:(group + 1) * P], ps[:, 4 + u % 2, 384:512]))
                if u >= 1:
                    ac.wait_ge(qk_ready[layer], u)
                nc.scalar.activation(qk_tmp[:, c0:384], ps[:, 4 + u % 2, c0:384], ACT.Square).then_inc(qk_square[layer], 1)
                ac.wait_ge(qk_sums[layer], u + 1)
                nc.scalar.activation(qk_std[:, h0:6], qk_sum[:, h0:6], ACT.Sqrt, bias=eps,
                                     scale=1.0 / HD).then_inc(qk_stds[layer], 1)

            def ln_squares(layer):
                n = S + (C if layer == 0 else 0)
                ac.wait_ge(ln_centred[layer], 1)
                for i in range(2):
                    nc.scalar.activation(square[:, i, 0:n], catT[:, 2 + i, 0:n], ACT.Square).then_inc(ln_sq[layer], 1)

            def ln_roots(layer):
                n = S + (C if layer == 0 else 0)
                ac.wait_ge(ln_psum[layer], 2)
                nc.scalar.activation(ln_std[:, 0:n], ps_flat[:, 2048:2048 + n], ACT.Sqrt, bias=eps,
                                     scale=1.0 / W_CF).then_inc(ln_stds[layer], 1)

            def ln_silu(layer):
                n = S + (C if layer == 0 else 0)
                for i in range(2):
                    ac.wait_ge(ln_scaled[layer], i + 1)
                    nc.scalar.activation(catT[:, 2 + i, 0:n], catT[:, 2 + i, 0:n], ACT.Silu,
                                         bias=sml(layer, "ln_b")[:, i:i + 1],
                                         scale=sml(layer, "ln_g")[:, i:i + 1]).then_inc(ln_done[layer], 1)

            def unit_exp(layer, u, unit):
                i, group, kv, r = unit
                a, b = key_tiles(layer, group, i)
                w = (b - a) * P
                base = (u % 2) * 1024
                ac.wait_ge(neg_max[layer], u + 1)
                if u >= 2:
                    ac.wait_ge(pT_psum[layer], u - 1)
                if u >= 4:
                    ac.wait_ge(o_ready[layer], u - 3)
                nc.scalar.activation(prob[:, u % 2, 512 - w:TOK], ps_flat[:, base + 512 - w:base + TOK], ACT.Exp,
                                     bias=stat[:, u % 4, 0:1], scale=SCALE,
                                     accum_out=stat[:, u % 4, 1:2]).then_inc(exp_done[layer], 1)
                if group == 1:
                    h = 2 * kv + r
                    nc.scalar.activation(stat[:, u % 4, 2:3], row[:, layer, 4 * HD + h:4 * HD + h + 1], ACT.Exp,
                                         bias=stat[:, u % 4, 0:1]).then_inc(sink_exp[layer], 1)

            def unit_pT(layer, u, unit):
                i, group, _, _ = unit
                a, b = key_tiles(layer, group, i)
                w = (b - a) * P
                ac.wait_ge(pT_psum[layer], u + 1)
                if u >= 2:
                    ac.wait_ge(o_psum[layer], u - 1)
                nc.scalar.copy(probT[:, u % 2, 512 - w:TOK], ps_flat[:, 2048 + 512 - w:2048 + TOK]).then_inc(pT_ready[layer], 1)

            def pad_keys(layer):
                ac.wait_ge(qkT_ready[layer], QKV_UNITS)
                ac.wait_ge(qkv_psum[layer], QKV_UNITS)
                for group in range(2):
                    for half, kv in ((slice(0, HD), 0), (slice(HD, P), 1)):
                        nc.scalar.copy(kT_pad[half, group, kv, :], kT[half, group, :]).then_inc(keys_padded[layer], 1)

            def attention(layer):
                units = units_of(layer)
                pad_keys(layer)
                unit_exp(layer, 0, units[0])
                unit_exp(layer, 1, units[1])
                for u, unit in enumerate(units):
                    if u == LN_MEAN:
                        ln_squares(layer)
                    if u == LN_VAR:
                        ln_roots(layer)
                    unit_pT(layer, u, unit)
                    if u + 2 < len(units):
                        unit_exp(layer, u + 2, units[u + 2])
                ln_silu(layer)

            def store_broadcasts(layer, which):
                for b, dst, j in which:
                    ac.wait_ge(bc_psum[layer], b + 1)
                    at = 2048 if dst is g2_b else (b % 2) * 1024
                    if dst is g2_b:
                        ac.wait_ge(logit_psum[layer], tiles_of(layer))
                    nc.scalar.copy(dst[:, j, :], ps_flat[:, at:at + 1024]).then_inc(bc_ready[layer], 1)

            def norm2(layer, i):
                tiles = tiles_of(layer)
                ac.wait_ge(x_mid[layer], tiles + i + 1)
                if i >= 2:
                    ac.wait_ge(h2T_psum[layer], i - 1)
                    ac.wait_ge(h2_stored[layer], 16 * (i - 1))
                own(nc.scalar.activation(h2_tok[:, i % 2, :], xres[:, i, :], ACT.Square, accum_out=ssq[:, i:i + 1]))
                settle()
                nc.scalar.activation(rstd[:, i:i + 1], ssq[:, i:i + 1], ACT.Sqrt, bias=eps, scale=1.0 / D).then_inc(std2[layer], 1)

            def store_h2T(layer, i):
                ac.wait_ge(h2T_psum[layer], i + 1)
                if i >= 2:
                    ac.wait_ge(logit_psum[layer], i - 1)
                nc.scalar.copy(h2T[:, i % 2, :, :].rearrange("p k t -> p (k t)"), ps_flat[:, 2048:3072]).then_inc(h2T_ready[layer], 1)

            def experts(layer):
                ac.wait_ge(route_done[layer], 1)
                blocks = ac.value_load(blk_table[0:1, NE:NE + 1], min_val=1, max_val=MAXB)
                nc.scalar.copy(silu[:, 0:1], ssq[:, 0:1]).then_inc(y_ready[layer], 1)
                ac.wait_ge(y_ready[layer], 1)

                def gate():
                    nc.scalar.activation(silu, ps[:, 0, 0:256], ACT.Silu).then_inc(silu_ready[layer], 1)

                def rows_out():
                    nc.scalar.copy(y_rows, ps[:, 3, :]).then_inc(y_ready[layer], 1)

                ac.wait_ge(gate_psum[layer], 1)
                gate()
                ac.wait_ge(y_psum[layer], 1)
                rows_out()
                with ac.Fori(1, blocks) as q:
                    ac.wait_ge(gate_psum[layer], q + 1)
                    gate()
                    ac.wait_ge(y_psum[layer], q + 1)
                    ac.wait_ge(scattered[layer], 16 * q)
                    rows_out()

            def combine(layer, i):
                y = y_pair[:, i % 2, 0, :]
                ac.wait_ge(y_loaded[i % 2][layer], 16 * (i // 2 + 1))
                nc.scalar.activation(y, y, ACT.Copy, scale=gates[:, 0, i:i + 1]).then_inc(y_scaled[layer], 1)

            ac.wait_ge(consts_in, 80)
            nc.scalar.activation(cond[:, :, :], cond[:, :, :], ACT.Silu).then_inc(cond_ready, 1)
            for layer in range(DEPTH):
                started = False
                for kind, n in steps_before_attention(layer):
                    if kind == "mod":
                        mod_sums(n)
                        continue
                    if not started:
                        rms_of_tokens(layer)
                        h1_latents(layer)
                        started = True
                    if kind == "conv" and n in CONV_ACT:
                        conv_copies(layer, [n])
                    if kind == "qkv":
                        qkv_copies(layer, n)
                attention(layer)
                store_broadcasts(layer, [(b, dst, j) for b, (_, _, dst, j) in enumerate(bc_list(layer))])
                tiles = tiles_of(layer)
                for i in range(tiles):
                    norm2(layer, i)
                    if i >= 1:
                        store_h2T(layer, i - 1)
                store_h2T(layer, tiles - 1)
                store_broadcasts(layer, [(len(bc_list(layer)) + j, g2_b, j) for j, _, _ in streams_of(layer)])
                ac.wait_ge(route_ask[layer], 1)
                nc.scalar.activation(part(1092, NT, NG + 1)[:, 0:tiles, :], part(1062, NT, NG + 1)[:, 0:tiles, :],
                                     ACT.Exp).then_inc(route_exp[layer], 1)
                experts(layer)
                if layer == DEPTH - 1:
                    for i in range(tiles):
                        combine(layer, i)

        @block.gpsimd
        def _(po):
            count = po.alloc_register("count")
            po.dma_start(xres[:, 0:XT, :], x.rearrange("o (i p) n -> p (o i) n", p=P)).then_inc(x_in, 16)
            po.dma_start(xres[:, XT:NT, :], ctx_tokens.rearrange("o (i p) n -> p (o i) n", p=P)).then_inc(x_in, 16)
            for layer in range(DEPTH):
                tiles = tiles_of(layer)
                if layer:
                    po.wait_ge(logit_psum[layer - 1], tiles_of(layer - 1))
                po.dma_start(router_w[:, :, :], w_router[layer].rearrange("(k p) n -> p k n", p=P)).then_inc(router_in, 16)
                po.wait_ge(qkv_psum[layer], QKV_UNITS)
                for group in range(2):
                    nc.gpsimd.memset(kT_pad[HD:P, group, 0, :], 0.0).then_inc(keys_padded[layer], 1)
                    nc.gpsimd.memset(kT_pad[0:HD, group, 1, :], 0.0).then_inc(keys_padded[layer], 1)
                for i in range(tiles):
                    po.wait_ge(h2_ready[layer], i + 1)
                    po.dma_start(h2_dram[layer].rearrange("(t h) n -> t (h n)", h=2)[i * P:(i + 1) * P, :], h2_tok[:, i % 2, :]).then_inc(h2_stored[layer], 16)
                    po.wait_ge(h2_stored[layer], 16 * (i + 1))
                for j, _, _ in streams_of(layer):
                    b = len(bc_list(layer)) + j
                    if j:
                        po.wait_ge(bc_psum[layer], b)
                    nc.gpsimd.tensor_tensor(diag2, ident.unsqueeze(1).to_broadcast([P, KD, P]),
                                            mod[:, layer, 5 * KD:6 * KD, j].unsqueeze(2).to_broadcast([P, KD, P]),
                                            ALU.mult).then_inc(diag_ready[layer], 1)
                po.wait_ge(route_done[layer], 1)
                blocks = po.value_load(blk_table[0:1, NE:NE + 1], min_val=1, max_val=MAXB)

                def gather(q):
                    nc.gpsimd.tensor_copy(idx_gather[:, :], list_gather[:, bass.ds(q, 1)]).then_inc(idx_copied[layer], 1)

                def gather_go():
                    po.indirect_dma_start(out=xg, out_offset=None, in_=h2_dram[layer],
                                          in_offset=bass.IndirectOffsetOnAxis(ap=idx_gather[:, 0:1], axis=0),
                                          ).then_inc(gathered[layer], 16)

                def scatter(q):
                    nc.gpsimd.tensor_copy(idx_scatter[:, :], list_scatter[:, bass.ds(q, 1)]).then_inc(idx_copied[layer], 1)

                def scatter_go():
                    po.indirect_dma_start(out=y_dram[layer], in_=y_rows, in_offset=None,
                                          out_offset=bass.IndirectOffsetOnAxis(ap=idx_scatter[:, 0:1], axis=0),
                                          ).then_inc(scattered[layer], 16)

                gather(0)
                po.wait_ge(idx_copied[layer], 1)
                gather_go()
                with po.Fori(0, blocks) as q:
                    po.reg_add(count, q, 1)
                    po.wait_ge(consts_in, 80)
                    po.wait_ge(xgT_psum[layer], count)
                    gather(q + 1)
                    po.reg_add(count, 2 * q, 2)
                    po.wait_ge(consts_in, 80)
                    po.wait_ge(idx_copied[layer], count)
                    gather_go()
                    po.reg_add(count, q, 2)
                    po.wait_ge(consts_in, 80)
                    po.wait_ge(y_ready[layer], count)
                    scatter(q)
                    po.reg_add(count, 2 * q, 3)
                    po.wait_ge(consts_in, 80)
                    po.wait_ge(idx_copied[layer], count)
                    scatter_go()
                po.reg_add(count, 16 * blocks, 0)
                po.wait_ge(consts_in, 80)
                po.wait_ge(scattered[layer], count)
                for i in range(tiles):
                    if i >= 2:
                        po.wait_ge(x_done[layer], i - 1)
                    t = tiles * P
                    po.dma_start(y_pair[:, i % 2, :, :],
                                 y_dram[layer][0:4 * t, :].rearrange("(c i p h) n -> i p c (h n)", c=2, p=P, h=2)[i]
                                 ).then_inc(y_loaded[i % 2][layer], 16)
            for i in range(XT):
                po.wait_ge(x_done[DEPTH - 1], i + 1)
                po.dma_start(out[0, i * P:(i + 1) * P, :], xres[:, i, :]).then_inc(out_stored, 16)
            po.wait_ge(out_stored, 16 * XT)


def shape_constants():
    import numpy as np

    c = np.zeros((P, N_CONST), np.float32)

    def put(name, values):
        a, n = CONST[name]
        c[:, a:a + n] = values

    p = np.arange(P, dtype=np.float32)[:, None]
    f = np.arange(P, dtype=np.float32)[None, :]
    put("ident", p == f)
    put("ones", 1.0)
    put("before", p < f)
    put("mask_prev", np.where(f < p, NEG, 0.0))
    put("mask_next", np.where(f > p, NEG, 0.0))
    half = HD // 2
    inv = np.float32(ROPE_THETA) ** (-np.arange(0, half, 2, dtype=np.float32) / np.float32(half))
    token = np.arange(S)
    ar = (token // GRID_W).astype(np.float32)[:, None] * inv
    ac = (token % GRID_W).astype(np.float32)[:, None] * inv
    angle = np.concatenate([ar, ar, ac, ac], axis=-1)
    sign = np.tile(np.repeat(np.float32([-1, 1]), half // 2), 2)
    put("cos", np.cos(angle).reshape(XT, P, HD).transpose(1, 0, 2).reshape(P, -1))
    put("sin", (np.sin(angle) * sign).reshape(XT, P, HD).transpose(1, 0, 2).reshape(P, -1))
    put("slot", np.arange(2 * B) % B)
    put("limit", B * np.arange(CONST["limit"][1]))
    put("token", p + P * np.arange(NT) + 1)
    put("slot_row", p % B)
    put("half", p // B)
    put("select", (p % 32) == np.arange(2))
    put("eps", EPS)
    return c


_OUTS = [((1, S, D), "float32")]


def kernel(**inputs):
    import numpy as _np
    import concourse.bacc as _bacc
    from concourse import mybir as _mybir
    from concourse.bass_utils import run_bass_kernel_spmd as _run

    a = {k: _np.asarray(v) for k, v in inputs.items()}

    def by_partition(v):
        return v.reshape(-1, P).T

    smalls, rows = [], []
    for layer in range(DEPTH):
        smalls.append(_np.concatenate([
            by_partition(a["norm1_g"][layer]), by_partition(a["norm2_g"][layer]), by_partition(a["mod_b"][layer]),
            a["conv_a_w"][layer].reshape(TAPS_A, 2, P).transpose(2, 1, 0).reshape(P, -1),
            a["conv_b_w"][layer].reshape(TAPS_B, 2, P).transpose(2, 1, 0).reshape(P, -1),
            by_partition(a["conv_b_b"][layer]), by_partition(a["ln_b_g"][layer]), by_partition(a["ln_b_b"][layer]),
        ], axis=1))
        rows.append(_np.concatenate([a["qn_c_g"][layer], a["kn_c_g"][layer], a["qn_d_g"][layer], a["kn_d_g"][layer],
                                     a["sink_d"][layer], a["rg_b"][layer], a["re_b"][layer]]))
    arrays = {
        "x": a["x"], "ctx_tokens": a["ctx"],
        "conditions": _np.pad(_np.stack([by_partition(a["c"][0]), by_partition(a["c_ctx"])], axis=2),
                              ((0, 0), (0, 0), (0, 30))),
        "consts": shape_constants(), "smalls": _np.stack(smalls), "rows": _np.stack(rows),
        "w_mod": a["mod_w"], "w_in": a["w_in"], "w_out": a["w_out"],
        "w_router": _np.concatenate([a["rg_w"], a["re_w"]], axis=2),
        "e_gate": a["e_gate"], "e_up": a["e_up"], "e_down": a["e_down"],
    }
    arrays = {f"in_{k}_dram": _np.ascontiguousarray(v) for k, v in arrays.items()}
    nc = _bacc.Bacc("TRN2", target_bir_lowering=False, num_devices=1)
    args = [nc.dram_tensor(k, v.shape, _mybir.dt.from_np(v.dtype), kind="ExternalInput").ap() for k, v in arrays.items()]
    for i, (shape, dtype) in enumerate(_OUTS):
        args.append(nc.dram_tensor(f"out_{i}_dram", shape, _mybir.dt.from_np(_np.dtype(dtype)), kind="ExternalOutput").ap())
    hybrid_flow_block(nc, *args)
    r = _run(nc, [arrays], core_ids=[0])
    got = tuple(r.results[0][f"out_{i}_dram"] for i in range(len(_OUTS)))
    return got[0]
```

```python
from contextlib import ExitStack

import concourse.bass as bass
from concourse import mybir

F32 = mybir.dt.float32
I32 = mybir.dt.int32
U32 = mybir.dt.uint32
ACT = mybir.ActivationFunctionType
ALU = mybir.AluOpType
AX = mybir.AxisListType

P = 128
D = 1024
KD = D // P
S = 512
C = 256
DEPTH = 2
XT, CT = S // P, C // P
NT = XT + CT
TOK = S + C
HD = 64
SCALE = HD ** -0.5
W_SC, W_CF, TAPS_A, TAPS_B = 256, 256, 3, 31
NG, NPG = 4, 8
NE = NG * NPG
DE = 512
B = 64
MAXB = NE + 2 * TOK // B
EPS = 1e-6
NEG = -1e30
D_IN = 2304
GRID_W = 64
ROPE_THETA = 10000.0

CONST = {}
_at = 0
for _name, _width in (("ident", P), ("ones", P), ("before", P), ("mask_prev", P), ("mask_next", P),
                      ("cos", XT * HD), ("sin", XT * HD), ("slot", 2 * B), ("limit", 2 * TOK // B // 2),
                      ("token", NT), ("slot_row", 1), ("half", 1), ("select", 2), ("eps", 1)):
    CONST[_name] = (_at, _width)
    _at += _width
N_CONST = _at

SMALL = {}
_at = 0
for _name, _width in (("norm1", KD), ("norm2", KD), ("mod_b", 6 * KD), ("conv_a", 2 * TAPS_A),
                      ("conv_b", 2 * TAPS_B), ("conv_bias", 2), ("ln_g", 2), ("ln_b", 2)):
    SMALL[_name] = (_at, _width)
    _at += _width
N_SMALL = _at
N_ROW = 4 * HD + 4 + NG + NE

SLOTS = 6
SLOT = 4096


QKV_UNITS = 2 * NT
CONV_ORDER = (6, 7, 8, 9, 0, 1, 2, 3, 4, 5)


def steps_before_attention(layer):
    conv = [("conv", ct) for ct in CONV_ORDER]
    qkv = [("qkv", u) for u in range(QKV_UNITS)]
    if layer:
        return conv + qkv
    mod = [("mod", n) for n in range(12 * DEPTH)]
    steps, mod = mod[:MOD_FIRST], mod[MOD_FIRST:]
    for n, step in enumerate(conv + qkv):
        beside = 2 if n == 9 else 0 if n in (14, 15, 21) else 1
        steps += [step, *mod[:beside]]
        mod = mod[beside:]
    return steps


MOD_FIRST = 4
MOD_CONV = MOD_FIRST + 11


def chunk_of(layer, step):
    kind, n = step
    if kind == "mod":
        return "mod", n // 12, n % 12 * 512, 512
    if kind == "conv":
        first = 768 if n >= 6 else 512 if n >= 4 else 0
        return "w_in", layer, first, 256 if first == 512 else 512
    return "w_in", layer, 1280 + n // NT * 512, 512


def chunks_before_experts(layer):
    chunks = []
    for step in steps_before_attention(layer):
        if chunk_of(layer, step) not in chunks:
            chunks.append(chunk_of(layer, step))
    return chunks + [("w_out", layer, c * 512, 512) for c in range(2)]


CHUNKS = [chunks_before_experts(layer) for layer in range(DEPTH)]
FIRST = [0, len(CHUNKS[0]) + 3 * NE]
EXPERTS = [FIRST[layer] + len(CHUNKS[layer]) for layer in range(DEPTH)]


def hybrid_flow_block(nc, x, ctx_tokens, conditions, consts, smalls, rows, w_mod, w_in, w_out, w_router,
                      e_gate, e_up, e_down, out):
    stack = ExitStack()
    with stack:
        def sb(name, shape, dt=F32):
            return stack.enter_context(nc.sbuf_tensor(name, shape, dt))

        def sem(name):
            return stack.enter_context(nc.semaphore(name))

        def sems(name):
            return [sem(f"{name}{layer}") for layer in range(DEPTH)]

        h2_dram = [nc.dram_tensor(f"h2_dram{l}", ((TOK, S)[l] * 2, D // 2), F32, kind="Internal").ap() for l in range(DEPTH)]
        y_dram = [nc.dram_tensor(f"y_dram{l}", ((2 * (TOK, S)[l] + B) * 2, D // 2), F32, kind="Internal").ap() for l in range(DEPTH)]

        ring = sb("ring", [P, SLOTS, SLOT])
        xres = sb("xres", [P, NT, D])
        r1 = sb("r1", [P, 6144])
        r2 = sb("r2", [P, 6144])
        r3 = sb("r3", [P, 6144])
        const = sb("const", [P, N_CONST])
        small = sb("small", [P, DEPTH, N_SMALL])
        row = sb("row", [P, DEPTH, N_ROW])
        cond = sb("cond", [P, KD, 32])
        mod_row = sb("mod_row", [P, 512])
        mod = sb("mod", [P, DEPTH, 6 * KD, 2])
        amp = sb("amp", [P, 2, KD])
        ssq = sb("ssq", [P, NT])
        rstd = sb("rstd", [P, NT])
        qk_sum = sb("qk_sum", [P, 8])
        qk_std = sb("qk_std", [P, 8])
        qk_rstd = sb("qk_rstd", [P, 8])
        inverse = mod_row[:, 0:2 * P].rearrange("p (b n) -> p b n", b=2)
        inv_rows = mod_row[:, 2 * P:3 * P]
        stat = sb("stat", [P, 4, 4])
        nsink = sb("nsink", [P, DEPTH, 4])
        router_w = sb("router_w", [P, KD, NG + NE])
        h1T = r1[:, :].rearrange("p (i k t) -> p i k t", i=NT, k=KD)
        prob = r1[:, 0:1536].rearrange("p (b n) -> p b n", b=2)
        probT = r1[:, 1536:3072].rearrange("p (b n) -> p b n", b=2)
        kT_pad = r1[:, 3072:6144].rearrange("p (g kv t) -> p g kv t", g=2, kv=2)
        h2T = r1[:, 0:2048].rearrange("p (b k t) -> p b k t", b=2, k=KD)
        h2_tok = r1[:, 2048:4096].rearrange("p (b n) -> p b n", b=2)
        scratch = r1[:, 4096:5120].rearrange("p (b n) -> p b n", b=2)
        catT = r2[:, :].rearrange("p (k t) -> p k t", k=8)
        glu_w = 15 + S + 15 + C + 15
        glu = r2[:, 3072:3072 + 2 * glu_w].rearrange("p (i t) -> p i t", i=2)
        square = r2[:, 3072:3072 + 1536].rearrange("p (i t) -> p i t", i=2)
        qk = r2[:, 4704:5088]
        qk_tmp = r2[:, 5088:5472]
        ln_std = r2[:, 3072:3072 + TOK]
        xg = r2[:, 0:512]
        xgT = r2[:, 1024:1536].rearrange("p (j h t) -> p j h t", j=4, h=2)
        silu = r2[:, 1536:1792]
        hid = r2[:, 1792:2048]
        hidT = r2[:, 2048:2304].rearrange("p (j h t) -> p j h t", j=2, h=2)
        y_rows = r2[:, 2560:3072]
        xn = r3[:, :].rearrange("p (i n) -> p i n", i=NT)
        v_tok = r3[:, 0:1536].rearrange("p (i n) -> p i n", i=NT)
        qT = r3[:, 1536:4608].rearrange("p (i t) -> p i t", i=4)
        kT = r3[:, 4608:6144].rearrange("p (i t) -> p i t", i=2)
        cx_w = 1 + S + 1 + C + 1
        cx = r3[:, 1536:1536 + 2 * cx_w].rearrange("p (i t) -> p i t", i=2)
        conv_a = r3[:, 4608:6144].rearrange("p (i t) -> p i t", i=2)
        g1_b = r3[:, 0:2048].rearrange("p (j n) -> p j n", j=2)
        amp2_b = r3[:, 2048:4096].rearrange("p (j n) -> p j n", j=2)
        sh2_b = r3[:, 4096:6144].rearrange("p (j n) -> p j n", j=2)
        g2_b = r1[:, 4096:6144].rearrange("p (j n) -> p j n", j=2)
        y_pair = [v.rearrange("p (c n) -> p c n", c=2) for v in (
            r1[:, 0:2048], r1[:, 2048:4096], r2[:, 0:2048], r2[:, 2048:4096], r2[:, 4096:6144], r3[:, 4096:6144])]
        def part(first, *dims):
            n = 1
            for d in dims:
                n *= d
            v = r3[:, first:first + n]
            if len(dims) == 2:
                v = v.rearrange("p (a b) -> p a b", a=dims[0])
            if len(dims) == 3:
                v = v.rearrange("p (a b c) -> p a b c", a=dims[0], b=dims[1])
            return v

        def cst(name):
            a, n = CONST[name]
            return const[:, a:a + n]

        def sml(layer, name):
            a, n = SMALL[name]
            return small[:, layer, a:a + n]

        ident, ones = cst("ident"), cst("ones")
        blk_table = sb("blk_table", [1, NE + 1], I32)
        list_gather = sb("list_gather", [P, MAXB + 1], U32)
        list_scatter = sb("list_scatter", [P, MAXB + 1], U32)
        idx_gather = sb("idx_gather", [P, 1], U32)
        idx_scatter = sb("idx_scatter", [P, 1], U32)
        gates = sb("gates", [P, 2, NT])

        ps = stack.enter_context(nc.psum_tensor("ps", [P, 8, 512], F32))
        ps_flat = ps[:, :, :].rearrange("p b n -> p (b n)")

        consts_in = sem("consts_in")
        x_in = sem("x_in")
        first_half, second_half = sem("first_half"), sem("second_half")
        vec = sem("vector_step")
        act_step = sem("scalar_step")
        cond_ready = sem("cond_ready")
        mod_psum = sems("mod_psum")
        mod_rows, mod_turned, mod_ready = sem("mod_rows"), sem("mod_turned"), sem("mod_ready")
        xn_ready = sems("xn_ready")
        rms_std = sems("rms_std")
        h1_psum, h1_act, h1_vec = sems("h1_psum"), sems("h1_act"), sems("h1_vec")
        conv_psum, conv_act, conv_mul = sems("conv_psum"), sems("conv_act"), sems("conv_mul")
        pads_ready = sems("pads_ready")
        qkv_psum, qk_square, qk_sums, qk_stds = sems("qkv_psum"), sems("qk_square"), sems("qk_sums"), sems("qk_stds")
        qk_scaled, qk_ready, qkT_psum, qkT_ready = sems("qk_scaled"), sems("qk_ready"), sems("qkT_psum"), sems("qkT_ready")
        conv_done, ln_psum, ln_centred, ln_sq = sems("conv_done"), sems("ln_psum"), sems("ln_centred"), sems("ln_sq")
        ln_stds, ln_done = sems("ln_stds"), sems("ln_done")
        s_psum, neg_max, exp_done, sink_exp = sems("s_psum"), sems("neg_max"), sems("exp_done"), sems("sink_exp")
        pT_psum, pT_ready, o_psum, o_ready = sems("pT_psum"), sems("pT_ready"), sems("o_psum"), sems("o_ready")
        keys_zeroed, keys_padded = sems("keys_zeroed"), sems("keys_padded")
        inv_ready = sems("inv_ready")
        amp_ready, bc_psum, bc_ready = sems("amp_ready"), sems("bc_psum"), sems("bc_ready")
        out_psum, out_read, x_mid = sems("out_psum"), sems("out_read"), sems("x_mid")
        h2_ready, h2_stored = sems("h2_ready"), sems("h2_stored")
        h2T_psum, h2T_ready, logit_psum = sems("h2T_psum"), sems("h2T_ready"), sems("logit_psum")
        router_in = sem("router_in")
        route_exp, route_ask = sems("route_exp"), sems("route_ask")
        chosen, rank_psum, onehots, list_psum, route_done = (sems("chosen"), sems("rank_psum"), sems("onehots"),
                                                             sems("list_psum"), sems("route_done"))
        idx_copied, gathered, scattered = sems("idx_copied"), sems("gathered"), sems("scattered")
        gate_psum, up_psum, silu_ready, hid_ready = sems("gate_psum"), sems("up_psum"), sems("silu_ready"), sems("hid_ready")
        xgT_psum, xgT_ready, hidT_psum, hidT_ready = sems("xgT_psum"), sems("xgT_ready"), sems("hidT_psum"), sems("hidT_ready")
        y_psum, y_ready = sems("y_psum"), sems("y_ready")
        y_loaded = [sem(f"y_loaded_tile{i}_") for i in range(NT)]
        y_scaled, y_weighted, x_done = sems("y_scaled"), sems("y_weighted"), sems("x_done")
        out_stored = sem("out_stored")

        def tiles_of(layer):
            return NT if layer == 0 else XT

        def streams_of(layer):
            return [(0, 0, S), (1, S, C)][:2 if layer == 0 else 1]

        def key_tiles(layer, group, i):
            if i >= XT:
                return 0, 0
            return (0, XT) if group == 0 else (max(i - 1, 0), min(i + 2, XT))

        def units_of(layer):
            return [(i, g, kv, r) for i in range(tiles_of(layer)) for g in range(2) for kv in range(2) for r in range(2)]

        def is_full(layer, i):
            return layer == 0 or i < XT

        LN_MEAN, LN_VAR = 7, 9
        TAPS_EARLY = 24
        CONV_ACT = {ct: n + 1 for n, ct in enumerate(CONV_ORDER[:8])}
        CONV_MUL = {4: 1, 5: 2}
        CONV_AT = {ct: n for n, ct in enumerate(CONV_ORDER)}
        VECTORS = [("g1", 16, g1_b), ("sh2", 24, sh2_b), ("amp2", None, amp2_b), ("g2", 40, g2_b)]

        def bc_list(layer):
            return [(n, m, dst, j) for n, m, dst in VECTORS for j, _, _ in streams_of(layer)]

        def bc_before(layer, name):
            return [v[0] for v in VECTORS].index(name) * len(streams_of(layer))

        def bc_bank(b):
            return 2 + 2 * (b % 2)

        block = stack.enter_context(nc.Block())

        def chunk_index(layer, step):
            return FIRST[layer] + CHUNKS[layer].index(chunk_of(layer, step))

        def mod_bank(n):
            return 5 + n % 2 if n < MOD_CONV else 0

        def turned_bank(n):
            return 7 if n < MOD_CONV else 1

        def slot_ap(n, width=512):
            return ring[:, n % SLOTS, 0:8 * width].rearrange("p (k n) -> p k n", k=8)

        def down_ap(n):
            return ring[:, n % SLOTS, :].rearrange("p (k n) -> p k n", k=4)

        def loaded(n):
            return 16 * (n + 1)

        PAIR = 16 * 2 * 3

        @block.sync
        def _(sp):
            sp.dma_start(const[:, :], consts).then_inc(consts_in, 16)
            sp.dma_start(small[:, :, :], smalls.rearrange("l p n -> p l n")).then_inc(consts_in, 16)
            sp.dma_start(cond[:, :, :], conditions).then_inc(consts_in, 16)
            for layer in range(DEPTH):
                sp.dma_start(row[:, layer, :], rows[layer].partition_broadcast(P)).then_inc(consts_in, 16)

            matrices = {"mod": w_mod, "w_in": w_in, "w_out": w_out}

            def used(layer, j):
                kind, m, a, _ = CHUNKS[layer][j]
                if kind == "mod":
                    return mod_psum[m], a // 512 + 1
                if kind == "w_in":
                    return {768: (conv_psum[m], 4), 0: (conv_psum[m], 8), 512: (conv_psum[m], 10),
                            1280: (qkv_psum[m], NT), 1792: (qkv_psum[m], 2 * NT)}[a]
                return out_psum[m], tiles_of(m) * (a // 512 + 1)

            def before_first_half(n):
                if n > 0:
                    sp.wait_ge(first_half, loaded(n - 1))

            def before_second_half(n):
                if n > 0:
                    sp.wait_ge(second_half, loaded(n - 1))

            def load_static(layer, j):
                n = FIRST[layer] + j
                kind, m, a, width = CHUNKS[layer][j]
                if n >= SLOTS and n - SLOTS < EXPERTS[0]:
                    sp.wait_ge(*used(0, n - SLOTS))
                src = matrices[kind][m].rearrange("(k p) n -> p k n", p=P)[:, :, a:a + width]
                dst = slot_ap(n, width)
                before_first_half(n)
                sp.dma_start(dst[:, 0:4, :], src[:, 0:4, :]).then_inc(first_half, 16)
                before_second_half(n)
                sp.dma_start(dst[:, 4:8, :], src[:, 4:8, :]).then_inc(second_half, 16)

            def expert_part(layer, j, e):
                w = (e_gate, e_up, e_down)[j]
                return w[layer, bass.ds(e, 1), :, :].rearrange("o (k p) n -> p (o k) n", p=P)

            count = sp.alloc_register("count")

            def load_expert(layer, j, e, n, turn):
                src = expert_part(layer, j, e)
                dst = slot_ap(n) if j < 2 else down_ap(n)
                half = 4 if j < 2 else 2
                if isinstance(turn, int):
                    before = loaded(n - 1)
                else:
                    before = count
                sp.wait_ge(first_half, before)
                sp.dma_start(dst[:, 0:half, :], src[:, 0:half, :]).then_inc(first_half, 16)
                sp.wait_ge(second_half, before)
                sp.dma_start(dst[:, half:, :], src[:, half:, :]).then_inc(second_half, 16)

            for layer in range(DEPTH):
                for j in range(len(CHUNKS[layer])):
                    if layer and j < SLOTS:
                        s = (gate_psum, up_psum, y_psum)[j % 3][layer - 1]
                        if j == 0 or j == 3:
                            end = sp.value_load(blk_table[0:1, NE - 1 + j // 3:NE + j // 3], min_val=1, max_val=MAXB)
                        sp.wait_ge(s, end)
                        if j == 1:
                            for i in range(tiles_of(layer - 1)):
                                sp.wait_ge(y_loaded[i], 16 * layer)
                    elif layer:
                        sp.wait_ge(*used(layer, j - SLOTS))
                    load_static(layer, j)
                for n in range(EXPERTS[layer], EXPERTS[layer] + 6):
                    sp.wait_ge(*used(layer, n - SLOTS - FIRST[layer]))
                    load_expert(layer, (n - EXPERTS[layer]) % 3, (n - EXPERTS[layer]) // 3, n, 0)
                sp.wait_ge(route_done[layer], 1)
                with sp.Fori(1, NE // 2) as pair:
                    for odd in range(2):
                        e = 2 * pair + odd
                        end = sp.value_load(blk_table[0:1, bass.ds(e - 1, 1)], min_val=1, max_val=MAXB)
                        for j in range(3):
                            sp.reg_add(count, PAIR * pair, loaded(EXPERTS[layer] + 3 * odd + j - 1))
                            sp.wait_ge((gate_psum, up_psum, y_psum)[j][layer], end)
                            load_expert(layer, j, e, EXPERTS[layer] + 3 * odd + j, pair)

        @block.tensor
        def _(pe):
            def wait_chunk(n):
                pe.wait_ge(first_half, loaded(n))
                pe.wait_ge(second_half, loaded(n))

            def mod_sums(n):
                wait_chunk(chunk_index(0, ("mod", n)))
                if n >= 2:
                    pe.wait_ge(mod_rows, n - 1 if n <= MOD_CONV else n)
                w = slot_ap(chunk_index(0, ("mod", n)))
                for k in range(2):
                    for g in range(4):
                        mm = pe.matmul(ps[32 * g:32 * g + 32, mod_bank(n), :], cond[:, 2 * g + k, :], w[:, 2 * g + k, :],
                                       start=(k == 0), stop=(k == 1), tile_position=(0, 32 * g))
                mm.then_inc(mod_psum[n // 12], 1)

            def mod_turn(n):
                pe.wait_ge(mod_rows, n + 1)
                for t in range(4):
                    at = 8 * n + 2 * t
                    mm = pe.matmul(ps[:, turned_bank(n), at:at + 2], mod_row[:, t * P:(t + 1) * P], cst("select"),
                                   start=True, stop=True)
                mm.then_inc(mod_turned, 1)

            def h1_transposes(layer):
                for i in range(NT):
                    pe.wait_ge(xn_ready[layer], i + 1)
                    if i >= 2:
                        pe.wait_ge(h1_act[layer], i - 1)
                        pe.wait_ge(h1_vec[layer], i - 1)
                    for k in range(KD):
                        at = i % 2 * 1024 + k * P
                        mm = pe.transpose(ps_flat[:, at:at + P], xn[:, i, k * P:(k + 1) * P], ident)
                    mm.then_inc(h1_psum[layer], 1)

            def conv_projection(layer, ct):
                _, _, first, width = chunk_of(layer, ("conv", ct))
                n = chunk_index(layer, ("conv", ct))
                at = CONV_AT[ct]
                if at == 0:
                    pe.wait_ge(h1_act[layer], NT)
                    pe.wait_ge(h1_vec[layer], NT)
                if at % 4 == 0:
                    wait_chunk(n)
                if at >= 2:
                    pe.wait_ge(conv_act[layer], at - 1)
                w = slot_ap(n, width)
                col = ct * P - first
                for j, t0, tn in streams_of(layer):
                    for k in range(KD):
                        mm = pe.matmul(ps[:, (ct % 2) * 2 + j, 0:tn], w[:, k, col:col + P],
                                       h1T[:, t0 // P:(t0 + tn) // P, k, :], start=(k == 0), stop=(k == KD - 1))
                mm.then_inc(conv_psum[layer], 1)

            def qk_transposes(layer, u):
                i = u % NT
                pe.wait_ge(qk_ready[layer], u + 1)
                if u >= 2:
                    pe.wait_ge(qkT_ready[layer], u - 1)
                elif layer == 0:
                    pe.wait_ge(mod_rows, MOD_CONV)
                    pe.wait_ge(mod_ready, 3)
                for r in range(2 if is_full(layer, i) else 0):
                    pe.transpose(ps[:, 6 + u % 2, r * P:(r + 1) * P], qk[:, r * P:(r + 1) * P], ident)
                pe.transpose(ps[:, 6 + u % 2, 2 * P:3 * P], qk[:, 256:384], ident).then_inc(qkT_psum[layer], 1)

            def qkv_projection(layer, u):
                i = u % NT
                n = chunk_index(layer, ("qkv", u))
                if i == 0:
                    wait_chunk(n)
                if u >= 2:
                    pe.wait_ge(qk_scaled[layer], u - 1)
                elif layer == 0 and u == 1:
                    pe.wait_ge(mod_rows, MOD_CONV)
                c0 = 0 if is_full(layer, i) else 256
                for k in range(KD):
                    mm = pe.matmul(ps[:, 4 + u % 2, c0:512], h1T[:, i, k, :], slot_ap(n)[:, k, c0:512],
                                   start=(k == 0), stop=(k == KD - 1))
                mm.then_inc(qkv_psum[layer], 1)
                if u >= 1:
                    qk_transposes(layer, u - 1)

            def ln_sums(layer, which):
                if which == 0:
                    pe.wait_ge(conv_done[layer], 2 * len(streams_of(layer)))
                    src = catT[:, 2:4, :]
                else:
                    pe.wait_ge(ln_sq[layer], 2)
                    src = square
                for j, t0, tn in streams_of(layer):
                    for i in range(2):
                        mm = pe.matmul(ps[:, 2 + j, 0:tn], ones, src[:, i, t0:t0 + tn], start=(i == 0), stop=(i == 1))
                mm.then_inc(ln_psum[layer], 1)

            def scores(layer, u, unit):
                i, group, kv, r = unit
                a, b = key_tiles(layer, group, i)
                w = (b - a) * P
                q = qT[:, group * 2 + r, i * P:(i + 1) * P]
                bank = (u % 2) * 2
                if u >= 2:
                    pe.wait_ge(exp_done[layer], u - 1)
                if u == 0 or u == 4:
                    pe.wait_ge(keys_padded[layer], 2 * (group + 1))
                if w:
                    masks = []
                    if group == 1 and i > 0:
                        masks.append((512 - w, cst("mask_prev")))
                    if group == 1 and i < XT - 1:
                        masks.append((512 - P, cst("mask_next")))
                    pe.matmul(ps[:, bank, 512 - w:512], q, kT_pad[:, group, kv, a * P:b * P], start=True, stop=not masks)
                    for m, (at, mask) in enumerate(masks):
                        pe.matmul(ps[:, bank, at:at + P], ident, mask, start=False, stop=m == len(masks) - 1)
                pe.matmul(ps[:, bank + 1, 0:C], q, kT_pad[:, group, kv, S:TOK], start=True, stop=True).then_inc(s_psum[layer], 1)

            def attend(layer, u, unit, last_pT):
                i, group, kv, r = unit
                a, b = key_tiles(layer, group, i)
                tiles = list(range(a, b)) + list(range(XT, NT))
                w = (b - a) * P
                pe.wait_ge(exp_done[layer], u + 1)
                if last_pT:
                    pe.wait_ge(*last_pT)
                for n in range(len(tiles)):
                    at = 512 - w + n * P
                    mm = pe.transpose(ps_flat[:, 2048 + at:2048 + at + P], prob[:, u % 2, at:at + P], ident)
                mm.then_inc(pT_psum[layer], 1)

            def weigh(layer, pair, unit):
                i, group, kv, _ = unit
                a, b = key_tiles(layer, group, i)
                tiles = list(range(a, b)) + list(range(XT, NT))
                w = (b - a) * P
                pe.wait_ge(pT_ready[layer], 2 * pair + 2)
                if pair >= 2:
                    pe.wait_ge(o_ready[layer], pair - 1)
                for n, t in enumerate(tiles):
                    at = 512 - w + n * P
                    for r in range(2):
                        mm = pe.matmul(ps[r * HD:(r + 1) * HD, 6 + pair % 2, 0:P],
                                       v_tok[:, t, group * P + kv * HD:group * P + (kv + 1) * HD],
                                       probT[:, r, at:at + P], start=(n == 0), stop=(n == len(tiles) - 1),
                                       tile_position=(0, r * HD))
                pe.wait_ge(inv_ready[layer], 2 * pair + 2)
                pe.transpose(ps[:, 6 + pair % 2, P:2 * P], inverse[:, pair % 2, :], ident).then_inc(o_psum[layer], 1)

            def attention(layer):
                units = units_of(layer)
                pe.wait_ge(qkT_ready[layer], NT)
                pe.wait_ge(ln_stds[layer], 1)
                scores(layer, 0, units[0])
                scores(layer, 1, units[1])
                qk_transposes(layer, QKV_UNITS - 1)
                pe.wait_ge(qkT_ready[layer], QKV_UNITS)
                last_pT = None
                for u, unit in enumerate(units):
                    attend(layer, u, unit, last_pT)
                    if u + 2 < len(units):
                        scores(layer, u + 2, units[u + 2])
                    if u % 2:
                        weigh(layer, u // 2, unit)
                    last_pT = (pT_ready[layer], u + 1)
                pe.wait_ge(o_ready[layer], len(units) // 2)
                return last_pT

            def broadcast(layer, b):
                _, column, _, j = bc_list(layer)[b]
                if column is None:
                    pe.wait_ge(amp_ready[layer], 4)
                if b >= 2:
                    pe.wait_ge(bc_ready[layer], b - 1)
                for k in range(KD):
                    value = amp[:, j, k:k + 1] if column is None else mod[:, layer, column + k, j:j + 1]
                    mm = pe.transpose(ps_flat[:, bc_bank(b) * 512 + k * P:bc_bank(b) * 512 + (k + 1) * P],
                                      value.to_broadcast([P, P]), ident)
                mm.then_inc(bc_psum[layer], 1)

            def h2_transposes(layer, i):
                pe.wait_ge(h2_ready[layer], i + 1)
                if i >= 1:
                    pe.wait_ge(h2T_ready[layer], i)
                for k in range(KD):
                    mm = pe.transpose(ps_flat[:, 2048 + k * P:2048 + (k + 1) * P], h2_tok[:, i % 2, k * P:(k + 1) * P], ident)
                mm.then_inc(h2T_psum[layer], 1)

            def logits(layer, i):
                if i == 0:
                    pe.wait_ge(router_in, 16 * (layer + 1))
                pe.wait_ge(h2T_ready[layer], i + 1)
                for k in range(KD):
                    mm = pe.matmul(ps[:, 6, i * 36:(i + 1) * 36], h2T[:, i % 2, k, :], router_w[:, k, :],
                                   start=(k == 0), stop=(k == KD - 1))
                mm.then_inc(logit_psum[layer], 1)

            def out_projection(layer):
                tiles = tiles_of(layer)
                nb = bc_before(layer, "g2")
                sent = len(streams_of(layer))
                for b in range(sent):
                    broadcast(layer, b)
                n0 = FIRST[layer] + [c[0] for c in CHUNKS[layer]].index("w_out")
                for u in range(2 * tiles):
                    c, i = divmod(u, tiles)
                    if i == 0:
                        wait_chunk(n0 + c)
                    if u < 2:
                        pe.wait_ge(ln_done[layer], 2)
                    else:
                        pe.wait_ge(out_read[layer], u - 1)
                    w = slot_ap(n0 + c)
                    for k in range(8):
                        mm = pe.matmul(ps[:, u % 2, :], catT[:, k, i * P:(i + 1) * P], w[:, k, :],
                                       start=(k == 0), stop=(k == 7))
                    mm.then_inc(out_psum[layer], 1)
                    if sent < nb:
                        broadcast(layer, sent)
                        sent += 1
                        if sent == nb:
                            pe.wait_ge(bc_ready[layer], nb)
                    if c == 1 and i >= 1:
                        h2_transposes(layer, i - 1)
                    if c == 1 and i >= 2:
                        logits(layer, i - 2)
                logits(layer, tiles - 2)
                h2_transposes(layer, tiles - 1)
                logits(layer, tiles - 1)

            def ranks(layer):
                tiles = tiles_of(layer)
                picked = part(0, NT, NE)
                pe.wait_ge(chosen[layer], 1)
                pe.matmul(ps[:, 0, 0:tiles * NE], cst("before"), picked[:, 0:tiles, :], start=True, stop=False)
                for back in range(1, tiles):
                    pe.matmul(ps[:, 0, back * NE:tiles * NE], ones, picked[:, 0:tiles - back, :],
                              start=False, stop=back == tiles - 1)
                mm = pe.matmul(ps[:, 1, 0:tiles * NE], ones, picked[:, 0:tiles, :], start=True, stop=True)
                mm.then_inc(rank_psum[layer], 1)

            def lists(layer):
                n = 2 * tiles_of(layer)
                for a in range(n):
                    pe.wait_ge(onehots[layer], a + 1)
                    mm = pe.matmul(ps[:, 2, 0:B], part(2048, 12, 2 * B)[:, a, :], part(3584, 12, B)[:, a, :],
                                   start=(a == 0), stop=(a == n - 1))
                mm.then_inc(list_psum[layer], 1)

            def experts(layer):

                def in_transposes():
                    for j in range(4):
                        mm = pe.transpose(ps[:, 4, j * P:(j + 1) * P], xg[:, j * P:(j + 1) * P], ident)
                    mm.then_inc(xgT_psum[layer], 1)

                def side_by_side(bank, width, x, w, k, last):
                    for g in range(2):
                        mm = pe.matmul(ps[g * B:(g + 1) * B, bank, 0:width], x, w[:, k, g * width:(g + 1) * width],
                                       start=(k == 0), stop=(k == last), tile_position=(0, g * B))
                    return mm

                pe.wait_ge(gathered[layer], 16)
                in_transposes()
                with pe.Fori(0, NE // 2) as pair:
                    for odd in range(2):
                        n = EXPERTS[layer] + 3 * odd
                        gate, up, down = slot_ap(n), slot_ap(n + 1), down_ap(n + 2)
                        first = pe.value_load(blk_table[0:1, bass.ds(2 * pair + odd, 1)], min_val=0, max_val=MAXB)
                        end = pe.value_load(blk_table[0:1, bass.ds(2 * pair + odd + 1, 1)], min_val=1, max_val=MAXB)
                        with pe.Fori(first, end) as q:
                            pe.wait_ge(xgT_ready[layer], q + 1)
                            pe.wait_ge(first_half, loaded(n) + PAIR * pair)
                            for k in range(KD):
                                if k == KD // 2:
                                    pe.wait_ge(second_half, loaded(n) + PAIR * pair)
                                mm = side_by_side(0, DE // 2, xgT[:, k % 4, k // 4, :], gate, k, KD - 1)
                            mm.then_inc(gate_psum[layer], 1)
                            pe.wait_ge(first_half, loaded(n + 1) + PAIR * pair)
                            for k in range(KD):
                                if k == KD // 2:
                                    pe.wait_ge(second_half, loaded(n + 1) + PAIR * pair)
                                mm = side_by_side(1, DE // 2, xgT[:, k % 4, k // 4, :], up, k, KD - 1)
                            mm.then_inc(up_psum[layer], 1)
                            pe.wait_ge(gathered[layer], 16 * q + 32)
                            in_transposes()
                            pe.wait_ge(hid_ready[layer], q + 1)
                            for j in range(2):
                                mm = pe.transpose(ps[:, 2, j * P:(j + 1) * P], hid[:, j * P:(j + 1) * P], ident)
                            mm.then_inc(hidT_psum[layer], 1)
                            pe.wait_ge(y_ready[layer], q + 1)
                            pe.wait_ge(first_half, loaded(n + 2) + PAIR * pair)
                            pe.wait_ge(hidT_ready[layer], q + 1)
                            for k in range(4):
                                if k == 2:
                                    pe.wait_ge(second_half, loaded(n + 2) + PAIR * pair)
                                mm = side_by_side(3, D // 2, hidT[:, k % 2, k // 2, :], down, k, 3)
                            mm.then_inc(y_psum[layer], 1)

            pe.wait_ge(consts_in, 80)
            pe.wait_ge(cond_ready, 1)
            for layer in range(DEPTH):
                turned = None
                started = False
                for kind, n in steps_before_attention(layer):
                    if kind != "mod" and not started:
                        if turned is not None:
                            mod_turn(turned)
                            turned = None
                        h1_transposes(layer)
                        started = True
                    if kind == "conv":
                        conv_projection(layer, n)
                    if kind == "qkv":
                        qkv_projection(layer, n)
                        if n in (LN_MEAN, LN_VAR):
                            ln_sums(layer, 0 if n == LN_MEAN else 1)
                    if turned is not None:
                        mod_turn(turned)
                        turned = None
                    if kind == "mod":
                        if n == MOD_CONV:
                            pe.wait_ge(conv_act[layer], 8)
                            pe.wait_ge(conv_mul[layer], 2)
                        mod_sums(n)
                        turned = n
                if layer == 0:
                    pe.wait_ge(mod_ready, 4)
                last_pT = attention(layer)
                pe.wait_ge(*last_pT)
                out_projection(layer)
                for b in range(bc_before(layer, "g2"), len(bc_list(layer))):
                    broadcast(layer, b)
                ranks(layer)
                pe.wait_ge(bc_ready[layer], len(bc_list(layer)))
                lists(layer)
                pe.wait_ge(route_done[layer], 1)
                experts(layer)

        @block.vector
        def _(ve):
            steps = [0]

            def own(ins):
                steps[0] += 1
                ins.then_inc(vec, 1)

            def settle(back=0):
                ve.wait_ge(vec, steps[0] - back)

            def amplitude(layer, name, column, before):
                for j in range(2):
                    ins = nc.vector.scalar_tensor_tensor(out=amp[:, j, :], in0=mod[:, layer, column:column + KD, j],
                                                         scalar=1.0, in1=sml(layer, name), op0=ALU.add, op1=ALU.mult)
                    ins.then_inc(amp_ready[layer], 1)
                ve.wait_ge(amp_ready[layer], before + 2)

            def mod_copy(layer, first, end, n, turned):
                ve.wait_ge(mod_turned, turned)
                bias = sml(layer, "mod_b")[:, 4 * first:4 * end].unsqueeze(2).to_broadcast([P, 4 * (end - first), 2])
                at = 8 * (12 * layer + first)
                nc.vector.tensor_tensor(mod[:, layer, 4 * first:4 * end, :],
                                        ps[:, n, at:at + 8 * (end - first)].rearrange("p (t j) -> p t j", j=2), bias,
                                        ALU.add).then_inc(mod_ready, 1)

            def scale_tokens(layer, i):
                ve.wait_ge(rms_std[layer], i + 1)
                own(nc.vector.reciprocal(rstd[:, i:i + 1], rstd[:, i:i + 1]))
                settle()
                nc.vector.tensor_scalar(xn[:, i, :], xres[:, i, :], rstd[:, i:i + 1], None,
                                        ALU.mult).then_inc(xn_ready[layer], 1)

            def modulate(layer, i):
                ve.wait_ge(h1_psum[layer], i + 1)
                j = 0 if i < XT else 1
                for k in range(KD // 2, KD):
                    at = i % 2 * 1024 + k * P
                    ins = nc.vector.tensor_scalar(h1T[:, i, k, :], ps_flat[:, at:at + P], amp[:, j, k:k + 1],
                                                  mod[:, layer, k, j:j + 1], ALU.mult, ALU.add)
                ins.then_inc(h1_vec[layer], 1)

            def tokens_in(layer):
                if layer == 0:
                    for i in range(NT):
                        scale_tokens(layer, i)
                    mod_copy(0, 0, MOD_FIRST, turned_bank(0), MOD_FIRST)
                    ve.wait_ge(mod_ready, 1)
                    amplitude(layer, "norm1", KD, 0)
                    for i in range(NT):
                        modulate(layer, i)
                    return
                ve.wait_ge(mod_ready, 4)
                amplitude(layer, "norm1", KD, 0)
                for n in range(NT + 3):
                    if n < NT:
                        combine(layer - 1, n)
                    if n - 2 == 4:
                        ve.wait_ge(x_done[layer - 1], NT)
                    if 2 <= n < NT + 2:
                        scale_tokens(layer, n - 2)
                    if n >= 3:
                        modulate(layer, n - 3)

            def clear_pads(layer):
                for pads in ((cx, (0, 1 + S, 2 + S + C), 1), (glu, (0, 15 + S, 30 + S + C), 15)):
                    for at in pads[1]:
                        ins = nc.vector.memset(pads[0][:, :, at:at + pads[2]], 0.0)
                ins.then_inc(pads_ready[layer], 1)
                ve.wait_ge(pads_ready[layer], 1)

            def conv_a_group(layer):
                w = sml(layer, "conv_a")
                for i in range(2):
                    ve.wait_ge(conv_act[layer], CONV_ACT[2 + i])
                    ve.wait_ge(conv_psum[layer], CONV_AT[4 + i] + 1)
                    for j, t0, tn in streams_of(layer):
                        at = t0 + 1 + j
                        ins = nc.vector.tensor_tensor(cx[:, i, at:at + tn], cx[:, i, at:at + tn],
                                                      ps[:, (i % 2) * 2 + j, 0:tn], ALU.mult)
                    ins.then_inc(conv_mul[layer], 1)
                for i in range(2):
                    ve.wait_ge(conv_mul[layer], i + 1)
                    for tap in range(TAPS_A):
                        for j, t0, tn in streams_of(layer):
                            src = cx[:, i, t0 + j + tap:t0 + j + tap + tn]
                            dst = conv_a[:, i, t0:t0 + tn]
                            wt = w[:, i * TAPS_A + tap:i * TAPS_A + tap + 1]
                            if tap == 0:
                                own(nc.vector.tensor_scalar(dst, src, wt, None, ALU.mult))
                            else:
                                own(nc.vector.scalar_tensor_tensor(out=dst, in0=src, scalar=wt, in1=dst,
                                                                   op0=ALU.mult, op1=ALU.add))
                        settle()
                    for j, t0, tn in streams_of(layer):
                        own(nc.vector.tensor_tensor(catT[:, i, t0:t0 + tn], catT[:, i, t0:t0 + tn],
                                                    conv_a[:, i, t0:t0 + tn], ALU.mult))

            def glu_product(layer):
                for i in range(2):
                    ve.wait_ge(conv_act[layer], CONV_ACT[8 + i])
                    for j, t0, tn in streams_of(layer):
                        at = t0 + 15 * (1 + j)
                        own(nc.vector.tensor_tensor(glu[:, i, at:at + tn], glu[:, i, at:at + tn],
                                                    catT[:, 2 + i, t0:t0 + tn], ALU.mult))
                settle()

            def conv_b_tap(layer, tap):
                w = sml(layer, "conv_b")
                ns = len(streams_of(layer))
                for i in range(2):
                    if tap:
                        settle(0 if tap == TAPS_B - 1 else ns)
                    for j, t0, tn in streams_of(layer):
                        src = glu[:, i, t0 + 15 * j + tap:t0 + 15 * j + tap + tn]
                        dst = catT[:, 2 + i, t0:t0 + tn]
                        wt = w[:, i * TAPS_B + tap:i * TAPS_B + tap + 1]
                        if tap == 0:
                            own(nc.vector.tensor_scalar(dst, src, wt, sml(layer, "conv_bias")[:, i:i + 1],
                                                        ALU.mult, ALU.add))
                            continue
                        ins = nc.vector.scalar_tensor_tensor(out=dst, in0=src, scalar=wt, in1=dst,
                                                             op0=ALU.mult, op1=ALU.add)
                        if tap == TAPS_B - 1:
                            ins.then_inc(conv_done[layer], 1)
                        else:
                            own(ins)

            def rotate(layer, u):
                group, i = divmod(u, NT)
                full = is_full(layer, i)
                c0 = 0 if full else 256
                nh = 6 if full else 2
                h0 = 6 - nh
                gains = row[:, layer, group * 2 * HD:(group + 1) * 2 * HD]
                ve.wait_ge(qk_square[layer], u + 1)
                nc.vector.tensor_reduce(qk_sum[:, h0:6], qk_tmp[:, c0:384].rearrange("p (h d) -> p h d", d=HD),
                                        AX.X, ALU.add).then_inc(qk_sums[layer], 1)
                ve.wait_ge(qk_stds[layer], u + 1)
                own(nc.vector.reciprocal(qk_rstd[:, h0:6], qk_std[:, h0:6]))
                settle()
                if u >= 1:
                    ve.wait_ge(qkT_psum[layer], u)
                bank = ps[:, 4 + u % 2, c0:384].rearrange("p (h d) -> p h d", d=HD)
                heads = qk[:, c0:384].rearrange("p (h d) -> p h d", d=HD)
                if full:
                    own(nc.vector.tensor_tensor(qk[:, 0:256].rearrange("p (r kv d) -> p kv r d", r=2, kv=2),
                                                bank[:, 0:4, :].rearrange("p (kv r) d -> p kv r d", kv=2),
                                                qk_rstd[:, 0:4].rearrange("p (kv r) -> p kv r", kv=2).unsqueeze(3)
                                                .to_broadcast([P, 2, 2, HD]), ALU.mult))
                nc.vector.tensor_tensor(heads[:, nh - 2:nh, :], bank[:, nh - 2:nh, :],
                                        qk_rstd[:, 4:6].unsqueeze(2).to_broadcast([P, 2, HD]),
                                        ALU.mult).then_inc(qk_scaled[layer], 1)
                settle()
                ve.wait_ge(qk_scaled[layer], u + 1)
                if full:
                    own(nc.vector.tensor_tensor(heads[:, 0:4, :], heads[:, 0:4, :],
                                                gains[:, 0:HD].unsqueeze(1).to_broadcast([P, 4, HD]), ALU.mult))
                ins = nc.vector.tensor_tensor(heads[:, nh - 2:nh, :], heads[:, nh - 2:nh, :],
                                              gains[:, HD:2 * HD].unsqueeze(1).to_broadcast([P, 2, HD]), ALU.mult)
                if i >= XT:
                    ins.then_inc(qk_ready[layer], 1)
                    return
                own(ins)
                settle()
                cos = cst("cos")[:, i * HD:(i + 1) * HD]
                sin = cst("sin")[:, i * HD:(i + 1) * HD]
                turned = qk_tmp.rearrange("p (h a b d) -> p h a b d", h=6, a=2, b=2)
                plain = qk.rearrange("p (h a b d) -> p h a b d", h=6, a=2, b=2)
                sins = sin.rearrange("p (a b d) -> p a b d", a=2, b=2)
                for b in range(2):
                    own(nc.vector.tensor_tensor(turned[:, :, :, b, :], plain[:, :, :, 1 - b, :],
                                                sins[:, :, b, :].unsqueeze(1).to_broadcast([P, 6, 2, 16]), ALU.mult))
                settle()
                own(nc.vector.tensor_tensor(heads, heads, cos.unsqueeze(1).to_broadcast([P, 6, HD]), ALU.mult))
                settle()
                nc.vector.tensor_tensor(qk[:, :], qk[:, :], qk_tmp[:, :], ALU.add).then_inc(qk_ready[layer], 1)

            def store_qk(layer, u):
                group, i = divmod(u, NT)
                ve.wait_ge(qkT_psum[layer], u + 1)
                bank = ps[:, 6 + u % 2, 0:384].rearrange("p (r t) -> p r t", r=3)
                if is_full(layer, i):
                    own(nc.vector.tensor_copy(qT[:, group * 2:group * 2 + 2, i * P:(i + 1) * P], bank[:, 0:2, :]))
                nc.vector.tensor_copy(kT[:, group, i * P:(i + 1) * P], bank[:, 2, :]).then_inc(qkT_ready[layer], 1)

            def ln_centre(layer):
                ve.wait_ge(ln_psum[layer], 1)
                for i in range(2):
                    for j, t0, tn in streams_of(layer):
                        ins = nc.vector.scalar_tensor_tensor(out=catT[:, 2 + i, t0:t0 + tn], in0=ps[:, 2 + j, 0:tn],
                                                             scalar=-1.0 / W_CF, in1=catT[:, 2 + i, t0:t0 + tn],
                                                             op0=ALU.mult, op1=ALU.add)
                ins.then_inc(ln_centred[layer], 1)

            def ln_scale(layer):
                n = S + (C if layer == 0 else 0)
                ve.wait_ge(ln_stds[layer], 1)
                own(nc.vector.reciprocal(ln_std[:, 0:n], ln_std[:, 0:n]))
                settle()
                for i in range(2):
                    nc.vector.tensor_tensor(catT[:, 2 + i, 0:n], catT[:, 2 + i, 0:n], ln_std[:, 0:n],
                                            ALU.mult).then_inc(ln_centred[layer], 1)

            def unit_max(layer, u, unit):
                i, group, kv, r = unit
                a, b = key_tiles(layer, group, i)
                w = (b - a) * P
                base = (u % 2) * 1024
                ve.wait_ge(s_psum[layer], u + 1)
                own(nc.vector.tensor_reduce(stat[:, u % 4, 3:4], ps_flat[:, base + 512 - w:base + TOK], AX.X, ALU.max))
                settle()
                if group == 0:
                    ins = nc.vector.tensor_scalar(stat[:, u % 4, 0:1], stat[:, u % 4, 3:4], -SCALE, None, ALU.mult)
                else:
                    h = 2 * kv + r
                    ins = nc.vector.tensor_scalar(stat[:, u % 4, 0:1], stat[:, u % 4, 3:4], -SCALE,
                                                  nsink[:, layer, h:h + 1], ALU.mult, ALU.min)
                ins.then_inc(neg_max[layer], 1)

            def unit_sum(layer, u, unit):
                _, group, _, _ = unit
                total = stat[:, u % 4, 1:2]
                if group == 1:
                    ve.wait_ge(sink_exp[layer], 4 * (u // 8) + u % 4 + 1)
                    own(nc.vector.tensor_tensor(total, total, stat[:, u % 4, 2:3], ALU.add))
                    settle()
                else:
                    ve.wait_ge(exp_done[layer], u + 1)
                nc.vector.reciprocal(inverse[:, u // 2 % 2, u % 2 * HD:(u % 2 + 1) * HD],
                                     total.to_broadcast([P, HD])).then_inc(inv_ready[layer], 1)

            def pair_out(layer, pair, unit):
                i, group, kv, _ = unit
                ve.wait_ge(o_psum[layer], pair + 1)
                own(nc.vector.tensor_copy(inv_rows[:, :], ps[:, 6 + pair % 2, P:2 * P]))
                settle()
                nc.vector.tensor_tensor(catT[:, 4 + 2 * group + kv, i * P:(i + 1) * P], ps[:, 6 + pair % 2, 0:P],
                                        inv_rows[:, :], ALU.mult).then_inc(o_ready[layer], 1)

            def attention(layer):
                units = units_of(layer)
                unit_max(layer, 0, units[0])
                unit_max(layer, 1, units[1])
                for u, unit in enumerate(units):
                    unit_sum(layer, u, unit)
                    if u + 2 < len(units):
                        unit_max(layer, u + 2, units[u + 2])
                    if u % 2 == 0 and u:
                        pair_out(layer, u // 2 - 1, units[u - 1])
                pair_out(layer, len(units) // 2 - 1, units[-1])

            def residual(layer, u):
                tiles = tiles_of(layer)
                c, i = divmod(u, tiles)
                j = 0 if i < XT else 1
                ve.wait_ge(out_psum[layer], u + 1)
                if u == 0:
                    ve.wait_ge(bc_ready[layer], bc_before(layer, "sh2"))
                cols = slice(c * 512, (c + 1) * 512)
                if u >= 2:
                    ve.wait_ge(x_mid[layer], u - 1)
                nc.vector.tensor_tensor(scratch[:, u % 2, :], ps[:, u % 2, :], g1_b[:, j, cols], ALU.mult).then_inc(out_read[layer], 1)
                ve.wait_ge(out_read[layer], u + 1)
                nc.vector.tensor_tensor(xres[:, i, cols], xres[:, i, cols], scratch[:, u % 2, :], ALU.add).then_inc(x_mid[layer], 1)

            def norm2(layer, i):
                j = 0 if i < XT else 1
                ve.wait_ge(rms_std[layer], NT + i + 1)
                if i == 0:
                    ve.wait_ge(bc_ready[layer], bc_before(layer, "g2"))
                own(nc.vector.reciprocal(rstd[:, i:i + 1], rstd[:, i:i + 1]))
                settle()
                if i >= 2:
                    ve.wait_ge(h2T_psum[layer], i - 1)
                    ve.wait_ge(h2_stored[layer], 16 * (i - 1))
                own(nc.vector.scalar_tensor_tensor(out=h2_tok[:, i % 2, :], in0=xres[:, i, :], scalar=rstd[:, i:i + 1],
                                                   in1=amp2_b[:, j, :], op0=ALU.mult, op1=ALU.mult))
                settle()
                nc.vector.tensor_tensor(h2_tok[:, i % 2, :], h2_tok[:, i % 2, :], sh2_b[:, j, :],
                                        ALU.add).then_inc(h2_ready[layer], 1)

            def route(layer):
                t = tiles_of(layer)
                picked = part(0, NT, NE)[:, 0:t, :]
                logit = part(192, NT, NG + NE)[:, 0:t, :]
                glog = logit[:, :, 0:NG]
                elog = logit[:, :, NG:NG + NE]
                tmp = part(408, NT, NE)[:, 0:t, :]
                one = [part(600, NT, NE)[:, 0:t, :], part(792, NT, NE)[:, 0:t, :]]
                g_one = part(984, NT, NG)[:, 0:t, :]
                g_tmp = part(1008, NT, NG)[:, 0:t, :]
                best = part(1032, NT)[:, 0:t]
                index = part(1038, NT)[:, 0:t]
                top = [part(1044, NT)[:, 0:t], part(1050, NT)[:, 0:t]]
                p_grp = part(1056, NT)[:, 0:t]
                ask = part(1062, NT, NG + 1)[:, 0:t, :]
                answer = part(1092, NT, NG + 1)[:, 0:t, :]
                rank = part(1130, NT, NE)[:, 0:t, :]
                count = part(1322, NE)
                over = part(1354, NE, 12)
                blocks = part(1738, NE)
                ends = part(1770, NE)
                starts = part(1802, NE)
                zeros = part(1834, NE)
                dest = part(1870, 2, NT)[:, :, 0:t]
                dest_q = part(1882, 2, NT)[:, :, 0:t]
                dest_r = part(1894, 2, NT)[:, :, 0:t]
                int_a = part(1906, 2, NT).bitcast(I32)[:, :, 0:t]
                int_b = part(1918, 2, NT).bitcast(I32)[:, :, 0:t]
                value = part(1930, 2, NT)[:, :, 0:t]
                hot_r = part(2048, 12, 2 * B)
                hot_q = part(3584, 12, B)

                def wide(v, n):
                    return v.unsqueeze(2).to_broadcast([P, t, n])

                def over_tiles(v, n):
                    return v.unsqueeze(1).to_broadcast([P, t, n])

                def first_best(values, names, n, best_, hot, work):
                    own(nc.vector.tensor_reduce(best_, values, AX.X, ALU.max))
                    settle()
                    own(nc.vector.tensor_tensor(work, values, wide(best_, n), ALU.is_equal))
                    settle()
                    own(nc.vector.tensor_scalar(work, work, -1000.0, 1000.0, ALU.mult, ALU.add))
                    settle()
                    own(nc.vector.tensor_tensor(work, work, over_tiles(names, n), ALU.add))
                    settle()
                    own(nc.vector.tensor_reduce(index, work, AX.X, ALU.min))
                    settle()
                    own(nc.vector.tensor_tensor(hot, wide(index, n), over_tiles(names, n), ALU.is_equal))
                    settle()

                ve.wait_ge(logit_psum[layer], t)
                own(nc.vector.tensor_tensor(logit, ps[:, 6, 0:t * 36].rearrange("p (i n) -> p i n", n=36),
                                            over_tiles(row[:, layer, 4 * HD + 4:N_ROW], NG + NE), ALU.add))
                settle()
                first_best(glog, cst("slot")[:, 0:NG], NG, best, g_one, g_tmp)
                own(nc.vector.tensor_tensor(ask[:, :, 0:NG], glog, wide(best, NG), ALU.subtract))
                own(nc.vector.tensor_scalar(g_one, g_one, -1.0, -NEG, ALU.add, ALU.mult))
                settle()
                for i in range(t):
                    own(nc.vector.tensor_tensor(elog[:, i, :].rearrange("p (g e) -> p g e", g=NG),
                                                elog[:, i, :].rearrange("p (g e) -> p g e", g=NG),
                                                g_one[:, i, :].unsqueeze(2).to_broadcast([P, NG, NPG]), ALU.add))
                settle()
                first_best(elog, cst("slot")[:, 0:NE], NE, top[0], one[0], tmp)
                own(nc.vector.tensor_scalar(tmp, one[0], NEG, None, ALU.mult))
                settle()
                own(nc.vector.tensor_tensor(elog, elog, tmp, ALU.add))
                settle()
                first_best(elog, cst("slot")[:, 0:NE], NE, top[1], one[1], tmp)
                nc.vector.tensor_tensor(picked, one[0], one[1], ALU.add).then_inc(chosen[layer], 1)
                nc.vector.tensor_tensor(ask[:, :, NG:NG + 1], top[1].unsqueeze(2), top[0].unsqueeze(2),
                                        ALU.subtract).then_inc(route_ask[layer], 1)
                own(nc.vector.memset(zeros, 0.0))
                ve.wait_ge(route_exp[layer], 1)
                own(nc.vector.tensor_reduce(p_grp, answer[:, :, 0:NG], AX.X, ALU.add))
                own(nc.vector.tensor_scalar(best.unsqueeze(2), answer[:, :, NG:NG + 1], 1.0, None, ALU.add))
                settle()
                own(nc.vector.tensor_tensor(best, best, p_grp, ALU.mult))
                settle()
                own(nc.vector.reciprocal(gates[:, 0, 0:t], best))
                settle()
                own(nc.vector.tensor_tensor(gates[:, 1, 0:t].unsqueeze(2), gates[:, 0, 0:t].unsqueeze(2),
                                            answer[:, :, NG:NG + 1], ALU.mult))
                ve.wait_ge(rank_psum[layer], 1)
                own(nc.vector.tensor_copy(rank, ps[:, 0, 0:t * NE].rearrange("p (i n) -> p i n", n=NE)))
                own(nc.vector.tensor_reduce(count, ps[:, 1, 0:t * NE].rearrange("p (i n) -> p n i", n=NE), AX.X, ALU.add))
                settle()
                own(nc.vector.tensor_tensor(over, count.unsqueeze(2).to_broadcast([P, NE, 12]),
                                            cst("limit").unsqueeze(1).to_broadcast([P, NE, 12]), ALU.is_gt))
                settle()
                own(nc.vector.tensor_reduce(blocks, over, AX.X, ALU.add))
                settle()
                own(nc.vector.tensor_scalar(blocks, blocks, 1.0, None, ALU.max))
                settle()
                own(nc.vector.tensor_tensor_scan(ends, blocks, zeros, 0.0, ALU.add, ALU.add))
                settle()
                own(nc.vector.tensor_tensor(starts, ends, blocks, ALU.subtract))
                settle()
                own(nc.vector.tensor_copy(blk_table[0:1, 0:NE], starts[0:1, :]))
                own(nc.vector.tensor_copy(blk_table[0:1, NE:NE + 1], ends[0:1, NE - 1:NE]))
                own(nc.vector.scalar_tensor_tensor(out=rank, in0=over_tiles(starts, NE), scalar=float(B), in1=rank,
                                                   op0=ALU.mult, op1=ALU.add))
                settle()
                for c in range(2):
                    own(nc.vector.tensor_tensor(tmp, rank, one[c], ALU.mult))
                    settle()
                    own(nc.vector.tensor_reduce(dest[:, c, :], tmp, AX.X, ALU.add))
                    settle()
                own(nc.vector.tensor_copy(int_a, dest))
                settle()
                own(nc.vector.tensor_scalar(int_b, int_a, 6, None, ALU.arith_shift_right))
                own(nc.vector.tensor_scalar(int_a, int_a, B - 1, None, ALU.bitwise_and))
                for c in range(2):
                    own(nc.vector.tensor_scalar(value[:, c, :], cst("token")[:, 0:t], float(c * t * P), None, ALU.add))
                settle()
                own(nc.vector.tensor_copy(dest_q, int_b))
                own(nc.vector.tensor_copy(dest_r, int_a))
                settle()
                for a in range(2 * t):
                    c, i = divmod(a, t)
                    own(nc.vector.tensor_scalar(hot_r[:, a, :], cst("slot"), dest_r[:, c, i:i + 1], None, ALU.is_equal))
                    nc.vector.tensor_scalar(hot_q[:, a, :], cst("slot")[:, 0:B], dest_q[:, c, i:i + 1], value[:, c, i:i + 1],
                                            ALU.is_equal, ALU.mult).then_inc(onehots[layer], 1)
                ve.wait_ge(list_psum[layer], 1)
                full = part(2048, B)
                want = part(2112, B)
                empty = part(2176, B)
                big = part(2240, B)
                dump = part(2304, 1)
                half = cst("half")
                own(nc.vector.tensor_scalar(full, ps[:, 2, 0:B], -1.0, None, ALU.add))
                own(nc.vector.tensor_scalar(dump, cst("slot_row"), float(2 * t * P + 1), None, ALU.add))
                settle()
                own(nc.vector.tensor_scalar(big, full, float(t * P), float(-t * P), ALU.is_ge, ALU.mult))
                own(nc.vector.tensor_scalar(empty, full, 0.0, dump[:, 0:1], ALU.is_lt, ALU.mult))
                settle()
                own(nc.vector.tensor_tensor(want, full, big, ALU.add))
                own(nc.vector.tensor_tensor(empty, empty, full, ALU.add))
                settle()
                own(nc.vector.tensor_scalar(want, want, 0.0, 2.0, ALU.max, ALU.mult))
                settle()
                own(nc.vector.tensor_scalar(list_gather[:, 0:MAXB + 1], want[:, 0:MAXB + 1], half, None, ALU.add))
                nc.vector.tensor_scalar(list_scatter[:, 0:MAXB + 1], empty[:, 0:MAXB + 1], 2.0, half, ALU.mult,
                                        ALU.add).then_inc(route_done[layer], 1)
                settle()

            def experts(layer):
                blocks = ve.value_load(blk_table[0:1, NE:NE + 1], min_val=1, max_val=MAXB)
                def turn_in():
                    nc.vector.tensor_copy(xgT[:, :, :, :].rearrange("p j h t -> p (j h t)"),
                                          ps[:, 4, :]).then_inc(xgT_ready[layer], 1)

                ve.wait_ge(xgT_psum[layer], 1)
                turn_in()
                with ve.Fori(0, blocks) as q:
                    ve.wait_ge(silu_ready[layer], q + 1)
                    ve.wait_ge(up_psum[layer], q + 1)
                    nc.vector.tensor_tensor(hid, silu, ps[:, 1, 0:256], ALU.mult).then_inc(hid_ready[layer], 1)
                    ve.wait_ge(hidT_psum[layer], q + 1)
                    nc.vector.tensor_copy(hidT[:, :, :, :].rearrange("p j h t -> p (j h t)"),
                                          ps[:, 2, 0:256]).then_inc(hidT_ready[layer], 1)
                    ve.wait_ge(xgT_psum[layer], q + 2)
                    turn_in()

            def combine(layer, i):
                j = 0 if i < XT else 1
                y = y_pair[i]
                ve.wait_ge(y_loaded[i], 16 * (layer + 1))
                ve.wait_ge(y_scaled[layer], i + 1)
                own(nc.vector.scalar_tensor_tensor(out=y[:, 0, :], in0=y[:, 1, :], scalar=gates[:, 1, i:i + 1],
                                                   in1=y[:, 0, :], op0=ALU.mult, op1=ALU.add))
                settle()
                nc.vector.tensor_tensor(y[:, 0, :], y[:, 0, :], g2_b[:, j, :], ALU.mult).then_inc(y_weighted[layer], 1)

            ve.wait_ge(consts_in, 80)
            for layer in range(DEPTH):
                own(nc.vector.tensor_scalar(nsink[:, layer, :], row[:, layer, 4 * HD:4 * HD + 4], -1.0, None, ALU.mult))
                tokens_in(layer)
                clear_pads(layer)
                glu_product(layer)
                for tap in range(TAPS_EARLY):
                    conv_b_tap(layer, tap)
                conv_a_group(layer)
                if layer == 0:
                    mod_copy(0, MOD_FIRST, 12, turned_bank(MOD_FIRST), MOD_CONV)
                    mod_copy(1, 0, MOD_CONV - 12, turned_bank(MOD_FIRST), MOD_CONV)
                for u in range(QKV_UNITS):
                    if layer == 0 and u == QKV_UNITS - 1:
                        mod_copy(1, MOD_CONV - 12, 12, turned_bank(MOD_CONV), 24)
                    rotate(layer, u)
                    if TAPS_EARLY + u < TAPS_B:
                        conv_b_tap(layer, TAPS_EARLY + u)
                    store_qk(layer, u)
                    if u == LN_MEAN:
                        ln_centre(layer)
                    if u == LN_VAR:
                        ln_scale(layer)
                amplitude(layer, "norm2", 4 * KD, 2)
                attention(layer)
                tiles = tiles_of(layer)
                for u in range(2 * tiles):
                    if u > tiles:
                        norm2(layer, u - tiles - 1)
                    residual(layer, u)
                norm2(layer, tiles - 1)
                route(layer)
                experts(layer)
                if layer == DEPTH - 1:
                    for i in range(tiles):
                        combine(layer, i)

        @block.scalar
        def _(ac):
            steps = [0]

            def own(ins):
                steps[0] += 1
                ins.then_inc(act_step, 1)

            def settle():
                ac.wait_ge(act_step, steps[0])

            eps = cst("eps")

            def rms_of_tokens(layer, i):
                if layer == 0:
                    if i == 0:
                        ac.wait_ge(x_in, 32)
                    squares = xn[:, i, :]
                else:
                    ac.wait_ge(x_done[layer - 1], i + 1)
                    squares = y_pair[i][:, 1, :]
                own(nc.scalar.activation(squares, xres[:, i, :], ACT.Square, accum_out=ssq[:, i:i + 1]))
                settle()
                nc.scalar.activation(rstd[:, i:i + 1], ssq[:, i:i + 1], ACT.Sqrt, bias=eps,
                                     scale=1.0 / D).then_inc(rms_std[layer], 1)

            def modulate(layer, i):
                ac.wait_ge(h1_psum[layer], i + 1)
                j = 0 if i < XT else 1
                if i == 0:
                    ac.wait_ge(amp_ready[layer], 2)
                for k in range(KD // 2):
                    at = i % 2 * 1024 + k * P
                    ins = nc.scalar.activation(h1T[:, i, k, :], ps_flat[:, at:at + P], ACT.Identity,
                                               bias=mod[:, layer, k, j:j + 1], scale=amp[:, j, k:k + 1])
                ins.then_inc(h1_act[layer], 1)

            def tokens_in(layer):
                if layer == 0:
                    for i in range(NT):
                        rms_of_tokens(layer, i)
                    return
                for n in range(NT + 3):
                    if n < NT:
                        combine(layer - 1, n)
                    if 2 <= n < NT + 2:
                        rms_of_tokens(layer, n - 2)
                    if n >= 3:
                        modulate(layer, n - 3)

            def mod_sums(n):
                ac.wait_ge(mod_psum[n // 12], n % 12 + 1)
                if n >= 1:
                    ac.wait_ge(mod_turned, n)
                nc.scalar.copy(mod_row[:, :], ps[:, mod_bank(n), :]).then_inc(mod_rows, 1)

            def conv_copies(layer, tiles):
                for ct in tiles:
                    ac.wait_ge(conv_psum[layer], CONV_AT[ct] + 1)
                    if ct == 6:
                        ac.wait_ge(pads_ready[layer], 1)
                    i = ct % 2
                    for j, t0, tn in streams_of(layer):
                        src = ps[:, i * 2 + j, 0:tn]
                        if ct < 2:
                            ins = nc.scalar.copy(catT[:, i, t0:t0 + tn], src)
                        elif ct < 4:
                            ins = nc.scalar.copy(cx[:, i, t0 + 1 + j:t0 + 1 + j + tn], src)
                        elif ct < 8:
                            ins = nc.scalar.copy(glu[:, i, t0 + 15 * (1 + j):t0 + 15 * (1 + j) + tn], src)
                        else:
                            ins = nc.scalar.activation(catT[:, 2 + i, t0:t0 + tn], src, ACT.Sigmoid)
                    ins.then_inc(conv_act[layer], 1)

            def qkv_copies(layer, u):
                group, i = divmod(u, NT)
                full = is_full(layer, i)
                c0 = 0 if full else 256
                h0 = 0 if full else 4
                ac.wait_ge(qkv_psum[layer], u + 1)
                if u == 0:
                    ac.wait_ge(conv_mul[layer], 2)
                own(nc.scalar.copy(v_tok[:, i, group * P:(group + 1) * P], ps[:, 4 + u % 2, 384:512]))
                if u >= 1:
                    ac.wait_ge(qk_ready[layer], u)
                nc.scalar.activation(qk_tmp[:, c0:384], ps[:, 4 + u % 2, c0:384], ACT.Square).then_inc(qk_square[layer], 1)
                ac.wait_ge(qk_sums[layer], u + 1)
                nc.scalar.activation(qk_std[:, h0:6], qk_sum[:, h0:6], ACT.Sqrt, bias=eps,
                                     scale=1.0 / HD).then_inc(qk_stds[layer], 1)

            def ln_squares(layer):
                n = S + (C if layer == 0 else 0)
                ac.wait_ge(ln_centred[layer], 1)
                for i in range(2):
                    nc.scalar.activation(square[:, i, 0:n], catT[:, 2 + i, 0:n], ACT.Square).then_inc(ln_sq[layer], 1)

            def ln_roots(layer):
                n = S + (C if layer == 0 else 0)
                ac.wait_ge(ln_psum[layer], 2)
                nc.scalar.activation(ln_std[:, 0:n], ps_flat[:, 1024:1024 + n], ACT.Sqrt, bias=eps,
                                     scale=1.0 / W_CF).then_inc(ln_stds[layer], 1)

            def ln_silu(layer):
                n = S + (C if layer == 0 else 0)
                for i in range(2):
                    ac.wait_ge(ln_centred[layer], i + 2)
                    nc.scalar.activation(catT[:, 2 + i, 0:n], catT[:, 2 + i, 0:n], ACT.Silu,
                                         bias=sml(layer, "ln_b")[:, i:i + 1],
                                         scale=sml(layer, "ln_g")[:, i:i + 1]).then_inc(ln_done[layer], 1)

            def unit_exp(layer, u, unit):
                i, group, kv, r = unit
                a, b = key_tiles(layer, group, i)
                w = (b - a) * P
                base = (u % 2) * 1024
                ac.wait_ge(neg_max[layer], u + 1)
                if u >= 2:
                    ac.wait_ge(pT_psum[layer], u - 1)
                if u >= 4:
                    ac.wait_ge(inv_ready[layer], u - 3)
                nc.scalar.activation(prob[:, u % 2, 512 - w:TOK], ps_flat[:, base + 512 - w:base + TOK], ACT.Exp,
                                     bias=stat[:, u % 4, 0:1], scale=SCALE,
                                     accum_out=stat[:, u % 4, 1:2]).then_inc(exp_done[layer], 1)
                if group == 1:
                    h = 2 * kv + r
                    nc.scalar.activation(stat[:, u % 4, 2:3], row[:, layer, 4 * HD + h:4 * HD + h + 1], ACT.Exp,
                                         bias=stat[:, u % 4, 0:1]).then_inc(sink_exp[layer], 1)

            def unit_pT(layer, u, unit):
                i, group, _, _ = unit
                a, b = key_tiles(layer, group, i)
                w = (b - a) * P
                ac.wait_ge(pT_psum[layer], u + 1)
                if u >= 2:
                    ac.wait_ge(o_psum[layer], u // 2)
                nc.scalar.copy(probT[:, u % 2, 512 - w:TOK], ps_flat[:, 2048 + 512 - w:2048 + TOK]).then_inc(pT_ready[layer], 1)

            def pad_keys(layer, group):
                ac.wait_ge(qkT_ready[layer], NT * (group + 1))
                ac.wait_ge(qkv_psum[layer], QKV_UNITS)
                ac.wait_ge(keys_zeroed[layer], 4)
                for half, kv in ((slice(0, HD), 0), (slice(HD, P), 1)):
                    nc.scalar.copy(kT_pad[half, group, kv, :], kT[half, group, :]).then_inc(keys_padded[layer], 1)

            def attention(layer):
                units = units_of(layer)
                pad_keys(layer, 0)
                unit_exp(layer, 0, units[0])
                unit_exp(layer, 1, units[1])
                pad_keys(layer, 1)
                for u in range(0, len(units), 2):
                    for v in (u, u + 1):
                        unit_pT(layer, v, units[v])
                    if u + 2 < len(units):
                        for v in (u + 2, u + 3):
                            unit_exp(layer, v, units[v])

            def store_broadcasts(layer, first, end):
                for b in range(first, end):
                    _, _, dst, j = bc_list(layer)[b]
                    ac.wait_ge(bc_psum[layer], b + 1)
                    at = bc_bank(b) * 512
                    if dst is g2_b:
                        ac.wait_ge(logit_psum[layer], tiles_of(layer))
                    nc.scalar.copy(dst[:, j, :], ps_flat[:, at:at + 1024]).then_inc(bc_ready[layer], 1)

            def norm2(layer, i):
                tiles = tiles_of(layer)
                ac.wait_ge(x_mid[layer], tiles + i + 1)
                if i >= 2:
                    ac.wait_ge(h2T_psum[layer], i - 1)
                    ac.wait_ge(h2_stored[layer], 16 * (i - 1))
                own(nc.scalar.activation(h2_tok[:, i % 2, :], xres[:, i, :], ACT.Square, accum_out=ssq[:, i:i + 1]))
                settle()
                nc.scalar.activation(rstd[:, i:i + 1], ssq[:, i:i + 1], ACT.Sqrt, bias=eps, scale=1.0 / D).then_inc(rms_std[layer], 1)

            def store_h2T(layer, i):
                ac.wait_ge(h2T_psum[layer], i + 1)
                if i >= 2:
                    ac.wait_ge(logit_psum[layer], i - 1)
                nc.scalar.copy(h2T[:, i % 2, :, :].rearrange("p k t -> p (k t)"), ps_flat[:, 2048:3072]).then_inc(h2T_ready[layer], 1)

            def experts(layer):
                ac.wait_ge(route_done[layer], 1)
                blocks = ac.value_load(blk_table[0:1, NE:NE + 1], min_val=1, max_val=MAXB)
                nc.scalar.copy(silu[:, 0:1], ssq[:, 0:1]).then_inc(y_ready[layer], 1)
                ac.wait_ge(y_ready[layer], 1)

                def gate():
                    nc.scalar.activation(silu, ps[:, 0, 0:256], ACT.Silu).then_inc(silu_ready[layer], 1)

                def rows_out():
                    nc.scalar.copy(y_rows, ps[:, 3, :]).then_inc(y_ready[layer], 1)

                ac.wait_ge(gate_psum[layer], 1)
                gate()
                ac.wait_ge(y_psum[layer], 1)
                rows_out()
                with ac.Fori(1, blocks) as q:
                    ac.wait_ge(gate_psum[layer], q + 1)
                    gate()
                    ac.wait_ge(y_psum[layer], q + 1)
                    ac.wait_ge(scattered[layer], 16 * q)
                    rows_out()

            def combine(layer, i):
                y = y_pair[i][:, 0, :]
                ac.wait_ge(y_loaded[i], 16 * (layer + 1))
                nc.scalar.activation(y, y, ACT.Copy, scale=gates[:, 0, i:i + 1]).then_inc(y_scaled[layer], 1)

            ac.wait_ge(consts_in, 80)
            nc.scalar.activation(cond[:, :, :], cond[:, :, :], ACT.Silu).then_inc(cond_ready, 1)
            for layer in range(DEPTH):
                tokens_in(layer)
                started = layer > 0
                for kind, n in steps_before_attention(layer):
                    if kind == "mod":
                        mod_sums(n)
                        continue
                    if not started:
                        for i in range(NT):
                            modulate(layer, i)
                        started = True
                    if kind == "conv" and n in CONV_ACT:
                        conv_copies(layer, [n])
                    if kind == "qkv":
                        qkv_copies(layer, n)
                        if n == LN_MEAN + 1:
                            ln_squares(layer)
                        if n == LN_VAR:
                            ln_roots(layer)
                        if n == LN_VAR + 1:
                            ln_silu(layer)
                attention(layer)
                store_broadcasts(layer, 0, bc_before(layer, "g2"))
                tiles = tiles_of(layer)
                for i in range(tiles):
                    norm2(layer, i)
                    if i >= 1:
                        store_h2T(layer, i - 1)
                store_h2T(layer, tiles - 1)
                store_broadcasts(layer, bc_before(layer, "g2"), len(bc_list(layer)))
                ac.wait_ge(route_ask[layer], 1)
                nc.scalar.activation(part(1092, NT, NG + 1)[:, 0:tiles, :], part(1062, NT, NG + 1)[:, 0:tiles, :],
                                     ACT.Exp).then_inc(route_exp[layer], 1)
                experts(layer)
                if layer == DEPTH - 1:
                    for i in range(tiles):
                        combine(layer, i)

        @block.gpsimd
        def _(po):
            count = po.alloc_register("count")
            count_in = po.alloc_register("count_in")
            po.dma_start(xres[:, 0:XT, :], x.rearrange("o (i p) n -> p (o i) n", p=P)).then_inc(x_in, 16)
            po.dma_start(xres[:, XT:NT, :], ctx_tokens.rearrange("o (i p) n -> p (o i) n", p=P)).then_inc(x_in, 16)
            for layer in range(DEPTH):
                tiles = tiles_of(layer)
                if layer:
                    po.wait_ge(logit_psum[layer - 1], tiles_of(layer - 1))
                po.dma_start(router_w[:, :, :], w_router[layer].rearrange("(k p) n -> p k n", p=P)).then_inc(router_in, 16)
                po.wait_ge(qkv_psum[layer], QKV_UNITS)
                for group in range(2):
                    nc.gpsimd.memset(kT_pad[HD:P, group, 0, :], 0.0).then_inc(keys_zeroed[layer], 1)
                    nc.gpsimd.memset(kT_pad[0:HD, group, 1, :], 0.0).then_inc(keys_zeroed[layer], 1)
                for i in range(tiles):
                    po.wait_ge(h2_ready[layer], i + 1)
                    po.dma_start(h2_dram[layer].rearrange("(t h) n -> t (h n)", h=2)[i * P:(i + 1) * P, :], h2_tok[:, i % 2, :]).then_inc(h2_stored[layer], 16)
                    po.wait_ge(h2_stored[layer], 16 * (i + 1))
                po.wait_ge(route_done[layer], 1)
                blocks = po.value_load(blk_table[0:1, NE:NE + 1], min_val=1, max_val=MAXB)

                def gather(q):
                    nc.gpsimd.tensor_copy(idx_gather[:, :], list_gather[:, bass.ds(q, 1)]).then_inc(idx_copied[layer], 1)

                def gather_go():
                    po.indirect_dma_start(out=xg, out_offset=None, in_=h2_dram[layer],
                                          in_offset=bass.IndirectOffsetOnAxis(ap=idx_gather[:, 0:1], axis=0),
                                          ).then_inc(gathered[layer], 16)

                def scatter(q):
                    nc.gpsimd.tensor_copy(idx_scatter[:, :], list_scatter[:, bass.ds(q, 1)]).then_inc(idx_copied[layer], 1)

                def scatter_go():
                    po.indirect_dma_start(out=y_dram[layer], in_=y_rows, in_offset=None,
                                          out_offset=bass.IndirectOffsetOnAxis(ap=idx_scatter[:, 0:1], axis=0),
                                          ).then_inc(scattered[layer], 16)

                gather(0)
                po.wait_ge(idx_copied[layer], 1)
                gather_go()
                with po.Fori(0, blocks) as q:
                    po.reg_add(count, q, 1)
                    po.wait_ge(consts_in, 80)
                    po.wait_ge(xgT_psum[layer], count)
                    gather(q + 1)
                    po.reg_add(count, 2 * q, 2)
                    po.wait_ge(consts_in, 80)
                    po.wait_ge(idx_copied[layer], count)
                    gather_go()
                    po.reg_add(count, q, 2)
                    po.wait_ge(consts_in, 80)
                    po.wait_ge(y_ready[layer], count)
                    scatter(q)
                    po.reg_add(count, 2 * q, 3)
                    po.wait_ge(consts_in, 80)
                    po.wait_ge(idx_copied[layer], count)
                    scatter_go()
                po.reg_add(count, 16 * blocks, 0)
                po.reg_add(count_in, blocks, 1)
                po.wait_ge(consts_in, 80)
                po.wait_ge(scattered[layer], count)
                po.wait_ge(xgT_ready[layer], count_in)
                rows = 4 * tiles * P
                for i in range(tiles):
                    po.dma_start(y_pair[i], y_dram[layer][0:rows, :].rearrange("(c i p h) n -> i p c (h n)", c=2, p=P, h=2)[i]
                                 ).then_inc(y_loaded[i], 16)
                for i in range(tiles):
                    po.wait_ge(y_weighted[layer], i + 1)
                    nc.gpsimd.tensor_tensor(xres[:, i, :], xres[:, i, :], y_pair[i][:, 0, :], ALU.add).then_inc(x_done[layer], 1)
                    if layer == DEPTH - 1:
                        po.wait_ge(x_done[layer], i + 1)
                        po.dma_start(out[0, i * P:(i + 1) * P, :], xres[:, i, :]).then_inc(out_stored, 16)
            po.wait_ge(out_stored, 16 * XT)


def shape_constants():
    import numpy as np

    c = np.zeros((P, N_CONST), np.float32)

    def put(name, values):
        a, n = CONST[name]
        c[:, a:a + n] = values

    p = np.arange(P, dtype=np.float32)[:, None]
    f = np.arange(P, dtype=np.float32)[None, :]
    put("ident", p == f)
    put("ones", 1.0)
    put("before", p < f)
    put("mask_prev", np.where(f < p, NEG, 0.0))
    put("mask_next", np.where(f > p, NEG, 0.0))
    half = HD // 2
    inv = np.float32(ROPE_THETA) ** (-np.arange(0, half, 2, dtype=np.float32) / np.float32(half))
    token = np.arange(S)
    ar = (token // GRID_W).astype(np.float32)[:, None] * inv
    ac = (token % GRID_W).astype(np.float32)[:, None] * inv
    angle = np.concatenate([ar, ar, ac, ac], axis=-1)
    sign = np.tile(np.repeat(np.float32([-1, 1]), half // 2), 2)
    put("cos", np.cos(angle).reshape(XT, P, HD).transpose(1, 0, 2).reshape(P, -1))
    put("sin", (np.sin(angle) * sign).reshape(XT, P, HD).transpose(1, 0, 2).reshape(P, -1))
    put("slot", np.arange(2 * B) % B)
    put("limit", B * np.arange(CONST["limit"][1]))
    put("token", p + P * np.arange(NT) + 1)
    put("slot_row", p % B)
    put("half", p // B)
    put("select", (p % 32) == np.arange(2))
    put("eps", EPS)
    return c


_OUTS = [((1, S, D), "float32")]


def kernel(**inputs):
    import numpy as _np
    import concourse.bacc as _bacc
    from concourse import mybir as _mybir
    from concourse.bass_utils import run_bass_kernel_spmd as _run

    a = {k: _np.asarray(v) for k, v in inputs.items()}

    def by_partition(v):
        return v.reshape(-1, P).T

    smalls, rows = [], []
    for layer in range(DEPTH):
        smalls.append(_np.concatenate([
            by_partition(a["norm1_g"][layer]), by_partition(a["norm2_g"][layer]), by_partition(a["mod_b"][layer]),
            a["conv_a_w"][layer].reshape(TAPS_A, 2, P).transpose(2, 1, 0).reshape(P, -1),
            a["conv_b_w"][layer].reshape(TAPS_B, 2, P).transpose(2, 1, 0).reshape(P, -1),
            by_partition(a["conv_b_b"][layer]), by_partition(a["ln_b_g"][layer]), by_partition(a["ln_b_b"][layer]),
        ], axis=1))
        rows.append(_np.concatenate([a["qn_c_g"][layer], a["kn_c_g"][layer], a["qn_d_g"][layer], a["kn_d_g"][layer],
                                     a["sink_d"][layer], a["rg_b"][layer], a["re_b"][layer]]))
    arrays = {
        "x": a["x"], "ctx_tokens": a["ctx"],
        "conditions": _np.pad(_np.stack([by_partition(a["c"][0]), by_partition(a["c_ctx"])], axis=2),
                              ((0, 0), (0, 0), (0, 30))),
        "consts": shape_constants(), "smalls": _np.stack(smalls), "rows": _np.stack(rows),
        "w_mod": a["mod_w"], "w_in": a["w_in"], "w_out": a["w_out"],
        "w_router": _np.concatenate([a["rg_w"], a["re_w"]], axis=2),
        "e_gate": a["e_gate"], "e_up": a["e_up"], "e_down": a["e_down"],
    }
    arrays = {f"in_{k}_dram": _np.ascontiguousarray(v) for k, v in arrays.items()}
    nc = _bacc.Bacc("TRN2", target_bir_lowering=False, num_devices=1)
    args = [nc.dram_tensor(k, v.shape, _mybir.dt.from_np(v.dtype), kind="ExternalInput").ap() for k, v in arrays.items()]
    for i, (shape, dtype) in enumerate(_OUTS):
        args.append(nc.dram_tensor(f"out_{i}_dram", shape, _mybir.dt.from_np(_np.dtype(dtype)), kind="ExternalOutput").ap())
    hybrid_flow_block(nc, *args)
    r = _run(nc, [arrays], core_ids=[0])
    got = tuple(r.results[0][f"out_{i}_dram"] for i in range(len(_OUTS)))
    return got[0]
```
